# Optimizing a Trainium2 kernel written in Bass

```python
import math
import jax
import jax.numpy as jnp
from jax import lax
import numpy as np
import jax, jax.numpy as jnp

D_MODEL = 1024
BATCH = 1
SEQ = 512
DEPTH = 1

CTX_LEN = 256
GRID_W = 64
EPS = 1e-6

N_ATTN_HEADS = 8
ATTN_DH = 64
ATTN_DV = 2 * ATTN_DH
ATTN_QK_DIM = N_ATTN_HEADS * 2 * ATTN_DH
ATTN_V_DIM = N_ATTN_HEADS * ATTN_DV
ATTN_SCALE = ATTN_DH ** -0.5
ATTN_QBLOCK = 128
ROPE_THETA = 10000.0
ROPE_AXIS_DIM = ATTN_DH // 2

D_SSD = D_MODEL
SSD_HEADDIM = 64
SSD_HEADS = D_SSD // SSD_HEADDIM
SSD_GROUPS = 4
SSD_HPG = SSD_HEADS // SSD_GROUPS
SSD_STATE = 128
SSD_CONV_W = 3
SSD_CHUNK = 64
XBC_DIM = D_SSD + 2 * SSD_GROUPS * SSD_STATE

IN_SPLITS = (ATTN_QK_DIM, 2 * ATTN_QK_DIM, 2 * ATTN_QK_DIM + ATTN_V_DIM, 2 * ATTN_QK_DIM + ATTN_V_DIM + D_SSD, 2 * ATTN_QK_DIM + ATTN_V_DIM + D_SSD + XBC_DIM, 2 * ATTN_QK_DIM + ATTN_V_DIM + D_SSD + XBC_DIM + 2 * SSD_HEADS)
IN_COLS = IN_SPLITS[-1] + 2 * D_MODEL

N_EXPERTS = 64
EXPERT_FF = 256
SHARED_FF = 256
TOP_K = 8
N_EXPERT_GROUPS = 8
TOPK_GROUPS = 4
ROUTED_SCALE = 2.5
MOE_BLOCK = 128


def rmsnorm(u, g):
    uf = u.astype(jnp.float32)
    y = uf * lax.rsqrt(jnp.mean(uf * uf, axis=-1, keepdims=True) + EPS)
    return (y * g.astype(jnp.float32)).astype(u.dtype)

def modulate(u, shift, scale):
    return u * (1 + scale) + shift

def rev(t):
    return jnp.flip(t, axis=1)

def axial_rope_tables(n_tok):
    rows = n_tok // GRID_W
    row = jnp.repeat(jnp.arange(rows, dtype=jnp.float32), GRID_W)
    col = jnp.broadcast_to(jnp.arange(GRID_W, dtype=jnp.float32)[None, :], (rows, GRID_W)).reshape(-1)
    inv_freq = ROPE_THETA ** (-jnp.arange(0, ROPE_AXIS_DIM, 2, dtype=jnp.float32) / ROPE_AXIS_DIM)
    ang = jnp.concatenate([row[:, None] * inv_freq, col[:, None] * inv_freq], axis=-1)
    ang = jnp.concatenate([ang, ang], axis=-1)
    return jnp.cos(ang), jnp.sin(ang)

def apply_rope(u, cos, sin):
    half = ATTN_DH // 2
    uf = u.astype(jnp.float32)
    rot = jnp.concatenate([-uf[..., half:], uf[..., :half]], axis=-1)
    return (uf * cos[:, None, None, :] + rot * sin[:, None, None, :]).astype(u.dtype)

def diff_attend(q, k, v, lam, g_subln, lam_init):
    s = jnp.einsum('bqhcd,bkhcd->bchqk', q.astype(jnp.float32), k.astype(jnp.float32)) * ATTN_SCALE
    p = jax.nn.softmax(s, axis=-1)
    w = p[:, 0] - lam * p[:, 1]
    o = jnp.einsum('bhqk,bkhd->bqhd', w, v.astype(jnp.float32))
    o = o * lax.rsqrt(jnp.mean(o * o, axis=-1, keepdims=True) + EPS) * g_subln.astype(jnp.float32)
    return (o * (1.0 - lam_init)).astype(v.dtype)

def centred_dwconv(u, w, b):
    pad = SSD_CONV_W // 2
    n = u.shape[1]
    up = jnp.pad(u, ((0, 0), (pad, pad), (0, 0)))
    out = b
    for i in range(SSD_CONV_W):
        out = out + up[:, i:i + n] * w[i]
    return out

def ssd_inputs(xbc, dt_raw, conv_w, conv_b, dt_bias):
    nb, nl, _ = xbc.shape
    u = jax.nn.silu(centred_dwconv(xbc, conv_w, conv_b)).astype(jnp.float32)
    xs, bm, cm = jnp.split(u, (D_SSD, D_SSD + SSD_GROUPS * SSD_STATE), axis=-1)
    xh = xs.reshape(nb, nl, SSD_GROUPS, SSD_HPG, SSD_HEADDIM)
    bm = bm.reshape(nb, nl, SSD_GROUPS, SSD_STATE)
    cm = cm.reshape(nb, nl, SSD_GROUPS, SSD_STATE)
    dt = jax.nn.softplus(dt_raw.astype(jnp.float32).reshape(nb, nl, 2, SSD_GROUPS, SSD_HPG) + dt_bias.astype(jnp.float32).reshape(2, SSD_GROUPS, SSD_HPG))
    return xh, bm, cm, dt[:, :, 0], dt[:, :, 1]

def ssd_chunked(xh, dt, a, bm, cm, h0, with_output):
    nb, nl, ng, nr, npd = xh.shape
    nn = bm.shape[-1]
    nc = nl // SSD_CHUNK
    xc = xh.reshape(nb, nc, SSD_CHUNK, ng, nr, npd)
    dtc = dt.reshape(nb, nc, SSD_CHUNK, ng, nr)
    bc = bm.reshape(nb, nc, SSD_CHUNK, ng, nn)
    acum = jnp.cumsum(dtc * a, axis=2)
    to_end = jnp.exp(acum[:, :, -1:] - acum)
    states = jnp.einsum('bcqgn,bcqgr,bcqgrp->bcgrpn', bc, to_end * dtc, xc)
    chunk_decay = jnp.exp(acum[:, :, -1])

    def step(h, inp):
        st, dec = inp
        return h * dec[..., None, None] + st, (h if with_output else None)

    h_last, h_prev = lax.scan(step, h0, (jnp.moveaxis(states, 1, 0), jnp.moveaxis(chunk_decay, 1, 0)))
    if not with_output:
        return None, h_last
    cc = cm.reshape(nb, nc, SSD_CHUNK, ng, nn)
    seg = acum[:, :, :, None] - acum[:, :, None]
    lower = (jnp.arange(SSD_CHUNK)[:, None] >= jnp.arange(SSD_CHUNK)[None, :])[:, :, None, None]
    decay = jnp.where(lower, jnp.exp(jnp.where(lower, seg, 0.0)), 0.0)
    cb = jnp.einsum('bcign,bcjgn->bcijg', cc, bc)
    y_diag = jnp.einsum('bcijg,bcijgr,bcjgr,bcjgrp->bcigrp', cb, decay, dtc, xc)
    y_off = jnp.einsum('bcign,cbgrpn,bcigr->bcigrp', cc, h_prev, jnp.exp(acum))
    y = (y_diag + y_off).reshape(nb, nl, ng, nr, npd)
    return y, h_last

def merge_branches(o_attn, y_ssd, z, gates, g_ssd_norm, w_branch_attn, w_branch_ssd, w_out):
    out_dtype = z.dtype
    y = y_ssd * jax.nn.silu(z.astype(jnp.float32))
    shp = y.shape
    yg = y.reshape(shp[:-1] + (SSD_GROUPS, D_SSD // SSD_GROUPS))
    yg = yg * lax.rsqrt(jnp.mean(yg * yg, axis=-1, keepdims=True) + EPS)
    y = (yg.reshape(shp) * g_ssd_norm.astype(jnp.float32)).astype(out_dtype)
    ya = o_attn @ w_branch_attn
    ys = y @ w_branch_ssd
    g_a, g_s = jnp.split(jax.nn.sigmoid(gates), 2, axis=-1)
    return (g_a * ya + g_s * ys) @ w_out

def token_mixer(h, hc, update_ctx, lam_init, w_in, lam_q1, lam_k1, lam_q2, lam_k2, g_attn_subln, conv_w, conv_b, dt_bias, a_log, d_skip, g_ssd_norm, w_branch_attn, w_branch_ssd, w_out):
    nb, ns, _ = h.shape
    nl = hc.shape[1]
    w_q, w_k, w_v, w_z, w_xbc, w_dt, w_g = jnp.split(w_in, IN_SPLITS, axis=1)
    q, k, v, z, xbc, dt_raw, gates = jnp.split(h @ w_in, IN_SPLITS, axis=-1)

    lam = (jnp.exp(jnp.sum(lam_q1.astype(jnp.float32) * lam_k1.astype(jnp.float32)))
           - jnp.exp(jnp.sum(lam_q2.astype(jnp.float32) * lam_k2.astype(jnp.float32))) + lam_init)
    cos, sin = axial_rope_tables(ns)
    q = apply_rope(q.reshape(nb, ns, N_ATTN_HEADS, 2, ATTN_DH), cos, sin)
    k = apply_rope(k.reshape(nb, ns, N_ATTN_HEADS, 2, ATTN_DH), cos, sin)
    v = v.reshape(nb, ns, N_ATTN_HEADS, ATTN_DV)
    kc = (hc @ w_k).reshape(nb, nl, N_ATTN_HEADS, 2, ATTN_DH)
    vc = (hc @ w_v).reshape(nb, nl, N_ATTN_HEADS, ATTN_DV)
    k_all = jnp.concatenate([kc, k], axis=1)
    v_all = jnp.concatenate([vc, v], axis=1)
    n_qb = ns // ATTN_QBLOCK
    q_blocks = jnp.swapaxes(q.reshape(nb, n_qb, ATTN_QBLOCK, N_ATTN_HEADS, 2, ATTN_DH), 0, 1)
    o = lax.map(lambda qb: diff_attend(qb, k_all, v_all, lam, g_attn_subln, lam_init), q_blocks)
    o_lat = jnp.swapaxes(o, 0, 1).reshape(nb, ns, ATTN_V_DIM)

    a = -jnp.exp(a_log.astype(jnp.float32)).reshape(2, SSD_GROUPS, SSD_HPG)
    d = d_skip.astype(jnp.float32).reshape(SSD_GROUPS, SSD_HPG, 1)
    xh_c, bm_c, cm_c, dtf_c, dtb_c = ssd_inputs(hc @ w_xbc, hc @ w_dt, conv_w, conv_b, dt_bias)
    h0 = jnp.zeros((nb, SSD_GROUPS, SSD_HPG, SSD_HEADDIM, SSD_STATE), jnp.float32)
    yf_c, hf = ssd_chunked(xh_c, dtf_c, a[0], bm_c, cm_c, h0, update_ctx)
    yb_c, hb = ssd_chunked(rev(xh_c), rev(dtb_c), a[1], rev(bm_c), rev(cm_c), h0, update_ctx)
    xh, bm, cm, dtf, dtb = ssd_inputs(xbc, dt_raw, conv_w, conv_b, dt_bias)
    yf, _ = ssd_chunked(xh, dtf, a[0], bm, cm, hf, True)
    yb, _ = ssd_chunked(rev(xh), rev(dtb), a[1], rev(bm), rev(cm), hb, True)
    y_lat = (yf + rev(yb) + d * xh).reshape(nb, ns, D_SSD)

    out_lat = merge_branches(o_lat, y_lat, z, gates, g_ssd_norm, w_branch_attn, w_branch_ssd, w_out)
    if not update_ctx:
        return out_lat, None
    qc = (hc @ w_q).reshape(nb, nl, N_ATTN_HEADS, 2, ATTN_DH)
    o_ctx = diff_attend(qc, kc, vc, lam, g_attn_subln, lam_init).reshape(nb, nl, ATTN_V_DIM)
    y_ctx = (yf_c + rev(yb_c) + d * xh_c).reshape(nb, nl, D_SSD)
    out_ctx = merge_branches(o_ctx, y_ctx, hc @ w_z, hc @ w_g, g_ssd_norm, w_branch_attn, w_branch_ssd, w_out)
    return out_lat, out_ctx

def moe_ffn(h, w_router, router_bias, w_e_gate, w_e_up, w_e_down, w_sh_gate, w_sh_up, w_sh_down):
    n_tok, d = h.shape
    scores = jax.nn.sigmoid((h @ w_router).astype(jnp.float32))
    sel = scores + router_bias.astype(jnp.float32)
    grp = sel.reshape(n_tok, N_EXPERT_GROUPS, N_EXPERTS // N_EXPERT_GROUPS)
    grp_score = lax.top_k(grp, 2)[0].sum(-1)
    top_g = lax.top_k(grp_score, TOPK_GROUPS)[1]
    gmask = jax.nn.one_hot(top_g, N_EXPERT_GROUPS, dtype=jnp.float32).sum(1) > 0
    emask = jnp.repeat(gmask, N_EXPERTS // N_EXPERT_GROUPS, axis=1)
    top_e = lax.top_k(jnp.where(emask, sel, -jnp.inf), TOP_K)[1]
    wts = jnp.take_along_axis(scores, top_e, axis=1)
    wts = wts / jnp.sum(wts, axis=-1, keepdims=True) * ROUTED_SCALE

    n_assign = n_tok * TOP_K
    n_blocks = -(-n_assign // MOE_BLOCK) + N_EXPERTS
    n_pad = n_blocks * MOE_BLOCK
    e_flat = top_e.reshape(-1)
    order = jnp.argsort(e_flat)
    e_sorted = e_flat[order]
    tok_sorted = (jnp.arange(n_assign, dtype=jnp.int32) // TOP_K)[order]
    w_sorted = wts.reshape(-1)[order]
    counts = jnp.bincount(e_flat, length=N_EXPERTS)
    start = jnp.cumsum(counts) - counts
    padded = (counts + MOE_BLOCK - 1) // MOE_BLOCK * MOE_BLOCK
    pend = jnp.cumsum(padded)
    pstart = pend - padded
    dest = pstart[e_sorted] + jnp.arange(n_assign, dtype=jnp.int32) - start[e_sorted]
    buf_tok = jnp.zeros((n_pad,), jnp.int32).at[dest].set(tok_sorted)
    buf_w = jnp.zeros((n_pad,), jnp.float32).at[dest].set(w_sorted)
    block_e = jnp.minimum(jnp.searchsorted(pend, jnp.arange(n_blocks, dtype=jnp.int32) * MOE_BLOCK, side='right'), N_EXPERTS - 1)

    def expert_block(args):
        tok_b, w_b, e = args
        xb = h[tok_b]
        hid = jax.nn.silu(xb @ w_e_gate[e]) * (xb @ w_e_up[e])
        return (hid @ w_e_down[e]) * w_b[:, None].astype(h.dtype)

    out = lax.map(expert_block, (buf_tok.reshape(n_blocks, MOE_BLOCK), buf_w.reshape(n_blocks, MOE_BLOCK), block_e))
    routed = jax.ops.segment_sum(out.reshape(n_pad, d), buf_tok, num_segments=n_tok)
    shared = (jax.nn.silu(h @ w_sh_gate) * (h @ w_sh_up)) @ w_sh_down
    return routed + shared

def first_inputs(seed: int = 0) -> dict:
    key = jax.random.key(seed)
    ks = jax.random.split(key, 40)
    f32 = jnp.float32

    def nrm(k, shape, scale):
        return jax.random.normal(k, shape, f32) * scale

    def gain(k, shape):
        return 1.0 + 0.05 * jax.random.normal(k, shape, f32)

    u_dt = jax.random.uniform(ks[18], (DEPTH, 2, SSD_HEADS), f32)
    dt0 = jnp.exp(u_dt * (math.log(0.1) - math.log(0.001)) + math.log(0.001))
    return {
        'x': nrm(ks[0], (BATCH, SEQ, D_MODEL), 1.0),
        'c': nrm(ks[1], (BATCH, D_MODEL), 1.0),
        'ctx': nrm(ks[2], (BATCH, CTX_LEN, D_MODEL), 1.0),
        'c_ctx': nrm(ks[3], (D_MODEL,), 1.0),
        'w_ada': nrm(ks[4], (DEPTH, D_MODEL, 6 * D_MODEL), 0.5 * D_MODEL ** -0.5),
        'b_ada': nrm(ks[5], (DEPTH, 6 * D_MODEL), 0.02),
        'g_pre_mix': gain(ks[6], (DEPTH, D_MODEL)),
        'g_post_mix': gain(ks[7], (DEPTH, D_MODEL)),
        'g_pre_ffn': gain(ks[8], (DEPTH, D_MODEL)),
        'g_post_ffn': gain(ks[9], (DEPTH, D_MODEL)),
        'w_in': nrm(ks[10], (DEPTH, D_MODEL, IN_COLS), D_MODEL ** -0.5),
        'lam_q1': nrm(ks[11], (DEPTH, ATTN_DH), 0.1),
        'lam_k1': nrm(ks[12], (DEPTH, ATTN_DH), 0.1),
        'lam_q2': nrm(ks[13], (DEPTH, ATTN_DH), 0.1),
        'lam_k2': nrm(ks[14], (DEPTH, ATTN_DH), 0.1),
        'g_attn_subln': gain(ks[15], (DEPTH, ATTN_DV)),
        'conv_w': nrm(ks[16], (DEPTH, SSD_CONV_W, XBC_DIM), SSD_CONV_W ** -0.5),
        'conv_b': nrm(ks[17], (DEPTH, XBC_DIM), 0.02),
        'dt_bias': dt0 + jnp.log(-jnp.expm1(-dt0)),
        'a_log': jnp.log(jax.random.uniform(ks[19], (DEPTH, 2, SSD_HEADS), f32, 1.0, 16.0)),
        'd_skip': gain(ks[20], (DEPTH, SSD_HEADS)),
        'g_ssd_norm': gain(ks[21], (DEPTH, D_SSD)),
        'w_branch_attn': nrm(ks[22], (DEPTH, ATTN_V_DIM, D_MODEL), ATTN_V_DIM ** -0.5),
        'w_branch_ssd': nrm(ks[23], (DEPTH, D_SSD, D_MODEL), D_SSD ** -0.5),
        'w_out': nrm(ks[24], (DEPTH, D_MODEL, D_MODEL), D_MODEL ** -0.5),
        'w_router': nrm(ks[25], (DEPTH, D_MODEL, N_EXPERTS), D_MODEL ** -0.5),
        'router_bias': nrm(ks[26], (DEPTH, N_EXPERTS), 0.01),
        'w_e_gate': nrm(ks[27], (DEPTH, N_EXPERTS, D_MODEL, EXPERT_FF), D_MODEL ** -0.5),
        'w_e_up': nrm(ks[28], (DEPTH, N_EXPERTS, D_MODEL, EXPERT_FF), D_MODEL ** -0.5),
        'w_e_down': nrm(ks[29], (DEPTH, N_EXPERTS, EXPERT_FF, D_MODEL), EXPERT_FF ** -0.5),
        'w_sh_gate': nrm(ks[30], (DEPTH, D_MODEL, SHARED_FF), D_MODEL ** -0.5),
        'w_sh_up': nrm(ks[31], (DEPTH, D_MODEL, SHARED_FF), D_MODEL ** -0.5),
        'w_sh_down': nrm(ks[32], (DEPTH, SHARED_FF, D_MODEL), SHARED_FF ** -0.5),
    }

def first_block(x, c, ctx, c_ctx, w_ada, b_ada, g_pre_mix, g_post_mix, g_pre_ffn, g_post_ffn, w_in, lam_q1, lam_k1, lam_q2, lam_k2, g_attn_subln, conv_w, conv_b, dt_bias, a_log, d_skip, g_ssd_norm, w_branch_attn, w_branch_ssd, w_out, w_router, router_bias, w_e_gate, w_e_up, w_e_down, w_sh_gate, w_sh_up, w_sh_down):
    nb, ns, d = x.shape
    for li in range(DEPTH):
        update_ctx = li < DEPTH - 1
        lam_init = 0.8 - 0.6 * math.exp(-0.3 * li)
        mod = jax.nn.silu(c) @ w_ada[li] + b_ada[li]
        sh1, sc1, gt1, sh2, sc2, gt2 = jnp.split(mod[:, None, :], 6, axis=-1)
        mod_c = jax.nn.silu(c_ctx) @ w_ada[li] + b_ada[li]
        sh1c, sc1c, gt1c, sh2c, sc2c, gt2c = jnp.split(mod_c, 6)

        h = modulate(rmsnorm(x, g_pre_mix[li]), sh1, sc1)
        hc = modulate(rmsnorm(ctx, g_pre_mix[li]), sh1c, sc1c)
        mix, mix_c = token_mixer(h, hc, update_ctx, lam_init, w_in[li], lam_q1[li], lam_k1[li], lam_q2[li], lam_k2[li], g_attn_subln[li], conv_w[li], conv_b[li], dt_bias[li], a_log[li], d_skip[li], g_ssd_norm[li], w_branch_attn[li], w_branch_ssd[li], w_out[li])
        x = x + gt1 * rmsnorm(mix, g_post_mix[li])

        h = modulate(rmsnorm(x, g_pre_ffn[li]), sh2, sc2)
        moe_w = (w_router[li], router_bias[li], w_e_gate[li], w_e_up[li], w_e_down[li], w_sh_gate[li], w_sh_up[li], w_sh_down[li])
        if update_ctx:
            ctx = ctx + gt1c * rmsnorm(mix_c, g_post_mix[li])
            hc = modulate(rmsnorm(ctx, g_pre_ffn[li]), sh2c, sc2c)
            f = moe_ffn(jnp.concatenate([h.reshape(-1, d), hc.reshape(-1, d)], axis=0), *moe_w)
            f_lat = f[: nb * ns]
            ctx = ctx + gt2c * rmsnorm(f[nb * ns:].reshape(ctx.shape), g_post_ffn[li])
        else:
            f_lat = moe_ffn(h.reshape(-1, d), *moe_w)
        x = x + gt2 * rmsnorm(f_lat.reshape(x.shape), g_post_ffn[li])
    return x


DEPTH_2 = 2

HEAD_DIM = 64
A_GROUPS = ((128, 1), (512, 4), (2048, 16))
A_HEADS_PER_GROUP = 4
A_HEADS = A_HEADS_PER_GROUP * len(A_GROUPS)
A_WIDTH = A_HEADS * HEAD_DIM
B_HEADS = D_MODEL // HEAD_DIM
B_WIDTH = B_HEADS * HEAD_DIM
N_A = DEPTH_2 // 2
N_B = DEPTH_2 - N_A
D_FF = 2816
CONV_W = 3
ROPE_DIM = HEAD_DIM // 4
ROPE_THETA_2 = 500000.0
BLK = 128
NEG = -1e30


def rms_norm(x, g):
    x32 = x.astype(jnp.float32)
    y = x32 * lax.rsqrt(jnp.mean(x32 * x32, axis=-1, keepdims=True) + EPS)
    return (y * g.astype(jnp.float32)).astype(x.dtype)

def rope_tables(T):
    pos = jnp.arange(T, dtype=jnp.float32)
    inv = ROPE_THETA_2 ** (-jnp.arange(0, ROPE_DIM, 2, dtype=jnp.float32) / ROPE_DIM)
    ang = pos[:, None] * inv[None, :]
    return jnp.cos(ang), jnp.sin(ang)

def apply_rope_2(t, cos, sin):
    half = ROPE_DIM // 2
    c = cos[None, :, None, :].astype(t.dtype)
    s = sin[None, :, None, :].astype(t.dtype)
    x1 = t[..., :half]
    x2 = t[..., half:ROPE_DIM]
    return jnp.concatenate([x1 * c - x2 * s, x2 * c + x1 * s, t[..., ROPE_DIM:]], axis=-1)

def banded_attention(q, k, v, n_back):
    N, L, H, D = q.shape
    nb = L // BLK
    qb = q.reshape(N, nb, BLK, H, D)
    kb = k.reshape(N, nb, BLK, H, D)
    vb = v.reshape(N, nb, BLK, H, D)

    def with_prev(t):
        prev = jnp.pad(t[:, :-1], ((0, 0), (1, 0), (0, 0), (0, 0), (0, 0)))
        return jnp.concatenate([prev, t], axis=2)

    kc, vc = with_prev(kb), with_prev(vb)
    s = jnp.einsum('nbqhd,nbkhd->nbhqk', qb, kc).astype(jnp.float32) * (D ** -0.5)
    rel = (jnp.arange(BLK)[:, None] + BLK) - jnp.arange(2 * BLK)[None, :]
    band = (rel >= 0) & (rel <= n_back)
    has_prev = (jnp.arange(nb)[:, None, None] > 0) | (jnp.arange(2 * BLK)[None, None, :] >= BLK)
    mask = band[None] & has_prev
    s = jnp.where(mask[None, :, None], s, NEG)
    m = jnp.max(s, axis=-1, keepdims=True)
    p = jnp.exp(s - m)
    l = jnp.sum(p, axis=-1, keepdims=True)
    o = jnp.einsum('nbhqk,nbkhd->nbqhd', (p / l).astype(v.dtype), vc)
    lse = (m + jnp.log(l))[..., 0]
    return o.reshape(N, L, H, D), lse.transpose(0, 1, 3, 2).reshape(N, L, H)

def dilated_mixer(xn, w_qkv, w_o, cos, sin):
    B, T, _ = xn.shape
    qkv = xn @ w_qkv
    q, k, v = jnp.split(qkv, 3, axis=-1)
    q = apply_rope_2(q.reshape(B, T, A_HEADS, HEAD_DIM), cos, sin)
    k = apply_rope_2(k.reshape(B, T, A_HEADS, HEAD_DIM), cos, sin)
    v = v.reshape(B, T, A_HEADS, HEAD_DIM)
    G = A_HEADS_PER_GROUP
    outs, lses = [], []
    for g, (window, r) in enumerate(A_GROUPS):
        L = T // r
        Lp = -(-L // BLK) * BLK

        def gather(t):
            t = t[:, :, g * G:(g + 1) * G].reshape(B, L, r, G, HEAD_DIM)
            t = t.transpose(0, 2, 1, 3, 4).reshape(B * r, L, G, HEAD_DIM)
            return jnp.pad(t, ((0, 0), (0, Lp - L), (0, 0), (0, 0)))

        o, lse = banded_attention(gather(q), gather(k), gather(v), window // r)
        o = o[:, :L].reshape(B, r, L, G, HEAD_DIM).transpose(0, 2, 1, 3, 4).reshape(B, T, G, HEAD_DIM)
        lse = lse[:, :L].reshape(B, r, L, G).transpose(0, 2, 1, 3).reshape(B, T, G)
        outs.append(o)
        lses.append(lse)
    alpha = jax.nn.softmax(jnp.stack(lses, axis=0), axis=0)
    o = jnp.concatenate([outs[g] * alpha[g][..., None].astype(outs[g].dtype)
                         for g in range(len(A_GROUPS))], axis=2)
    return o.reshape(B, T, A_WIDTH) @ w_o

def fox_mixer(xn, w_q, w_o, k, v, c):
    B, T, _ = xn.shape
    q = (xn @ w_q).reshape(B, T, B_HEADS, HEAD_DIM)
    c_t = c.transpose(0, 2, 1)
    scale = HEAD_DIM ** -0.5
    outs = []
    for i in range(T // BLK):
        q0, q1 = i * BLK, (i + 1) * BLK
        s = jnp.einsum('bqhd,bkhd->bhqk', q[:, q0:q1], k[:, :q1]).astype(jnp.float32) * scale
        s = s + (c_t[:, :, q0:q1, None] - c_t[:, :, None, :q1])
        causal = jnp.arange(q0, q1)[:, None] >= jnp.arange(q1)[None, :]
        s = jnp.where(causal, s, NEG)
        p = jax.nn.softmax(s, axis=-1).astype(v.dtype)
        outs.append(jnp.einsum('bhqk,bkhd->bqhd', p, v[:, :q1]))
    o = jnp.concatenate(outs, axis=1)
    return o.reshape(B, T, B_WIDTH) @ w_o

def conv_ffn(xn, w_up, cw, cb, w_down):
    a = xn @ w_up
    T = a.shape[1]
    ap = jnp.pad(a, ((0, 0), (CONV_W - 1, 0), (0, 0)))
    a = sum(ap[:, j:j + T] * cw[j] for j in range(CONV_W)) + cb
    gate, val = jnp.split(a, 2, axis=-1)
    return (jax.nn.gelu(gate, approximate=True) * val) @ w_down

def second_inputs(seed: int = 0) -> dict:
    key = jax.random.key(seed)
    ks = jax.random.split(key, 14)

    def nrm(k, shape, fan_in):
        return jax.random.normal(k, shape, jnp.float32) * fan_in ** -0.5

    return {
        "x": jax.random.normal(ks[0], (BATCH, SEQ, D_MODEL), jnp.float32),
        "norm_gains": 1.0 + 0.05 * jax.random.normal(ks[1], (DEPTH_2, 4, D_MODEL), jnp.float32),
        "w_qkv_a": nrm(ks[2], (N_A, D_MODEL, 3 * A_WIDTH), D_MODEL),
        "w_o_a": nrm(ks[3], (N_A, A_WIDTH, D_MODEL), A_WIDTH),
        "w_q_b": nrm(ks[4], (N_B, D_MODEL, B_WIDTH), D_MODEL),
        "w_o_b": nrm(ks[5], (N_B, B_WIDTH, D_MODEL), B_WIDTH),
        "kv_norm": 1.0 + 0.05 * jax.random.normal(ks[6], (D_MODEL,), jnp.float32),
        "w_kvf": nrm(ks[7], (D_MODEL, 2 * B_WIDTH + B_HEADS), D_MODEL),
        "b_f": 3.0 + 0.5 * jax.random.normal(ks[8], (B_HEADS,), jnp.float32),
        "w_up": nrm(ks[9], (DEPTH_2, D_MODEL, 2 * D_FF), D_MODEL),
        "conv_w": nrm(ks[10], (DEPTH_2, CONV_W, 2 * D_FF), CONV_W),
        "conv_b": 0.01 * jax.random.normal(ks[11], (DEPTH_2, 2 * D_FF), jnp.float32),
        "w_down": nrm(ks[12], (DEPTH_2, D_FF, D_MODEL), D_FF),
    }

def second_block(x, norm_gains, w_qkv_a, w_o_a, w_q_b, w_o_b, kv_norm, w_kvf, b_f,
              w_up, conv_w, conv_b, w_down):
    B, T, _ = x.shape
    cos, sin = rope_tables(T)
    h = x
    k_sh = v_sh = c_sh = None
    for l in range(DEPTH_2):
        g = norm_gains[l]
        if l < N_A:
            mix = dilated_mixer(rms_norm(h, g[0]), w_qkv_a[l], w_o_a[l], cos, sin)
        else:
            if l == N_A:
                kvf = rms_norm(h, kv_norm) @ w_kvf
                k_sh = kvf[..., :B_WIDTH].reshape(B, T, B_HEADS, HEAD_DIM)
                v_sh = kvf[..., B_WIDTH:2 * B_WIDTH].reshape(B, T, B_HEADS, HEAD_DIM)
                log_f = jax.nn.log_sigmoid((kvf[..., 2 * B_WIDTH:] + b_f).astype(jnp.float32))
                c_sh = jnp.cumsum(log_f, axis=1)
            j = l - N_A
            mix = fox_mixer(rms_norm(h, g[0]), w_q_b[j], w_o_b[j], k_sh, v_sh, c_sh)
        h = h + rms_norm(mix, g[1])
        f = conv_ffn(rms_norm(h, g[2]), w_up[l], conv_w[l], conv_b[l], w_down[l])
        h = h + rms_norm(f, g[3])
    return h


def setup_inputs(seed=0):
    out = dict(first_inputs(seed))
    for name, value in second_inputs(seed + 1).items():
        if name != "x":
            out[name + "_2"] = value
    return out


def reference(
    x, c, ctx, c_ctx, w_ada, b_ada, g_pre_mix, g_post_mix, g_pre_ffn, g_post_ffn, w_in, lam_q1,
    lam_k1, lam_q2, lam_k2, g_attn_subln, conv_w, conv_b, dt_bias, a_log, d_skip, g_ssd_norm,
    w_branch_attn, w_branch_ssd, w_out, w_router, router_bias, w_e_gate, w_e_up, w_e_down,
    w_sh_gate, w_sh_up, w_sh_down, norm_gains_2, w_qkv_a_2, w_o_a_2, w_q_b_2, w_o_b_2,
    kv_norm_2, w_kvf_2, b_f_2, w_up_2, conv_w_2, conv_b_2, w_down_2,
):
    x = first_block(
        x, c, ctx, c_ctx, w_ada, b_ada, g_pre_mix, g_post_mix, g_pre_ffn, g_post_ffn, w_in,
        lam_q1, lam_k1, lam_q2, lam_k2, g_attn_subln, conv_w, conv_b, dt_bias, a_log, d_skip,
        g_ssd_norm, w_branch_attn, w_branch_ssd, w_out, w_router, router_bias, w_e_gate, w_e_up,
        w_e_down, w_sh_gate, w_sh_up, w_sh_down,
    )
    return second_block(
        x, norm_gains_2, w_qkv_a_2, w_o_a_2, w_q_b_2, w_o_b_2, kv_norm_2, w_kvf_2, b_f_2,
        w_up_2, conv_w_2, conv_b_2, w_down_2,
    )


_drawn_inputs = setup_inputs


def setup_inputs(seed=0):
    import zlib

    import numpy as np

    out = dict(_drawn_inputs(seed))
    spreads = {}
    factors = {'lam_k2': 2.92, 'd_skip': 2.817, 'conv_b_2': 4.95}
    for name, (base, spread) in spreads.items():
        noise = np.random.default_rng([zlib.crc32(name.encode()), seed]).standard_normal(out[name].shape)
        drawn = base * np.exp(spread * noise) if base else spread * noise
        out[name] = jnp.asarray(drawn.astype(out[name].dtype))
    for name, factor in factors.items():
        out[name] = (out[name] * factor).astype(out[name].dtype)
    return out
```

```python
import numpy as np
import concourse.bass as bass
from concourse import mybir
from contextlib import ExitStack

F32 = mybir.dt.float32
ACT = mybir.ActivationFunctionType
ALU = mybir.AluOpType
AX = mybir.AxisListType.X

P = 128
D = 1024
KD = D // P
SEQ = 512
NT = SEQ // P
CTX = 256
NC = CTX // P
EPS = 1e-6
GW = 512
SLOTS = 3


class Link:

    def __init__(self, sem):
        self.sem, self.n = sem, 0

    def __call__(self, eng, ins):
        self.n += 1
        ins.then_inc(self.sem, 1)
        eng.wait_ge(self.sem, self.n)


class Ring:

    def __init__(self, buf, landed, used):
        self.buf, self.landed, self.used = buf, landed, used
        self.sent, self.taken, self.owed = 0, 0, False
        self.filled = [0] * SLOTS

    def slot(self, n):
        return self.buf[:, n % SLOTS]


class Chip:

    def __init__(self, nc, ctx, t):
        self.nc, self.ctx, self.t = nc, ctx, t
        self.uid = 0
        self.sems = []
        self.ps = ctx.enter_context(nc.psum_tensor("banks", [P, 8, GW], F32))
        self.x = self.sb(ctx, "x_tok", [P, NT, D])
        self.hT = self.sb(ctx, "hT", [P, KD, SEQ])
        self.ident = self.sb(ctx, "ident", [P, P])
        self.vlink = Link(self.sem("vector_step"))
        self.alink = Link(self.sem("scalar_step"))
        self.glink = Link(self.sem("pool_step"))
        self.ring = Ring(self.sb(ctx, "weights", [P, SLOTS, KD * GW]),
                         [self.sem(f"weights_landed{i}") for i in range(SLOTS)], self.sem("weights_used"))
        self.gate = self.sb(ctx, "gate_rows", [P, 2, D])
        self.shift2 = self.sb(ctx, "shift2", [P, KD])
        self.scale2 = self.sb(ctx, "scale2", [P, KD])
        self.half = self.sb(ctx, "minus_half", [P, 8])
        self.sems = []

    def sb(self, ctx, name, shape, dt=F32):
        self.uid += 1
        return ctx.enter_context(self.nc.sbuf_tensor(f"{name}_{self.uid}", shape, dt))

    def sem(self, name):
        self.uid += 1
        s = self.nc.alloc_semaphore(f"{name}_{self.uid}")
        self.sems.append(s)
        return s

    def clear_sems(self):
        self.nc.clear_and_free_semaphores(self.sems)
        self.nc.all_engine_barrier()
        self.sems = []


def cols(ap, c0, n=GW):
    return ap[:, c0:c0 + n].rearrange("(k p) n -> p k n", p=P)


def load_weights(c, sp, tiles):
    r = c.ring
    for parts in tiles:
        n = r.sent
        if n >= SLOTS:
            sp.wait_ge(r.used, n - SLOTS + 1)
        for at, k, w, src in parts:
            dst = r.slot(n)[:, at:at + k * w].rearrange("p (k w) -> p k w", k=k)
            sp.dma_start(dst, src).then_inc(r.landed[n % SLOTS], 16)
        r.sent += 1


def whole(src):
    k, w = src.shape[1], src.shape[2]
    return [(0, k, w, src)]


def take(c, pe, parts):
    c.ring.owed = c.ring.taken > 0
    r = c.ring
    n = r.taken
    r.taken += 1
    r.filled[n % SLOTS] += 16 * parts
    pe.wait_ge(r.landed[n % SLOTS], r.filled[n % SLOTS])
    return r.slot(n)


def mm(c, out, lhs, rhs, start, stop):
    ins = c.nc.tensor.matmul(out, lhs, rhs, start=start, stop=stop)
    if c.ring.owed:
        c.ring.owed = False
        ins.then_inc(c.ring.used, 1)
    return ins


def norm_transpose(c, src, nt, outs, order=None, eps_scale=1.0 / D, dynamic=None):
    nc = c.nc
    with ExitStack() as s:
        sq = c.sb(s, "squares", [P, D])
        ss = c.sb(s, "sum_squares", [P, nt])
        rs = c.sb(s, "rstd", [P, nt])
        xs = c.sb(s, "x_scaled", [P, 2, D])
        summed = c.sem("nt_summed")
        meaned = c.sem("nt_meaned")
        rooted = c.sem("nt_rooted")
        scaled = c.sem("nt_scaled")
        turned = c.sem("nt_turned")
        taken_v = c.sem("nt_taken_v")
        taken_a = c.sem("nt_taken_a")
        block = s.enter_context(nc.Block())

        @block.scalar
        def _(act):
            for t in range(nt):
                if t:
                    act.wait_ge(summed, t)
                nc.scalar.activation(sq[:], src[:, t], ACT.Square, accum_out=ss[:, t:t + 1]).then_inc(summed, 1)
            for t in range(nt):
                act.wait_ge(turned, 2 * t + 2)
                for k in range(4, 8):
                    for dst, gain, shift in outs:
                        last = nc.scalar.activation(dst(k, t), turned_block(c, t, k, order), ACT.Identity,
                                                    scale=gain(k), bias=shift(k) if shift else 0.0)
                last.then_inc(taken_a, 1)

        @block.gpsimd
        def _(pool):
            pool.wait_ge(meaned, 1)
            nc.gpsimd.tensor_tensor(rs[:], rs[:], c.half[:, 0:nt], ALU.pow).then_inc(rooted, 1)

        @block.vector
        def _(dve):
            dve.wait_ge(summed, nt)
            nc.vector.tensor_scalar(rs[:], ss[:], eps_scale, EPS, ALU.mult, ALU.add).then_inc(meaned, 1)
            dve.wait_ge(rooted, 1)
            for t in range(nt + 1):
                if t < nt:
                    if t >= 2:
                        dve.wait_ge(turned, 2 * t - 2)
                    nc.vector.tensor_scalar(xs[:, t % 2], src[:, t], rs[:, t:t + 1], None, ALU.mult).then_inc(scaled, 1)
                if t:
                    u = t - 1
                    dve.wait_ge(turned, 2 * u + 1)
                    for k in range(4):
                        for dst, gain, shift in outs:
                            if shift:
                                last = nc.vector.tensor_scalar(dst(k, u), turned_block(c, u, k, order), gain(k), shift(k),
                                                               ALU.mult, ALU.add)
                            else:
                                last = nc.vector.tensor_scalar(dst(k, u), turned_block(c, u, k, order), gain(k), None, ALU.mult)
                    last.then_inc(taken_v, 1)

        @block.tensor
        def _(pe):
            for t in range(nt):
                pe.wait_ge(scaled, t + 1)
                if t >= 2:
                    pe.wait_ge(taken_v, t - 1)
                    pe.wait_ge(taken_a, t - 1)
                for k in range(KD):
                    b = 2 * (t % 2) + k // 4
                    last = nc.tensor.transpose(c.ps[:, b, (k % 4) * P:(k % 4 + 1) * P], xs[:, t % 2, k * P:(k + 1) * P],
                                               c.ident[:])
                    if k % 4 == 3:
                        last.then_inc(turned, 1)


def turned_block(c, t, k, order):
    blk = c.ps[:, 2 * (t % 2) + k // 4, (k % 4) * P:(k % 4 + 1) * P]
    return order(blk) if order else blk


def plain_transpose(c, src, nt, nk, dst, gain):
    nc = c.nc
    with ExitStack() as s:
        turned = c.sem("pt_turned")
        taken_v = c.sem("pt_taken_v")
        taken_a = c.sem("pt_taken_a")
        block = s.enter_context(nc.Block())

        @block.scalar
        def _(act):
            for t in range(nt):
                act.wait_ge(turned, 2 * t + 2)
                for k in range(4, nk):
                    last = nc.scalar.activation(dst(k, t), turned_block(c, t, k, None), ACT.Copy, scale=gain(k) if gain else 1.0)
                last.then_inc(taken_a, 1)

        @block.vector
        def _(dve):
            for t in range(nt):
                dve.wait_ge(turned, 2 * t + 1)
                for k in range(4):
                    if gain:
                        last = nc.vector.tensor_scalar(dst(k, t), turned_block(c, t, k, None), gain(k), None, ALU.mult)
                    else:
                        last = nc.vector.tensor_copy(dst(k, t), turned_block(c, t, k, None))
                last.then_inc(taken_v, 1)

        @block.tensor
        def _(pe):
            for t in range(nt):
                if t >= 2:
                    pe.wait_ge(taken_v, t - 1)
                    pe.wait_ge(taken_a, t - 1)
                for k in range(nk):
                    b = 2 * (t % 2) + k // 4
                    last = nc.tensor.transpose(c.ps[:, b, (k % 4) * P:(k % 4 + 1) * P], src(t)[:, k * P:(k + 1) * P],
                                               c.ident[:])
                    if k in (3, nk - 1):
                        last.then_inc(turned, 1)


def project_residual(c, w_halves, lhs, gain_b):
    nc = c.nc
    with ExitStack() as s:
        f = c.sb(s, "f", [P, NT, D])
        sq = c.sb(s, "squares", [P, GW])
        ss = c.sb(s, "sum_squares", [P, NT, 2])
        rs = c.sb(s, "rstd", [P, NT])
        done = c.sem("pr_done")
        summed = c.sem("pr_summed")
        copied = c.sem("pr_copied")
        meaned = c.sem("pr_meaned")
        rooted = c.sem("pr_rooted")
        block = s.enter_context(nc.Block())

        @block.sync
        def _(sp):
            load_weights(c, sp, [whole(src) for half in w_halves for k, src in half])

        @block.tensor
        def _(pe):
            for hf, half in enumerate(w_halves):
                total = sum(k for k, _ in half)
                k0 = 0
                for k, _ in half:
                    w = take(c, pe, 1).rearrange("p (k n) -> p k n", n=GW)
                    for t in range(NT):
                        for j in range(k):
                            last = mm(c, c.ps[:, 4 * hf + t], lhs(k0 + j, t), w[:, j],
                                      k0 + j == 0, k0 + j == total - 1)
                        if k0 + k == total:
                            last.then_inc(done, 1)
                    k0 += k

        @block.scalar
        def _(act):
            for i in range(2 * NT):
                hf, t = divmod(i, NT)
                act.wait_ge(copied, i + 1)
                if i:
                    act.wait_ge(summed, i)
                nc.scalar.activation(sq[:], f[:, t, hf * GW:(hf + 1) * GW], ACT.Square,
                                     accum_out=ss[:, t, hf:hf + 1]).then_inc(summed, 1)

        @block.gpsimd
        def _(pool):
            pool.wait_ge(meaned, 1)
            nc.gpsimd.tensor_tensor(rs[:], rs[:], c.half[:, 0:NT], ALU.pow).then_inc(rooted, 1)

        @block.vector
        def _(dve):
            for i in range(2 * NT):
                hf, t = divmod(i, NT)
                dve.wait_ge(done, i + 1)
                nc.vector.tensor_copy(f[:, t, hf * GW:(hf + 1) * GW], c.ps[:, i]).then_inc(copied, 1)
            dve.wait_ge(summed, 2 * NT)
            c.vlink(dve, nc.vector.tensor_tensor(rs[:], ss[:, :, 0], ss[:, :, 1], ALU.add))
            nc.vector.tensor_scalar(rs[:], rs[:], 1.0 / D, EPS, ALU.mult, ALU.add).then_inc(meaned, 1)
            dve.wait_ge(rooted, 1)
            dve.wait_ge(copied, 2 * NT)
            for t in range(NT):
                last = nc.vector.scalar_tensor_tensor(f[:, t], f[:, t], rs[:, t:t + 1], gain_b, ALU.mult, ALU.mult)
                if t == NT - 1:
                    c.vlink(dve, last)
            for t in range(NT):
                nc.vector.tensor_tensor(c.x[:, t], c.x[:, t], f[:, t], ALU.add)
NEG = -1e30
A_HEADS, A_W = 12, 768
KA = A_W // P
B_HEADS = 16
DH = 64
FF = 2816
KF = FF // P
FT = 256


def attention(c, units, finish=None):
    nc = c.nc
    U = len(units)
    with ExitStack() as s:
        pr = c.sb(s, "probs", [P, 2, SEQ])
        prT = c.sb(s, "probsT", [P, 2, NT, P])
        nm = c.sb(s, "minus_max", [P, 2])
        scored = c.sem("at_scored")
        maxed = c.sem("at_maxed")
        biased = c.sem("at_biased")
        expd = c.sem("at_exp")
        turned = c.sem("at_turned")
        copied = c.sem("at_copied")
        summed = c.sem("at_summed")
        left = c.sem("at_left")
        block = s.enter_context(nc.Block())

        @block.tensor
        def _(pe):
            for i in range(U + 2):
                if i < U:
                    u = units[i]
                    W = u["W"]
                    if i >= 2:
                        pe.wait_ge(expd, i - 1)
                    adds = u["adds"]
                    last = nc.tensor.matmul(c.ps[:, i % 2, 0:W], u["q"], u["k"], start=True, stop=not adds)
                    for n, (lhs, rhs, c0) in enumerate(adds):
                        last = nc.tensor.matmul(c.ps[:, i % 2, c0:W], lhs, rhs, start=False, stop=n == len(adds) - 1)
                    last.then_inc(scored, 1)
                if 0 <= i - 1 < U:
                    j = i - 1
                    u = units[j]
                    pe.wait_ge(expd, j + 1)
                    if j >= 2:
                        pe.wait_ge(copied, j - 1)
                    for b in range(u["W"] // P):
                        last = nc.tensor.transpose(c.ps[:, 2 + j % 2, b * P:(b + 1) * P], pr[:, j % 2, b * P:(b + 1) * P],
                                                   c.ident[:])
                    last.then_inc(turned, 1)
                if 0 <= i - 2 < U:
                    j = i - 2
                    u = units[j]
                    pe.wait_ge(copied, j + 1)
                    if j >= 2:
                        pe.wait_ge(left, j - 1)
                    nb = u["W"] // P
                    for b in range(nb):
                        last = nc.tensor.matmul(c.ps[:, 4 + j % 2, 0:DH], prT[:, j % 2, b], u["v"][b],
                                                start=b == 0, stop=b == nb - 1)
                    last.then_inc(summed, 1)

        @block.scalar
        def _(act):
            for i in range(U):
                u = units[i]
                act.wait_ge(biased, i + 1)
                if i >= 2:
                    act.wait_ge(turned, i - 1)
                nc.scalar.activation(pr[:, i % 2, 0:u["W"]], c.ps[:, i % 2, 0:u["W"]], ACT.Exp, bias=nm[:, i % 2:i % 2 + 1],
                                     scale=DH ** -0.5, accum_out=u["l"]).then_inc(expd, 1)

        @block.vector
        def _(dve):
            for i in range(U + 2):
                if i < U:
                    u = units[i]
                    dve.wait_ge(scored, i + 1)
                    nc.vector.reduce_max(u["m"], c.ps[:, i % 2, 0:u["W"]], AX).then_inc(maxed, 1)
                    dve.wait_ge(maxed, i + 1)
                    if i >= 2:
                        dve.wait_ge(expd, i - 1)
                    nc.vector.tensor_scalar(nm[:, i % 2:i % 2 + 1], u["m"], -DH ** -0.5, None, ALU.mult).then_inc(biased, 1)
                if 0 <= i - 1 < U:
                    j = i - 1
                    u = units[j]
                    dve.wait_ge(turned, j + 1)
                    if j >= 2:
                        dve.wait_ge(summed, j - 1)
                    nc.vector.tensor_copy(prT[:, j % 2, 0:u["W"] // P], c.ps[:, 2 + j % 2, 0:u["W"]]).then_inc(copied, 1)
                if 0 <= i - 2 < U:
                    j = i - 2
                    u = units[j]
                    dve.wait_ge(summed, j + 1)
                    nc.vector.tensor_copy(u["out"], c.ps[:, 4 + j % 2, 0:DH]).then_inc(left, 1)


def project_heads(c, jobs):
    nc = c.nc
    works = [(n, w) for n, (_, ws) in enumerate(jobs) for w in ws]
    ropes = [w for _, w in works if w["rope"]]
    place = [sum(bool(v["rope"]) == bool(w["rope"]) for _, v in works[:i]) for i, (_, w) in enumerate(works)]
    with ExitStack() as s:
        raw = c.sb(s, "unrotated", [P, 2, GW])
        turn = c.sb(s, "rotated", [P, GW])
        done = c.sem("ph_done")
        left = c.sem("ph_left")
        rawed = c.sem("ph_raw")
        rotd = c.sem("ph_rotated")
        roped = c.sem("ph_roped")
        mixed = c.sem("ph_mixed")
        block = s.enter_context(nc.Block())

        @block.sync
        def _(sp):
            load_weights(c, sp, [parts for parts, _ in jobs])

        @block.tensor
        def _(pe):
            def rotate(r):
                pe.wait_ge(rawed, r + 1)
                w = ropes[r]
                if r >= 2:
                    pe.wait_ge(mixed, r - 1)
                nc.tensor.matmul(c.ps[:, 4 + r % 2, 0:w["n"]], w["rope"][2], raw[:, r % 2, 0:w["n"]],
                                 start=True, stop=True).then_inc(rotd, 1)

            i, r = 0, 0
            pending = None
            for parts, ws in jobs:
                slot = take(c, pe, len(parts))
                for w in ws:
                    if i >= 4:
                        pe.wait_ge(rawed if works[i - 4][1]["rope"] else left, place[i - 4] + 1)
                    for k in range(KD):
                        last = mm(c, c.ps[0:w["m"], i % 4, 0:w["n"]], w["lhs"](slot, k), w["rhs"](slot, k), k == 0, k == KD - 1)
                    last.then_inc(done, 1)
                    if pending is not None:
                        rotate(pending)
                        pending = None
                    if w["rope"]:
                        pending = r
                        r += 1
                    i += 1
            if pending is not None:
                rotate(pending)

        @block.scalar
        def _(act):
            r = 0
            for i, (_, w) in enumerate(works):
                act.wait_ge(done, i + 1)
                n = w["n"]
                src = c.ps[0:w["m"], i % 4, 0:n]
                if w["rope"]:
                    if r >= 2:
                        act.wait_ge(roped, r - 1)
                    nc.scalar.activation(raw[:, r % 2, 0:n], src, ACT.Copy).then_inc(rawed, 1)
                    r += 1
                else:
                    nc.scalar.activation(w["out"], src, ACT.Copy).then_inc(left, 1)

        @block.vector
        def _(dve):
            for r, w in enumerate(ropes):
                n = w["n"]
                cos, sin, _ = w["rope"]
                dve.wait_ge(rotd, r + 1)
                if r:
                    dve.wait_ge(roped, r)
                nc.vector.tensor_tensor(turn[:, 0:n], c.ps[:, 4 + r % 2, 0:n], sin, ALU.mult).then_inc(mixed, 1)
                c.vlink(dve, nc.vector.tensor_tensor(w["out"], raw[:, r % 2, 0:n], cos, ALU.mult))
                dve.wait_ge(mixed, r + 1)
                nc.vector.tensor_tensor(w["out"], w["out"], turn[:, 0:n], ALU.add).then_inc(roped, 1)


def ffn_up(c, w_up, conv, bias, gT):
    nc = c.nc
    with ExitStack() as s:
        a = c.sb(s, "convolved", [P, 2, 2, SEQ])
        g = c.sb(s, "gelu", [P, 2, SEQ])
        done = c.sem("up_done")
        begun = c.sem("up_begun")
        middle = c.sem("up_middle")
        convd = c.sem("up_convd")
        gelud = c.sem("up_gelu")
        multd = c.sem("up_multiplied")
        block = s.enter_context(nc.Block())

        @block.sync
        def _(sp):
            load_weights(c, sp, [[(0, KD, FT, cols(w_up, j * FT, FT)), (KD * FT, KD, FT, cols(w_up, FF + j * FT, FT))]
                                 for j in range(FF // FT)])

        @block.tensor
        def _(pe):
            for j in range(FF // FT):
                w = take(c, pe, 2).rearrange("p (v k n) -> p v k n", v=2, k=KD)
                for f in range(2 * j, 2 * j + 2):
                    if f >= 4:
                        pe.wait_ge(convd, 2 * (f - 3))
                    for v in range(2):
                        for k in range(KD):
                            last = mm(c, c.ps[:, 2 * (f % 4) + v], w[:, v, k, (f % 2) * P:(f % 2 + 1) * P], c.hT[:, k], k == 0, k == KD - 1)
                        last.then_inc(done, 1)

        @block.scalar
        def _(act):
            for f in range(KF + 1):
                if f < KF:
                    for v in range(2):
                        act.wait_ge(done, 2 * f + v + 1)
                        if f >= 2:
                            act.wait_ge(multd, f - 1)
                        ch = v * KF + f
                        nc.scalar.activation(a[:, f % 2, v], c.ps[:, 2 * (f % 4) + v], ACT.Identity, scale=conv[:, 2, ch:ch + 1],
                                             bias=bias[:, ch:ch + 1]).then_inc(begun, 1)
                if f:
                    u = f - 1
                    act.wait_ge(convd, 2 * u + 2)
                    nc.scalar.activation(g[:, u % 2], a[:, u % 2, 0], ACT.Gelu_apprx_tanh).then_inc(gelud, 1)

        @block.vector
        def _(dve):
            for f in range(KF + 1):
                if f < KF:
                    for v in range(2):
                        ch = v * KF + f
                        dve.wait_ge(begun, 2 * f + v + 1)
                        nc.vector.scalar_tensor_tensor(a[:, f % 2, v, 1:], c.ps[:, 2 * (f % 4) + v, 0:SEQ - 1], conv[:, 1, ch:ch + 1],
                                                       a[:, f % 2, v, 1:], ALU.mult, ALU.add).then_inc(middle, 1)
                    for v in range(2):
                        ch = v * KF + f
                        dve.wait_ge(middle, 2 * f + v + 1)
                        nc.vector.scalar_tensor_tensor(a[:, f % 2, v, 2:], c.ps[:, 2 * (f % 4) + v, 0:SEQ - 2], conv[:, 0, ch:ch + 1],
                                                       a[:, f % 2, v, 2:], ALU.mult, ALU.add).then_inc(convd, 1)
                if f:
                    u = f - 1
                    dve.wait_ge(gelud, u + 1)
                    dve.wait_ge(convd, 2 * u + 2)
                    nc.vector.tensor_tensor(gT[:, u], g[:, u % 2], a[:, u % 2, 1], ALU.mult).then_inc(multd, 1)


def block2(c):
    nc, t = c.nc, c.t
    gains = t["norm_gains_2"]
    with ExitStack() as s2:
        gcol = c.sb(s2, "gain_columns", [P, 5, KD])
        grow = c.sb(s2, "gain_rows", [P, 4, D])
        got = c.sem("constants_landed")
        with ExitStack() as s:
            block = s.enter_context(nc.Block())

            @block.sync
            def _(sp):
                n = 0
                for l in range(2):
                    for i in range(2):
                        sp.dma_start(gcol[:, 2 * l + i], gains[l, 2 * i].rearrange("(k p) -> p k", p=P), allow_slow_non_contiguous=True).then_inc(got, 16)
                        sp.dma_start(grow[:, 2 * l + i], gains[l, 2 * i + 1:2 * i + 2].to_broadcast([P, D])).then_inc(got, 16)
                        n += 2
                sp.dma_start(gcol[:, 4], t["kv_norm_2"].rearrange("(k p) -> p k", p=P), allow_slow_non_contiguous=True).then_inc(got, 16)
                sp.wait_ge(got, 16 * (n + 1))

        def col(i):
            return lambda k: gcol[:, i, k:k + 1]

        def plain(k, tile):
            return c.hT[:, k, tile * P:(tile + 1) * P]

        def ffn(l):
            norm_transpose(c, c.x, NT, [(plain, col(2 * l + 1), None)])
            with ExitStack() as s:
                gT = c.sb(s, "gated", [P, KF, SEQ])
                conv = c.sb(s, "taps", [P, 3, 2 * KF])
                bias = c.sb(s, "conv_bias", [P, 2 * KF])
                landed = c.sem("taps_landed")
                with ExitStack() as b:
                    block = b.enter_context(nc.Block())

                    @block.sync
                    def _(sp):
                        for j in range(3):
                            sp.dma_start(conv[:, j], t["conv_w_2"][l, j].rearrange("(k p) -> p k", p=P), allow_slow_non_contiguous=True).then_inc(landed, 16)
                        sp.dma_start(bias[:], t["conv_b_2"][l].rearrange("(k p) -> p k", p=P), allow_slow_non_contiguous=True).then_inc(landed, 16)
                        sp.wait_ge(landed, 64)
                ffn_up(c, t["w_up_2"][l], conv, bias, gT)
                wd = t["w_down_2"][l]
                project_residual(c, [[(n, wd[k0 * P:(k0 + n) * P, hf * GW:(hf + 1) * GW].rearrange("(k p) n -> p k n", p=P))
                                      for k0, n in ((0, 8), (8, 8), (16, 6))] for hf in range(2)],
                                 lambda k, tile: gT[:, k, tile * P:(tile + 1) * P], grow[:, 2 * l + 1])

        norm_transpose(c, c.x, NT, [(lambda k, tile: c.hT[:, k].rearrange("p (c u) -> p u c", c=4)[:, 32 * tile:32 * tile + 32, :],
                                     col(0), None)], order=lambda a: a.rearrange("p (u c) -> p u c", c=4))
        with ExitStack() as s:
            o = c.sb(s, "heads_out", [P, NT, A_W])
            with ExitStack() as sa:
                qT = c.sb(sa, "qT", [P, KA, SEQ])
                kT = c.sb(sa, "kT", [P, KA, SEQ])
                v = c.sb(sa, "v", [P, NT, A_W])
                rope = c.sb(sa, "rope", [P, 2, SEQ])
                rot = c.sb(sa, "rotation", [P, P])
                band = c.sb(sa, "band", [P, NT, SEQ])
                diag = c.sb(sa, "diagonal_masks", [P, 2, P])
                m = c.sb(sa, "maxima", [P, NT, A_HEADS])
                l = c.sb(sa, "sums", [P, NT, A_HEADS])
                landed = c.sem("masks_landed")
                with ExitStack() as b:
                    block = b.enter_context(nc.Block())

                    @block.sync
                    def _(sp):
                        sp.dma_start(rope[:], t["rope2"].rearrange("a p n -> p a n")).then_inc(landed, 16)
                        sp.dma_start(rot[:], t["rot2"]).then_inc(landed, 16)
                        sp.dma_start(band[:], t["band"].rearrange("a p n -> p a n")).then_inc(landed, 16)
                        sp.dma_start(diag[:], t["diag"].rearrange("a p n -> p a n")).then_inc(landed, 16)
                        sp.wait_ge(landed, 64)
                jobs = []
                W3 = 3 * P
                for dst, off in ((qT, 0), (kT, A_W)):
                    for n in range(2):
                        jobs.append(([(0, KD, W3, cols(t["w_qkv_a_2"][0], off + n * W3, W3))],
                                     [dict(m=P, n=SEQ, out=dst[:, 3 * n + f], rope=(rope[:, 0], rope[:, 1], rot[:]),
                                           lhs=lambda w, k, f=f: w[:, k * W3 + f * P:k * W3 + (f + 1) * P],
                                           rhs=lambda w, k: c.hT[:, k]) for f in range(3)]))
                for n in range(2):
                    jobs.append(([(0, KD, W3, cols(t["w_qkv_a_2"][0], 2 * A_W + n * W3, W3))],
                                 [dict(m=P, n=W3, out=v[:, tile, n * W3:(n + 1) * W3], rope=None,
                                       lhs=lambda w, k, tile=tile: plain(k, tile),
                                       rhs=lambda w, k: w[:, k * W3:(k + 1) * W3]) for tile in range(NT)]))
                project_heads(c, jobs)
                units = []
                for cc in range(4):
                    for h in range(A_HEADS):
                        p0 = DH * (h % 2)
                        g = h // 4
                        keys = slice(0, SEQ) if g == 0 else slice(cc * P, (cc + 1) * P)
                        units.append(dict(
                            W=SEQ if g == 0 else P, q=qT[p0:p0 + DH, h // 2, cc * P:(cc + 1) * P], k=kT[p0:p0 + DH, h // 2, keys],
                            adds=[(c.ident[:], band[:, cc] if g == 0 else diag[:, g - 1], 0)],
                            v=[v[:, b, h * DH:(h + 1) * DH] for b in (range(NT) if g == 0 else [cc])],
                            out=o[:, cc, h * DH:(h + 1) * DH], m=m[:, cc, h:h + 1], l=l[:, cc, h:h + 1]))
                attention(c, units)
                with ExitStack() as b:
                    lse = c.sb(b, "lse", [P, NT, A_HEADS])
                    top = c.sb(b, "top", [P, NT, 4])
                    ready = c.sem("alpha_ready")
                    block = b.enter_context(nc.Block())

                    @block.scalar
                    def _(act):
                        nc.scalar.activation(lse[:], l[:], ACT.Ln).then_inc(ready, 1)
                        act.wait_ge(ready, 2)
                        nc.scalar.activation(lse[:], lse[:], ACT.Exp).then_inc(ready, 1)

                    @block.vector
                    def _(dve):
                        g = lambda i: lse[:, :, 4 * i:4 * i + 4]
                        L = lambda ins: c.vlink(dve, ins)
                        dve.wait_ge(ready, 1)
                        L(nc.vector.scalar_tensor_tensor(lse[:], m[:], DH ** -0.5, lse[:], ALU.mult, ALU.add))
                        L(nc.vector.tensor_tensor(top[:], g(0), g(1), ALU.max))
                        L(nc.vector.tensor_tensor(top[:], top[:], g(2), ALU.max))
                        L(nc.vector.tensor_tensor(g(0), g(0), top[:], ALU.subtract))
                        L(nc.vector.tensor_tensor(g(1), g(1), top[:], ALU.subtract))
                        nc.vector.tensor_tensor(g(2), g(2), top[:], ALU.subtract).then_inc(ready, 1)
                        dve.wait_ge(ready, 3)
                        L(nc.vector.tensor_tensor(top[:], g(0), g(1), ALU.add))
                        L(nc.vector.tensor_tensor(top[:], top[:], g(2), ALU.add))
                        L(nc.vector.reciprocal(top[:], top[:]))
                        L(nc.vector.reciprocal(l[:], l[:]))
                        for i in range(3):
                            L(nc.vector.tensor_tensor(g(i), g(i), top[:], ALU.mult))
                        L(nc.vector.tensor_tensor(lse[:], lse[:], l[:], ALU.mult))
                        for cc in range(4):
                            oc = o[:, cc].rearrange("p (h d) -> p h d", d=DH)
                            nc.vector.tensor_tensor(oc, oc, lse[:, cc].unsqueeze(2).to_broadcast([P, A_HEADS, DH]), ALU.mult)
            oT = c.sb(s, "oT", [P, KA, SEQ])
            plain_transpose(c, lambda tile: o[:, tile], NT, KA,
                            lambda k, cc: oT[:, k].rearrange("p (u c) -> p u c", c=4)[:, :, cc], None)
            wo = t["w_o_a_2"][0]
            project_residual(c, [[(KA, cols(wo, hf * GW))] for hf in range(2)],
                             lambda k, tile: oT[:, k, tile * P:(tile + 1) * P], grow[:, 0])
        ffn(0)

        with ExitStack() as s:
            o = c.sb(s, "heads_out", [P, NT, D])
            with ExitStack() as sa:
                hk = c.sb(sa, "hT_kv", [P, KD, SEQ])
                norm_transpose(c, c.x, NT, [(plain, col(2), None),
                                            (lambda k, tile: hk[:, k, tile * P:(tile + 1) * P], col(4), None)])
                qT = c.sb(sa, "qT", [P, KD, SEQ])
                kT = c.sb(sa, "kT", [P, KD, SEQ])
                v = c.sb(sa, "v", [P, NT, D])
                lf = c.sb(sa, "log_forget", [P, NT, B_HEADS])
                cT = c.sb(sa, "cumulated", [B_HEADS, SEQ])
                m = c.sb(sa, "maxima", [P, NT, B_HEADS])
                l = c.sb(sa, "sums", [P, NT, B_HEADS])
                tri = c.sb(sa, "triangles", [P, 3, P])
                pick = c.sb(sa, "minus_head", [B_HEADS, B_HEADS, P])
                bf = c.sb(sa, "forget_bias", [P, B_HEADS])
                landed = c.sem("fox_landed")
                jobs = []
                for w, c0, dst, src in ((t["w_q_b_2"][0], 0, qT, c.hT), (t["w_kvf_2"], 0, kT, hk)):
                    for n in range(2):
                        jobs.append(([(0, KD, GW, cols(w, c0 + n * GW))],
                                     [dict(m=P, n=SEQ, out=dst[:, 4 * n + f], rope=None,
                                           lhs=lambda w, k, f=f: w[:, k * GW + f * P:k * GW + (f + 1) * P],
                                           rhs=lambda w, k, src=src: src[:, k]) for f in range(4)]))
                for n in range(2):
                    jobs.append(([(0, KD, GW, cols(t["w_kvf_2"], D + n * GW))],
                                 [dict(m=P, n=GW, out=v[:, tile, n * GW:(n + 1) * GW], rope=None,
                                       lhs=lambda w, k, tile=tile: hk[:, k, tile * P:(tile + 1) * P],
                                       rhs=lambda w, k: w[:, k * GW:(k + 1) * GW]) for tile in range(NT)]))
                jobs.append(([(0, KD, B_HEADS, cols(t["w_kvf_2"], 2 * D, B_HEADS))],
                             [dict(m=P, n=B_HEADS, out=lf[:, tile], rope=None,
                                   lhs=lambda w, k, tile=tile: hk[:, k, tile * P:(tile + 1) * P],
                                   rhs=lambda w, k: w[:, k * B_HEADS:(k + 1) * B_HEADS]) for tile in range(NT)]))
                project_heads(c, jobs)
                with ExitStack() as b:
                    z = c.sb(b, "z", [P, NT, B_HEADS])
                    e = c.sb(b, "e", [P, NT, B_HEADS])
                    ready = c.sem("forget_ready")
                    summed = c.sem("forget_summed")
                    block = b.enter_context(nc.Block())

                    @block.sync
                    def _(sp):
                        sp.dma_start(tri[:, 0], t["tri"][0]).then_inc(landed, 16)
                        sp.dma_start(tri[:, 1], t["tri"][4]).then_inc(landed, 16)
                        sp.dma_start(tri[:, 2], t["causal"]).then_inc(landed, 16)
                        sp.dma_start(pick[:], t["pick"]).then_inc(landed, 16)
                        sp.dma_start(bf[:], t["b_f_2"].unsqueeze(0).to_broadcast([P, B_HEADS])).then_inc(landed, 16)
                        sp.wait_ge(landed, 80)

                    @block.scalar
                    def _(act):
                        act.wait_ge(ready, 1)
                        nc.scalar.activation(e[:], e[:], ACT.Exp, scale=-1.0).then_inc(ready, 1)
                        act.wait_ge(ready, 2)
                        nc.scalar.activation(e[:], e[:], ACT.Ln, bias=1.0).then_inc(ready, 1)

                    @block.vector
                    def _(dve):
                        L = lambda ins: c.vlink(dve, ins)
                        dve.wait_ge(landed, 80)
                        L(nc.vector.tensor_tensor(z[:], lf[:], bf[:].unsqueeze(1).to_broadcast([P, NT, B_HEADS]), ALU.add))
                        nc.vector.scalar_tensor_tensor(e[:], z[:], -1.0, z[:], ALU.mult, ALU.max).then_inc(ready, 1)
                        dve.wait_ge(ready, 3)
                        nc.vector.scalar_tensor_tensor(lf[:], z[:], 0.0, e[:], ALU.min, ALU.subtract).then_inc(ready, 1)
                        dve.wait_ge(summed, 1)
                        nc.vector.tensor_copy(cT[:], c.ps[0:B_HEADS, 0])

                    @block.tensor
                    def _(pe):
                        pe.wait_ge(ready, 4)
                        for i in range(NT):
                            for j in range(i + 1):
                                last = nc.tensor.matmul(c.ps[0:B_HEADS, 0, i * P:(i + 1) * P], lf[:, j], tri[:, 0 if j == i else 1],
                                                        start=j == 0, stop=j == i)
                        last.then_inc(summed, 1)
                units = []
                for i in range(NT):
                    for h in range(B_HEADS):
                        p0 = DH * (h % 2)
                        W = (i + 1) * P
                        units.append(dict(
                            W=W, q=qT[p0:p0 + DH, h // 2, i * P:(i + 1) * P], k=kT[p0:p0 + DH, h // 2, 0:W],
                            adds=[(pick[:, h], cT[:, 0:W], 0), (c.ident[:], tri[:, 2], i * P)],
                            v=[v[:, b, h * DH:(h + 1) * DH] for b in range(i + 1)],
                            out=o[:, i, h * DH:(h + 1) * DH], m=m[:, i, h:h + 1], l=l[:, i, h:h + 1]))
                attention(c, units)
                with ExitStack() as b:
                    block = b.enter_context(nc.Block())

                    @block.vector
                    def _(dve):
                        c.vlink(dve, nc.vector.reciprocal(l[:], l[:]))
                        for i in range(NT):
                            oi = o[:, i].rearrange("p (h d) -> p h d", d=DH)
                            nc.vector.tensor_tensor(oi, oi, l[:, i].unsqueeze(2).to_broadcast([P, B_HEADS, DH]), ALU.mult)
            oT = c.sb(s, "oT", [P, KD, SEQ])
            plain_transpose(c, lambda tile: o[:, tile], NT, KD, lambda k, tile: oT[:, k, tile * P:(tile + 1) * P], None)
            wo = t["w_o_b_2"][0]
            project_residual(c, [[(KD, cols(wo, hf * GW))] for hf in range(2)],
                             lambda k, tile: oT[:, k, tile * P:(tile + 1) * P], grow[:, 2])
        ffn(1)


def constants():
    i = np.arange(P)
    out = {"ident": np.eye(P)}
    le = i[:, None] <= i[None, :]
    out["tri"] = np.stack([le, i[:, None] > i[None, :], i[:, None] >= i[None, :], i[:, None] < i[None, :], le | True])
    out["causal"] = np.where(i[:, None] >= i[None, :], 0.0, NEG)
    tok = np.concatenate([np.arange(SEQ)[r::4] for r in range(4)])
    rel = tok[:, None] - tok[None, :]
    out["band"] = np.where((rel >= 0) & (rel <= 128), 0.0, NEG).reshape(NT, P, SEQ)
    causal = i[:, None] >= i[None, :]
    out["diag"] = np.stack([np.where(causal, 0.0, NEG), np.where(causal & (i[:, None] % 4 == i[None, :] % 4), 0.0, NEG)])
    pick = np.zeros((B_HEADS, B_HEADS, P))
    pick[np.arange(B_HEADS), np.arange(B_HEADS)] = -(DH ** 0.5)
    out["pick"] = pick
    rd = DH // 4
    half = rd // 2
    inv = np.float32(500000.0) ** (-np.arange(0, rd, 2, dtype=np.float32) / np.float32(rd))
    ang = tok.astype(np.float32)[None, :] * inv[:, None]
    cos, sin = np.ones((DH, SEQ), np.float32), np.zeros((DH, SEQ), np.float32)
    cos[:rd] = np.tile(np.cos(ang), (2, 1))
    sin[:rd] = np.tile(np.sin(ang), (2, 1))
    out["rope2"] = np.stack([np.tile(cos, (2, 1)), np.tile(sin, (2, 1))])
    rot = np.zeros((P, P))
    for base in (0, DH):
        for d in range(half):
            rot[base + half + d, base + d] = -1.0
            rot[base + d, base + half + d] = 1.0
    out["rot2"] = rot
    dh1, ax = 64, 32
    inv = np.float32(10000.0) ** (-np.arange(0, ax, 2, dtype=np.float32) / np.float32(ax))
    row = (np.arange(SEQ) // 64).astype(np.float32)
    colm = (np.arange(SEQ) % 64).astype(np.float32)
    ang = np.concatenate([inv[:, None] * row, inv[:, None] * colm], 0)
    ang = np.concatenate([ang, ang], 0)
    out["rope1"] = np.stack([np.tile(np.cos(ang), (2, 1)), np.tile(np.sin(ang), (2, 1))])
    rot = np.zeros((P, P))
    for base in (0, 64):
        for d in range(32):
            rot[base + 32 + d, base + d] = -1.0
            rot[base + d, base + 32 + d] = 1.0
    out["rot1"] = rot
    return {k: np.ascontiguousarray(v, dtype=np.float32) for k, v in out.items()}
Q0, K0, V0, Z0, XBC0, DT0, G0 = 0, 1024, 2048, 3072, 4096, 6144, 6176
LAM_INIT = 0.2
FT2 = 256
SSD_H, SSD_G, SSD_P = 16, 4, 64
TC = NC + NT


def block1_mixer(c):
    nc, t = c.nc, c.t
    w_in = t["w_in"][0]
    with ExitStack() as s1:
        hcT = c.sb(s1, "hcT", [P, KD, CTX])
        lam = c.sb(s1, "minus_lambda", [P, 1])
        modulation(c, s1, hcT, lam)
        yT = c.sb(s1, "yT", [P, KD, SEQ])
        with ExitStack() as s:
            xt = c.sb(s, "x_ssd", [P, TC, D])
            with ExitStack() as st:
                ssd(c, st, w_in, hcT, xt, yT)
            gate_y(c, w_in, xt, yT)
        oT = c.sb(s1, "oT", [P, KD, SEQ])
        diff_attention(c, w_in, hcT, lam, oT)
        merge(c, w_in, yT, oT)


def modulation(c, s1, hcT, lam):
    nc, t = c.nc, c.t
    b_ada = t["b_ada"]
    SHIFT1, SCALE1, SHIFT2, SCALE2 = range(4)
    with ExitStack() as s:
        cc = c.sb(s, "conditions", [P, KD, 2])
        cb = c.sb(s, "condition_wide", [P, KD, P])
        brow = c.sb(s, "bias_rows", [2, 4, D])
        mrow = c.sb(s, "mod_rows", [2, 4, D])
        mcol = c.sb(s, "mod_columns", [P, 4, KD, 2])
        gcol = c.sb(s, "gain_columns", [P, 2, KD])
        prow = c.sb(s, "post_rows", [P, 2, D])
        lv = c.sb(s, "lambda_rows", [P, 4, 64])
        lp = c.sb(s, "lambda_products", [P, 2, 64])
        le = c.sb(s, "lambda_sums", [P, 2])
        ctx_tok = c.sb(s, "context", [P, NC, D])
        landed = c.sem("ada_landed")
        silud = c.sem("ada_silu")
        wide = c.sem("ada_wide")
        done = c.sem("ada_done")
        left = c.sem("ada_left")
        turned = c.sem("ada_turned")
        lamd = c.sem("lambda_steps")
        LOADS = 2 + 2 + 4 + 2 + 2 + 4 + 1
        with ExitStack() as b:
            block = b.enter_context(nc.Block())

            @block.sync
            def _(sp):
                def load(dst, src, slow=False):
                    sp.dma_start(dst, src, allow_slow_non_contiguous=slow).then_inc(landed, 16)
                load(cc[:, :, 0], t["c"][0].rearrange("(k p) -> p k", p=P), True)
                load(cc[:, :, 1], t["c_ctx"].rearrange("(k p) -> p k", p=P), True)
                for i, kind in enumerate((2, 5)):
                    load(c.gate[:, i], b_ada[:, kind * D:(kind + 1) * D].to_broadcast([P, D]))
                for i, kind in enumerate((0, 1, 3, 4)):
                    load(brow[:, i], b_ada[:, kind * D:(kind + 1) * D].to_broadcast([2, D]))
                load(gcol[:, 0], t["g_pre_mix"][0].rearrange("(k p) -> p k", p=P), True)
                load(gcol[:, 1], t["g_pre_ffn"][0].rearrange("(k p) -> p k", p=P), True)
                load(prow[:, 0], t["g_post_mix"].to_broadcast([P, D]))
                load(prow[:, 1], t["g_post_ffn"].to_broadcast([P, D]))
                for i, name in enumerate(("lam_q1", "lam_k1", "lam_q2", "lam_k2")):
                    load(lv[:, i], t[name].to_broadcast([P, 64]))
                load(ctx_tok[:], t["ctx"][0].rearrange("(t p) d -> p t d", p=P))
                load_weights(c, sp, [whole(cols(t["w_ada"][0], n * GW)) for n in range(12)])
                sp.wait_ge(landed, 16 * LOADS)

            @block.scalar
            def _(act):
                act.wait_ge(landed, 16 * LOADS)
                nc.scalar.activation(cc[:], cc[:], ACT.Silu).then_inc(silud, 1)
                act.wait_ge(lamd, 2)
                nc.scalar.activation(le[:], le[:], ACT.Exp).then_inc(lamd, 1)

            @block.tensor
            def _(pe):
                pe.wait_ge(wide, 1)
                pe.wait_ge(silud, 1)
                for n in range(12):
                    w = take(c, pe, 1).rearrange("p (k n) -> p k n", n=GW)
                    gate = n // 2 in (2, 5)
                    if n >= 4:
                        pe.wait_ge(left, n - 3)
                    for k in range(KD):
                        out = c.ps[:, n % 4] if gate else c.ps[0:2, n % 4]
                        last = mm(c, out, cb[:, k] if gate else cc[:, k], w[:, k], k == 0, k == KD - 1)
                    last.then_inc(done, 1)
                pe.wait_ge(left, 12)
                for i in range(4):
                    for k in range(KD):
                        j = i * KD + k
                        last = nc.tensor.transpose(c.ps[:, 4, 2 * j:2 * j + 2], mrow[:, i, k * P:(k + 1) * P], c.ident[0:2, 0:2])
                last.then_inc(turned, 1)

            @block.vector
            def _(dve):
                dve.wait_ge(silud, 1)
                nc.vector.tensor_copy(cb[:], cc[:, :, 0:1].to_broadcast([P, KD, P])).then_inc(wide, 1)
                c.vlink(dve, nc.vector.tensor_tensor(lp[:, 0], lv[:, 0], lv[:, 1], ALU.mult))
                c.vlink(dve, nc.vector.tensor_tensor(lp[:, 1], lv[:, 2], lv[:, 3], ALU.mult))
                nc.vector.reduce_sum(le[:, 0:1], lp[:, 0], AX).then_inc(lamd, 1)
                nc.vector.reduce_sum(le[:, 1:2], lp[:, 1], AX).then_inc(lamd, 1)
                dve.wait_ge(lamd, 3)
                c.vlink(dve, nc.vector.tensor_tensor(lam[:], le[:, 1:2], le[:, 0:1], ALU.subtract))
                c.vlink(dve, nc.vector.tensor_scalar(lam[:], lam[:], -LAM_INIT, None, ALU.add))
                kinds = (0, 1, None, 2, 3, None)
                for n in range(12):
                    i, hf = kinds[n // 2], slice((n % 2) * GW, (n % 2 + 1) * GW)
                    dve.wait_ge(done, n + 1)
                    if i is None:
                        g = c.gate[:, n // 6, hf]
                        c.vlink(dve, nc.vector.tensor_tensor(g, c.ps[:, n % 4], g, ALU.add))
                        nc.vector.tensor_tensor(g, g, prow[:, n // 6, hf], ALU.mult).then_inc(left, 1)
                    else:
                        nc.vector.tensor_tensor(mrow[:, i, hf], c.ps[0:2, n % 4], brow[:, i, hf], ALU.add).then_inc(left, 1)
                dve.wait_ge(turned, 1)
                c.vlink(dve, nc.vector.tensor_copy(mcol[:], c.ps[:, 4, 0:8 * KD]))
                for n, (kind, who, g) in enumerate(((SCALE1, 0, 0), (SCALE1, 1, 0), (SCALE2, 0, 1))):
                    nc.vector.scalar_tensor_tensor(mcol[:, kind, :, who], mcol[:, kind, :, who], 1.0, gcol[:, g], ALU.add, ALU.mult)
                c.vlink(dve, nc.vector.tensor_copy(c.shift2[:], mcol[:, SHIFT2, :, 0]))
                c.vlink(dve, nc.vector.tensor_copy(c.scale2[:], mcol[:, SCALE2, :, 0]))
        norm_transpose(c, c.x, NT, [(lambda k, tile: c.hT[:, k, tile * P:(tile + 1) * P],
                                     lambda k: mcol[:, SCALE1, k, 0:1], lambda k: mcol[:, SHIFT1, k, 0:1])])
        norm_transpose(c, ctx_tok, NC, [(lambda k, tile: hcT[:, k, tile * P:(tile + 1) * P],
                                         lambda k: mcol[:, SCALE1, k, 1:2], lambda k: mcol[:, SHIFT1, k, 1:2])])


def ssd(c, s0, w_in, hcT, xt, yT):
    nc, t = c.nc, c.t
    HG = SSD_H // SSD_G
    GP = HG * SSD_P
    bT = c.sb(s0, "B_T", [P, SSD_G, CTX + SEQ])
    cT = c.sb(s0, "C_T", [P, SSD_G, SEQ])
    dt = c.sb(s0, "dt", [P, TC, 2 * SSD_H])
    da = c.sb(s0, "dt_a", [P, TC, 2 * SSD_H])
    tri = c.sb(s0, "triangles", [P, 5, P])
    LE, GT, GE, LT, ONES = range(5)
    ex = c.sb(s0, "decays", [P, TC, 6 * SSD_H])
    drow = c.sb(s0, "d_skip", [P, SSD_H])
    hs = [yT[:].rearrange("p k n -> p (k n)").rearrange("p (t d) -> p t d", d=D),
          c.sb(s0, "states_backward", [P, NT, D])]
    with ExitStack() as s:
        btok = c.sb(s, "B_tokens", [P, TC, SSD_G * P])
        with ExitStack() as b:
            taps = c.sb(b, "taps", [P, 3, 16])
            bias = c.sb(b, "conv_bias", [P, 16])
            arow = c.sb(b, "a_row", [P, 2 * SSD_H])
            dbias = c.sb(b, "dt_bias", [P, 2 * SSD_H])
            landed = c.sem("ssd_landed")
            with ExitStack() as bb:
                block = bb.enter_context(nc.Block())

                @block.sync
                def _(sp):
                    for j in range(3):
                        sp.dma_start(taps[:, j], t["conv_w"][0, j].rearrange("(k p) -> p k", p=P), allow_slow_non_contiguous=True).then_inc(landed, 16)
                    sp.dma_start(bias[:], t["conv_b"][0].rearrange("(k p) -> p k", p=P), allow_slow_non_contiguous=True).then_inc(landed, 16)
                    sp.dma_start(arow[:], t["a_log"].rearrange("a d h -> a (d h)").to_broadcast([P, 2 * SSD_H])).then_inc(landed, 16)
                    sp.dma_start(dbias[:], t["dt_bias"].rearrange("a d h -> a (d h)").to_broadcast([P, 2 * SSD_H])).then_inc(landed, 16)
                    sp.dma_start(tri[:], t["tri"].rearrange("a p n -> p a n")).then_inc(landed, 16)
                    sp.dma_start(drow[:], t["d_skip"].to_broadcast([P, SSD_H])).then_inc(landed, 16)
                    sp.wait_ge(landed, 128)
            conv_project(c, w_in, hcT, xt, bT, cT, btok, taps, bias)
            with ExitStack() as bb:
                z = c.sb(bb, "z", [P, TC, 2 * SSD_H])
                done = c.sem("dt_done")
                step = c.sem("dt_steps")
                summed = c.sem("dt_summed")
                block = bb.enter_context(nc.Block())

                @block.sync
                def _(sp):
                    load_weights(c, sp, [whole(cols(w_in, DT0, 2 * SSD_H))])

                @block.tensor
                def _(pe):
                    w = take(c, pe, 1)
                    for tile in range(TC):
                        for k in range(KD):
                            lhs = hcT[:, k, tile * P:(tile + 1) * P] if tile < NC else c.hT[:, k, (tile - NC) * P:(tile - NC + 1) * P]
                            last = mm(c, c.ps[:, 0, tile * 32:(tile + 1) * 32], lhs, w[:, k * 32:(k + 1) * 32], k == 0, k == KD - 1)
                    last.then_inc(done, 1)
                    pe.wait_ge(step, 5)
                    for tile in range(TC):
                        bank, at = 1 + tile // 3, (tile % 3) * 6 * SSD_H
                        for n, (m, c0, w) in enumerate(((LE, 0, 16), (GT, 0, 16), (GE, 16, 16), (LT, 16, 16), (ONES, 0, 32))):
                            last = nc.tensor.matmul(c.ps[:, bank, at + 16 * n:at + 16 * n + w], tri[:, m], da[:, tile, c0:c0 + w],
                                                    start=True, stop=True)
                    last.then_inc(summed, 1)

                @block.scalar
                def _(act):
                    nc.scalar.activation(arow[:], arow[:], ACT.Exp).then_inc(step, 1)
                    act.wait_ge(step, 2)
                    nc.scalar.activation(dt[:], dt[:], ACT.Exp, scale=-1.0).then_inc(step, 1)
                    act.wait_ge(step, 3)
                    nc.scalar.activation(dt[:], dt[:], ACT.Ln, bias=1.0).then_inc(step, 1)
                    act.wait_ge(summed, 1)
                    for n in range(2):
                        nc.scalar.activation(ex[:, 3 * n:3 * n + 3], c.ps[:, 1 + n, 0:18 * SSD_H], ACT.Exp)

                @block.vector
                def _(dve):
                    dve.wait_ge(done, 1)
                    dve.wait_ge(step, 1)
                    c.vlink(dve, nc.vector.tensor_tensor(z[:], c.ps[:, 0, 0:TC * 32].rearrange("p (t h) -> p t h", h=32),
                                                         dbias[:].unsqueeze(1).to_broadcast([P, TC, 32]), ALU.add))
                    nc.vector.scalar_tensor_tensor(dt[:], z[:], -1.0, z[:], ALU.mult, ALU.max).then_inc(step, 1)
                    dve.wait_ge(step, 4)
                    c.vlink(dve, nc.vector.scalar_tensor_tensor(dt[:], z[:], 0.0, dt[:], ALU.max, ALU.add))
                    c.vlink(dve, nc.vector.tensor_scalar(arow[:], arow[:], -1.0, None, ALU.mult))
                    nc.vector.tensor_tensor(da[:], dt[:], arow[:].unsqueeze(1).to_broadcast([P, TC, 32]), ALU.mult).then_inc(step, 1)

        with ExitStack() as b:
            wt = c.sb(b, "end_weights", [P, TC, 2 * SSD_H])
            xw = c.sb(b, "x_weighted", [P, 2, D])
            weighted = c.sem("st_weighted")
            outer = c.sem("st_outer")
            kept = c.sem("st_kept")
            block = b.enter_context(nc.Block())
            plan = []
            for n in range(5):
                plan.append((0, n, max(n - 1, 0), max(n - 2, 0) if n else None))
                plan.append((1, (1, 0, 5, 4, 3)[n], (3, 3, 2, 1, 0)[n], (None, 3, 3, 2, 1)[n]))

            @block.tensor
            def _(pe):
                for i, (d, ch, _, _) in enumerate(plan):
                    pe.wait_ge(weighted, i + 1)
                    if i >= 2:
                        pe.wait_ge(kept, i - 1)
                    for g in range(SSD_G):
                        last = nc.tensor.matmul(c.ps[:, 2 * (i % 2) + g // 2, (g % 2) * GP:(g % 2 + 1) * GP],
                                                btok[:, ch, g * P:(g + 1) * P], xw[:, i % 2, g * GP:(g + 1) * GP], start=True, stop=True)
                    last.then_inc(outer, 1)

            @block.vector
            def _(dve):
                L = lambda ins: c.vlink(dve, ins)
                nc.vector.tensor_tensor(wt[:, :, 0:16], dt[:, :, 0:16], ex[:, :, 16:32], ALU.mult)
                L(nc.vector.tensor_tensor(wt[:, :, 16:32], dt[:, :, 16:32], ex[:, :, 48:64], ALU.mult))

                def weigh(i):
                    d, ch, _, _ = plan[i]
                    if i >= 2:
                        dve.wait_ge(outer, i - 1)
                    nc.vector.tensor_tensor(xw[:, i % 2].rearrange("p (h q) -> p h q", q=SSD_P), xt[:, ch].rearrange("p (h q) -> p h q", q=SSD_P),
                                            wt[:, ch, 16 * d:16 * d + 16].unsqueeze(2).to_broadcast([P, SSD_H, SSD_P]), ALU.mult).then_inc(weighted, 1)
                weigh(0)
                for i, (d, ch, to, frm) in enumerate(plan):
                    if i + 1 < len(plan):
                        weigh(i + 1)
                    if i >= 2:
                        dve.wait_ge(kept, i - 1)
                    new = hs[d][:, to]
                    psum = c.ps[:, 2 * (i % 2):2 * (i % 2) + 2].rearrange("p b n -> p (b n)")
                    if frm is None:
                        dve.wait_ge(outer, i + 1)
                        nc.vector.tensor_copy(new, psum).then_inc(kept, 1)
                    else:
                        L(nc.vector.tensor_tensor(new.rearrange("p (h q) -> p h q", q=SSD_P), hs[d][:, frm].rearrange("p (h q) -> p h q", q=SSD_P),
                                                  ex[:, ch, 64 + 16 * d:80 + 16 * d].unsqueeze(2).to_broadcast([P, SSD_H, SSD_P]), ALU.mult))
                        dve.wait_ge(outer, i + 1)
                        nc.vector.tensor_tensor(new, new, psum, ALU.add).then_inc(kept, 1)

    with ExitStack() as s:
        dtail = c.sb(s, "dt_a_masked", [P, 2, 2, HG, P])
        xd = c.sb(s, "x_dt", [P, 2, 2, GP])
        mt = c.sb(s, "mixing", [P, 2, 2, HG, P])
        cb = c.sb(s, "masked_CB", [P, 2, P])
        off = c.sb(s, "from_states", [P, 2 * GP])
        skip = c.sb(s, "skip", [P, GP])
        spread = c.sem("so_spread")
        done = c.sem("so_products")
        expd = c.sem("so_exp")
        mixed = c.sem("so_mixed")
        diag = c.sem("so_diagonal")
        ready = c.sem("so_ready")
        block = s.enter_context(nc.Block())
        units = [(tile, g) for tile in range(NT) for g in range(SSD_G)]
        U = len(units)
        heads4 = lambda a: a.rearrange("p (h q) -> p h q", q=SSD_P)

        @block.gpsimd
        def _(pool):
            for i, (tile, g) in enumerate(units):
                ch = tile + NC
                if i >= 2:
                    pool.wait_ge(done, i - 1)
                    pool.wait_ge(diag, i - 1)
                for d, m in ((0, LE), (1, GE)):
                    nc.gpsimd.tensor_tensor(dtail[:, i % 2, d], tri[:, m:m + 1].to_broadcast([P, HG, P]),
                                            da[:, ch, 16 * d + HG * g:16 * d + HG * (g + 1)].unsqueeze(2).to_broadcast([P, HG, P]), ALU.mult)
                for d in range(2):
                    last = nc.gpsimd.tensor_tensor(heads4(xd[:, i % 2, d]), heads4(xt[:, ch, g * GP:(g + 1) * GP]),
                                                   dt[:, ch, 16 * d + HG * g:16 * d + HG * (g + 1)].unsqueeze(2).to_broadcast([P, HG, SSD_P]), ALU.mult)
                last.then_inc(spread, 1)

        @block.tensor
        def _(pe):
            for i in range(U + 1):
                if i < U:
                    tile, g = units[i]
                    b = 4 * (i % 2)
                    pe.wait_ge(spread, i + 1)
                    if i >= 2:
                        pe.wait_ge(ready, i - 1)
                    tok = slice(tile * P, (tile + 1) * P)
                    nc.tensor.matmul(c.ps[:, b, 0:P], bT[:, g, CTX + tile * P:CTX + (tile + 1) * P], cT[:, g, tok], start=True, stop=True)
                    nc.tensor.matmul(c.ps[:, b + 1], tri[:, GT], dtail[:, i % 2, 0], start=True, stop=True)
                    nc.tensor.matmul(c.ps[:, b + 2], tri[:, LT], dtail[:, i % 2, 1], start=True, stop=True)
                    for d in range(2):
                        last = nc.tensor.matmul(c.ps[:, b + 3, d * GP:(d + 1) * GP], cT[:, g, tok], hs[d][:, tile, g * GP:(g + 1) * GP],
                                                start=True, stop=True)
                    last.then_inc(done, 1)
                if i:
                    j = i - 1
                    b = 4 * (j % 2)
                    pe.wait_ge(mixed, j + 1)
                    for h in range(HG):
                        for d in range(2):
                            last = nc.tensor.matmul(c.ps[:, b, GP + h * SSD_P:GP + (h + 1) * SSD_P], mt[:, j % 2, d, h],
                                                    xd[:, j % 2, d, h * SSD_P:(h + 1) * SSD_P], start=d == 0, stop=d == 1)
                    last.then_inc(diag, 1)

        @block.scalar
        def _(act):
            for i in range(U):
                b = 4 * (i % 2)
                act.wait_ge(done, i + 1)
                if i >= 2:
                    act.wait_ge(diag, i - 1)
                nc.scalar.activation(mt[:, i % 2].rearrange("p d h n -> p (d h n)"), c.ps[:, b + 1:b + 3].rearrange("p b n -> p (b n)"), ACT.Exp).then_inc(expd, 1)

        @block.vector
        def _(dve):
            L = lambda ins: c.vlink(dve, ins)
            for i in range(U + 1):
                if i < U:
                    b = 4 * (i % 2)
                    dve.wait_ge(done, i + 1)
                    if i:
                        dve.wait_ge(mixed, i)
                    nc.vector.tensor_tensor(cb[:, 0], c.ps[:, b, 0:P], tri[:, LE], ALU.mult)
                    L(nc.vector.tensor_tensor(cb[:, 1], c.ps[:, b, 0:P], tri[:, GE], ALU.mult))
                    dve.wait_ge(expd, i + 1)
                    for d in range(2):
                        last = nc.vector.tensor_tensor(mt[:, i % 2, d], mt[:, i % 2, d],
                                                       cb[:, d:d + 1].to_broadcast([P, HG, P]), ALU.mult)
                    last.then_inc(mixed, 1)
                if i:
                    j = i - 1
                    tile, g = units[j]
                    ch = tile + NC
                    b = 4 * (j % 2)
                    x_g = xt[:, ch, g * GP:(g + 1) * GP]
                    if j:
                        dve.wait_ge(ready, j)
                    for d in range(2):
                        nc.vector.tensor_tensor(heads4(off[:, d * GP:(d + 1) * GP]), heads4(c.ps[:, b + 3, d * GP:(d + 1) * GP]),
                                                ex[:, ch, 32 * d + HG * g:32 * d + HG * (g + 1)].unsqueeze(2).to_broadcast([P, HG, SSD_P]), ALU.mult)
                    L(nc.vector.tensor_tensor(heads4(skip[:]), heads4(x_g), drow[:, HG * g:HG * (g + 1)].unsqueeze(2).to_broadcast([P, HG, SSD_P]), ALU.mult))
                    L(nc.vector.tensor_tensor(off[:, 0:GP], off[:, 0:GP], off[:, GP:], ALU.add))
                    L(nc.vector.tensor_tensor(skip[:], skip[:], off[:, 0:GP], ALU.add))
                    dve.wait_ge(diag, j + 1)
                    nc.vector.tensor_tensor(x_g, skip[:], c.ps[:, b, GP:2 * GP], ALU.add).then_inc(ready, 1)


def conv_project(c, w_in, hcT, xt, bT, cT, btok, taps, bias):
    nc = c.nc
    N = 16
    ALL = CTX + SEQ
    parts = lambda i: ((0, CTX), (CTX, ALL)) if i < 12 else ((CTX, ALL),)
    with ExitStack() as s:
        ua = c.sb(s, "convolved", [P, 2, ALL])
        xf = c.sb(s, "x_features", [P, 2, ALL])
        done = c.sem("cp_done")
        begun = c.sem("cp_begun")
        back = c.sem("cp_back")
        convd = c.sem("cp_convd")
        silud = c.sem("cp_silu")
        turned = c.sem("cp_turned")
        taken_v = c.sem("cp_taken_v")
        taken_a = c.sem("cp_taken_a")
        block = s.enter_context(nc.Block())

        def bank(i, a):
            return c.ps[:, 2 + i % 2, 0:CTX] if a == 0 else c.ps[:, i % 2]

        def feature(i):
            return xf[:, i % 2] if i < 8 else bT[:, i - 8] if i < 12 else cT[:, i - 12]

        @block.sync
        def _(sp):
            load_weights(c, sp, [whole(cols(w_in, XBC0 + n * GW)) for n in range(4)])

        @block.tensor
        def _(pe):
            for i in range(N + 1):
                if i < N:
                    if i % 4 == 0:
                        w = take(c, pe, 1).rearrange("p (k n) -> p k n", n=GW)
                    if i >= 2:
                        pe.wait_ge(convd, i - 1)
                    for a, z in parts(i):
                        for k in range(KD):
                            last = mm(c, bank(i, a), w[:, k, (i % 4) * P:(i % 4 + 1) * P], hcT[:, k] if a == 0 else c.hT[:, k], k == 0, k == KD - 1)
                    last.then_inc(done, 1)
                if i and i - 1 < 12:
                    j = i - 1
                    pe.wait_ge(silud, j + 1)
                    if j >= 2:
                        pe.wait_ge(taken_v, j - 1)
                        pe.wait_ge(taken_a, j - 1)
                    for tile in range(TC):
                        last = nc.tensor.transpose(c.ps[:, 4 + 2 * (j % 2) + tile // 4, (tile % 4) * P:(tile % 4 + 1) * P],
                                                   feature(j)[:, tile * P:(tile + 1) * P], c.ident[:])
                    last.then_inc(turned, 1)

        def tokens(j, a, z):
            return xt[:, a:z, j * P:(j + 1) * P] if j < 8 else btok[:, a:z, (j - 8) * P:(j - 7) * P]

        @block.scalar
        def _(act):
            for i in range(N + 2):
                if i < N:
                    act.wait_ge(done, i + 1)
                    if i >= 2:
                        act.wait_ge(silud, i - 1)
                    for a, z in parts(i):
                        last = nc.scalar.activation(ua[:, i % 2, a:z], bank(i, a), ACT.Identity, scale=taps[:, 1, i:i + 1], bias=bias[:, i:i + 1])
                    last.then_inc(begun, 1)
                    act.wait_ge(convd, i + 1)
                    if 2 <= i < 8:
                        act.wait_ge(turned, i - 1)
                    a = 0 if i < 12 else CTX
                    nc.scalar.activation(feature(i), ua[:, i % 2, a:], ACT.Silu).then_inc(silud, 1)
                if i and i - 1 < 12:
                    j = i - 1
                    act.wait_ge(turned, j + 1)
                    nc.scalar.activation(tokens(j, 4, 6), c.ps[:, 5 + 2 * (j % 2), 0:2 * P].rearrange("p (t n) -> p t n", n=P), ACT.Copy).then_inc(taken_a, 1)

        @block.vector
        def _(dve):
            for i in range(N + 1):
                if i < N:
                    dve.wait_ge(begun, i + 1)
                    for a, z in parts(i):
                        src = bank(i, a)
                        last = nc.vector.scalar_tensor_tensor(ua[:, i % 2, a + 1:z], src[:, 0:z - a - 1], taps[:, 0, i:i + 1], ua[:, i % 2, a + 1:z], ALU.mult, ALU.add)
                    last.then_inc(back, 1)
                    dve.wait_ge(back, i + 1)
                    for a, z in parts(i):
                        src = bank(i, a)
                        last = nc.vector.scalar_tensor_tensor(ua[:, i % 2, a:z - 1], src[:, 1:z - a], taps[:, 2, i:i + 1], ua[:, i % 2, a:z - 1], ALU.mult, ALU.add)
                    last.then_inc(convd, 1)
                if i and i - 1 < 12:
                    j = i - 1
                    dve.wait_ge(turned, j + 1)
                    nc.vector.tensor_copy(tokens(j, 0, 4), c.ps[:, 4 + 2 * (j % 2)].rearrange("p (t n) -> p t n", n=P)).then_inc(taken_v, 1)


def gate_y(c, w_in, xt, yT):
    nc, t = c.nc, c.t
    GP = D // SSD_G
    with ExitStack() as s:
        gcol = c.sb(s, "ssd_gain", [P, KD])
        with ExitStack() as b:
            sz = c.sb(b, "silu_z", [P, 2, GW])
            sq = c.sb(b, "squares", [P, GP])
            ss = c.sb(b, "sum_squares", [P, NT, SSD_G])
            landed = c.sem("gy_landed")
            done = c.sem("gy_done")
            silud = c.sem("gy_silu")
            gated = c.sem("gy_gated")
            summed = c.sem("gy_summed")
            meaned = c.sem("gy_meaned")
            block = b.enter_context(nc.Block())

            @block.sync
            def _(sp):
                sp.dma_start(gcol[:], t["g_ssd_norm"][0].rearrange("(k p) -> p k", p=P), allow_slow_non_contiguous=True).then_inc(landed, 16)
                load_weights(c, sp, [whole(cols(w_in, Z0 + n * GW)) for n in range(2)])
                sp.wait_ge(landed, 16)

            @block.tensor
            def _(pe):
                for i in range(2 * NT):
                    if i % NT == 0:
                        w = take(c, pe, 1).rearrange("p (k n) -> p k n", n=GW)
                    if i >= 4:
                        pe.wait_ge(silud, i - 3)
                    tile = i % NT
                    for k in range(KD):
                        last = mm(c, c.ps[:, i % 4], c.hT[:, k, tile * P:(tile + 1) * P], w[:, k], k == 0, k == KD - 1)
                    last.then_inc(done, 1)

            @block.scalar
            def _(act):
                for i in range(2 * NT + 1):
                    if i < 2 * NT:
                        act.wait_ge(done, i + 1)
                        if i >= 2:
                            act.wait_ge(gated, i - 1)
                        nc.scalar.activation(sz[:, i % 2], c.ps[:, i % 4], ACT.Silu).then_inc(silud, 1)
                    if i:
                        hf, tile = divmod(i - 1, NT)
                        act.wait_ge(gated, i)
                        for g in range(2):
                            n = 2 * (i - 1) + g
                            if n:
                                act.wait_ge(summed, n)
                            a = hf * GW + g * GP
                            nc.scalar.activation(sq[:], xt[:, NC + tile, a:a + GP], ACT.Square,
                                                 accum_out=ss[:, tile, 2 * hf + g:2 * hf + g + 1]).then_inc(summed, 1)

            @block.gpsimd
            def _(pool):
                pool.wait_ge(meaned, 1)
                nc.gpsimd.tensor_tensor(ss[:], ss[:], c.half[:, 0:4].unsqueeze(1).to_broadcast([P, NT, SSD_G]), ALU.pow).then_inc(meaned, 1)

            @block.vector
            def _(dve):
                for i in range(2 * NT):
                    hf, tile = divmod(i, NT)
                    dve.wait_ge(silud, i + 1)
                    y = xt[:, NC + tile, hf * GW:(hf + 1) * GW]
                    nc.vector.tensor_tensor(y, y, sz[:, i % 2], ALU.mult).then_inc(gated, 1)
                dve.wait_ge(summed, 4 * NT)
                nc.vector.tensor_scalar(ss[:], ss[:], 1.0 / GP, EPS, ALU.mult, ALU.add).then_inc(meaned, 1)
                dve.wait_ge(meaned, 2)
                dve.wait_ge(gated, 2 * NT)
                for tile in range(NT):
                    y = xt[:, NC + tile].rearrange("p (g q) -> p g q", q=GP)
                    nc.vector.tensor_tensor(y, y, ss[:, tile].unsqueeze(2).to_broadcast([P, SSD_G, GP]), ALU.mult)
        plain_transpose(c, lambda tile: xt[:, NC + tile], NT, KD, lambda k, tile: yT[:, k, tile * P:(tile + 1) * P], lambda k: gcol[:, k:k + 1])


def diff_attention(c, w_in, hcT, lam, oT):
    nc, t = c.nc, c.t
    ALL = CTX + SEQ
    with ExitStack() as s:
        o = c.sb(s, "heads_out", [P, NT, D])
        ss = c.sb(s, "sum_squares", [P, NT, 8])
        gcol = c.sb(s, "subln_gain", [P, 1])
        with ExitStack() as sa:
            rope = c.sb(sa, "rope", [P, 2, SEQ])
            rot = c.sb(sa, "rotation", [P, P])
            landed = c.sem("rope_landed")
            with ExitStack() as b:
                block = b.enter_context(nc.Block())

                @block.sync
                def _(sp):
                    sp.dma_start(rope[:], t["rope1"].rearrange("a p n -> p a n")).then_inc(landed, 16)
                    sp.dma_start(rot[:], t["rot1"]).then_inc(landed, 16)
                    sp.dma_start(gcol[:], t["g_attn_subln"].rearrange("a p -> p a"), allow_slow_non_contiguous=True).then_inc(landed, 16)
                    sp.wait_ge(landed, 48)

                @block.vector
                def _(dve):
                    dve.wait_ge(landed, 48)
                    nc.vector.tensor_scalar(gcol[:], gcol[:], 1.0 - LAM_INIT, None, ALU.mult)
            for hh in range(2):
                with ExitStack() as sh:
                    qT = c.sb(sh, "qT", [P, 4, SEQ])
                    kT = c.sb(sh, "kT", [P, 4, ALL])
                    v = c.sb(sh, "v", [P, TC, GW])
                    fl = lambda f: (lambda w, k: w[:, k * GW + f * P:k * GW + (f + 1) * P])
                    lat = lambda w, k: c.hT[:, k]
                    con = lambda w, k: hcT[:, k]
                    turns = (rope[:, 0], rope[:, 1], rot[:])
                    jobs = [([(0, KD, GW, cols(w_in, Q0 + hh * GW))],
                             [dict(m=P, n=SEQ, out=qT[:, f], rope=turns, lhs=fl(f), rhs=lat) for f in range(4)]),
                            ([(0, KD, GW, cols(w_in, K0 + hh * GW))],
                             [dict(m=P, n=SEQ, out=kT[:, f, CTX:], rope=turns, lhs=fl(f), rhs=lat) for f in range(4)] +
                             [dict(m=P, n=CTX, out=kT[:, f, 0:CTX], rope=None, lhs=fl(f), rhs=con) for f in range(4)]),
                            ([(0, KD, GW, cols(w_in, V0 + hh * GW))],
                             [dict(m=P, n=GW, out=v[:, tile], rope=None,
                                   lhs=(lambda w, k, tile=tile: hcT[:, k, tile * P:(tile + 1) * P]) if tile < NC else
                                       (lambda w, k, tile=tile: c.hT[:, k, (tile - NC) * P:(tile - NC + 1) * P]),
                                   rhs=lambda w, k: w[:, k * GW:(k + 1) * GW]) for tile in range(TC)])]
                    project_heads(c, jobs)
                    diff_units(c, hh, qT, kT, v, o, ss, lam)
        with ExitStack() as b:
            step = c.sem("sub_steps")
            block = b.enter_context(nc.Block())

            @block.gpsimd
            def _(pool):
                pool.wait_ge(step, 1)
                nc.gpsimd.tensor_tensor(ss[:], ss[:], c.half[:].unsqueeze(1).to_broadcast([P, NT, 8]), ALU.pow).then_inc(step, 1)

            @block.vector
            def _(dve):
                nc.vector.tensor_scalar(ss[:], ss[:], 1.0 / P, EPS, ALU.mult, ALU.add).then_inc(step, 1)
                dve.wait_ge(step, 2)
                for tile in range(NT):
                    ot = o[:, tile].rearrange("p (h q) -> p h q", q=P)
                    nc.vector.tensor_tensor(ot, ot, ss[:, tile].unsqueeze(2).to_broadcast([P, 8, P]), ALU.mult)
        plain_transpose(c, lambda tile: o[:, tile], NT, KD, lambda k, tile: oT[:, k, tile * P:(tile + 1) * P], lambda k: gcol[:])


def diff_units(c, hh, qT, kT, v, o, ss, lam):
    nc = c.nc
    ALL = CTX + SEQ
    SC = 64 ** -0.5
    units = [(tile, h) for tile in range(NT) for h in range(4)]
    U = len(units)
    with ExitStack() as s:
        pr = c.sb(s, "probs", [P, 3, 2, ALL])
        prT = c.sb(s, "probsT", [P, 2, TC, P])
        mx = c.sb(s, "maxima", [P, 2, 2])
        ls = c.sb(s, "sums", [P, 3, 2])
        sq = c.sb(s, "squares", [P, P])
        scored = c.sem("du_scored")
        first = c.sem("du_first_component")
        biased = c.sem("du_biased")
        expd = c.sem("du_exp")
        mixed = c.sem("du_mixed")
        turned = c.sem("du_turned")
        copied_a = c.sem("du_copied_a")
        copied_v = c.sem("du_copied_v")
        summed = c.sem("du_summed")
        left = c.sem("du_left")
        squared = c.sem("du_squared")
        block = s.enter_context(nc.Block())

        def scores(i):
            return c.ps[:, 3 * (i % 2):3 * (i % 2) + 3].rearrange("p b n -> p (b n)")

        @block.tensor
        def _(pe):
            for i in range(U + 3):
                def score(m, a, z):
                    tile, h = units[i]
                    r = slice(64 * m, 64 * m + 64)
                    return nc.tensor.matmul(scores(i)[:, m * ALL + a:m * ALL + z], qT[r, h, tile * P:(tile + 1) * P], kT[r, h, a:z], start=True, stop=True)
                if i < U:
                    if i >= 2:
                        pe.wait_ge(expd, 2 * (i - 1))
                    score(0, 512, ALL).then_inc(first, 1)
                    score(0, 0, 512)
                if 0 <= i - 3 < U:
                    j = i - 3
                    tile, h = units[j]
                    pe.wait_ge(copied_a, j + 1)
                    pe.wait_ge(copied_v, j + 1)
                    for b in range(TC):
                        last = nc.tensor.matmul(c.ps[:, 7, 2 * P:3 * P], prT[:, j % 2, b], v[:, b, h * P:(h + 1) * P], start=b == 0, stop=b == TC - 1)
                    last.then_inc(summed, 1)
                if i < U:
                    pe.wait_ge(first, i + 1)
                    score(1, 0, 256)
                    score(1, 256, ALL).then_inc(scored, 1)
                if 0 <= i - 2 < U:
                    j = i - 2
                    pe.wait_ge(mixed, j + 1)
                    if j:
                        pe.wait_ge(left, j)
                        pe.wait_ge(copied_a, j)
                    for b in range(TC):
                        last = nc.tensor.transpose(c.ps[:, 6 + b // 4, (b % 4) * P:(b % 4 + 1) * P], pr[:, j % 3, 0, b * P:(b + 1) * P], c.ident[:])
                    last.then_inc(turned, 1)

        @block.scalar
        def _(act):
            for i in range(U + 3):
                if i < U:
                    act.wait_ge(biased, i + 1)
                    if i >= 3:
                        act.wait_ge(turned, i - 2)
                    for m in range(2):
                        nc.scalar.activation(pr[:, i % 3, m], scores(i)[:, m * ALL:(m + 1) * ALL], ACT.Exp, bias=mx[:, i % 2, m:m + 1], scale=SC,
                                             accum_out=ls[:, i % 3, m:m + 1]).then_inc(expd, 1)
                if 0 <= i - 2 < U:
                    j = i - 2
                    act.wait_ge(turned, j + 1)
                    if j >= 2:
                        act.wait_ge(summed, j - 1)
                    nc.scalar.activation(prT[:, j % 2, 0:4], c.ps[:, 6].rearrange("p (b n) -> p b n", n=P), ACT.Copy).then_inc(copied_a, 1)
                if 0 <= i - 3 < U:
                    j = i - 3
                    tile, h = units[j]
                    n = hh * 4 + h
                    act.wait_ge(left, j + 1)
                    if j:
                        act.wait_ge(squared, j)
                    nc.scalar.activation(sq[:], o[:, tile, n * P:(n + 1) * P], ACT.Square, accum_out=ss[:, tile, n:n + 1]).then_inc(squared, 1)

        @block.vector
        def _(dve):
            L = lambda ins: c.vlink(dve, ins)
            for i in range(U + 3):
                if i < U:
                    dve.wait_ge(scored, i + 1)
                    if i >= 2:
                        dve.wait_ge(expd, 2 * (i - 1))
                    L(nc.vector.tensor_reduce(mx[:, i % 2], scores(i).rearrange("p (m n) -> p m n", n=ALL), AX, ALU.max))
                    nc.vector.tensor_scalar(mx[:, i % 2], mx[:, i % 2], -SC, None, ALU.mult).then_inc(biased, 1)
                if 0 <= i - 3 < U:
                    j = i - 3
                    tile, h = units[j]
                    n = hh * 4 + h
                    dve.wait_ge(summed, j + 1)
                    nc.vector.tensor_copy(o[:, tile, n * P:(n + 1) * P], c.ps[:, 7, 2 * P:3 * P]).then_inc(left, 1)
                if 0 <= i - 1 < U:
                    j = i - 1
                    r = ls[:, j % 3]
                    dve.wait_ge(expd, 2 * j + 2)
                    L(nc.vector.reciprocal(r, r))
                    nc.vector.tensor_scalar(pr[:, j % 3, 0], pr[:, j % 3, 0], r[:, 0:1], None, ALU.mult)
                    L(nc.vector.tensor_tensor(r[:, 1:2], r[:, 1:2], lam[:], ALU.mult))
                    nc.vector.scalar_tensor_tensor(pr[:, j % 3, 0], pr[:, j % 3, 1], r[:, 1:2], pr[:, j % 3, 0], ALU.mult, ALU.add).then_inc(mixed, 1)
                if 0 <= i - 2 < U:
                    j = i - 2
                    dve.wait_ge(turned, j + 1)
                    if j >= 2:
                        dve.wait_ge(summed, j - 1)
                    nc.vector.tensor_copy(prT[:, j % 2, 4:6], c.ps[:, 7, 0:2 * P].rearrange("p (b n) -> p b n", n=P)).then_inc(copied_v, 1)


def merge(c, w_in, yT, oT):
    nc, t = c.nc, c.t
    with ExitStack() as s:
        mT = c.sb(s, "mergedT", [P, KD, SEQ])
        with ExitStack() as b:
            sg = c.sb(b, "sigmoids", [P, 2, 2, SEQ])
            tmp = c.sb(b, "gated_ssd", [P, SEQ])
            done = c.sem("mg_done")
            gates = c.sem("mg_gates")
            sigd = c.sem("mg_sigmoid")
            left = c.sem("mg_left")
            tiles = [(cols(w_in, G0 + hf * GW), cols(w_in, G0 + D + hf * GW), cols(t["w_branch_attn"][0], hf * GW), cols(t["w_branch_ssd"][0], hf * GW))
                     for hf in range(2)]
            block = b.enter_context(nc.Block())

            @block.sync
            def _(sp):
                load_weights(c, sp, [[(0, KD, FT2, src[:, :, q * FT2:(q + 1) * FT2]), (KD * FT2, KD, FT2, src2[:, :, q * FT2:(q + 1) * FT2])]
                                     for hf in range(2) for q in range(2) for src, src2 in (tiles[hf][0:2], tiles[hf][2:4])])

            @block.tensor
            def _(pe):
                for n in range(4):
                    for pair in range(2):
                        w = take(c, pe, 2).rearrange("p (v k n) -> p v k n", v=2, k=KD)
                        for f in range(2):
                            i = 2 * n + f
                            b0 = 4 * (i % 2)
                            if i >= 2 and pair == 0:
                                pe.wait_ge(left, i - 1)
                            for v in range(2):
                                src = c.hT if pair == 0 else (oT, yT)[v]
                                for k in range(KD):
                                    last = mm(c, c.ps[:, b0 + 2 * pair + v], w[:, v, k, f * P:(f + 1) * P], src[:, k], k == 0, k == KD - 1)
                            last.then_inc(gates if pair == 0 else done, 1)

            @block.scalar
            def _(act):
                for i in range(KD):
                    act.wait_ge(gates, i + 1)
                    if i >= 2:
                        act.wait_ge(left, i - 1)
                    nc.scalar.activation(sg[:, i % 2].rearrange("p v n -> p (v n)"), c.ps[:, 4 * (i % 2):4 * (i % 2) + 2].rearrange("p b n -> p (b n)"),
                                         ACT.Sigmoid).then_inc(sigd, 1)

            @block.vector
            def _(dve):
                for i in range(KD):
                    dve.wait_ge(done, i + 1)
                    dve.wait_ge(sigd, i + 1)
                    b0 = 4 * (i % 2)
                    if i:
                        dve.wait_ge(left, i)
                    nc.vector.tensor_tensor(tmp[:], c.ps[:, b0 + 3], sg[:, i % 2, 1], ALU.mult)
                    c.vlink(dve, nc.vector.tensor_tensor(mT[:, i], c.ps[:, b0 + 2], sg[:, i % 2, 0], ALU.mult))
                    nc.vector.tensor_tensor(mT[:, i], mT[:, i], tmp[:], ALU.add).then_inc(left, 1)
        wo = t["w_out"][0]
        project_residual(c, [[(KD, cols(wo, hf * GW))] for hf in range(2)], lambda k, tile: mT[:, k, tile * P:(tile + 1) * P], c.gate[:, 0])
I32 = mybir.dt.int32
EXPERTS, TOP_K, GROUPS, TOP_GROUPS, EF = 64, 8, 8, 4, 256
ROUTED_SCALE = 2.5
MOST_BLOCKS = SEQ * TOP_K // P + EXPERTS
TABLE = MOST_BLOCKS + 4
SKIPPED = 1 << 20
PICKED = -3e30


def moe(c):
    nc, t = c.nc, c.t
    h_dram = nc.dram_tensor("h2_tokens", (SEQ, D), F32, kind="Internal").ap()
    table = nc.dram_tensor("block_table", (TABLE * P, 4), I32, kind="Internal").ap()
    y_dram = nc.dram_tensor("expert_rows", (SEQ * TOP_K, D), F32, kind="Internal").ap()
    norm_transpose(c, c.x, NT, [(lambda k, tile: c.hT[:, k, tile * P:(tile + 1) * P],
                                 lambda k: c.scale2[:, k:k + 1], lambda k: c.shift2[:, k:k + 1])])
    with ExitStack() as s:
        acc = c.sb(s, "ffn_out", [P, NT, D])
        erow = c.sb(s, "block_expert", [1, TABLE], I32)
        count = c.sb(s, "block_count", [1, 1], I32)
        route(c, h_dram, table, erow, count)
        shared_expert(c, acc)
        expert_blocks(c, h_dram, table, y_dram, erow, count)
        combine(c, y_dram, acc)


def route(c, h_dram, table, erow, count):
    nc, t = c.nc, c.t
    LE, LT, ONES = range(3)
    E = EXPERTS
    with ExitStack() as s:
        ht = c.sb(s, "h_tokens", [P, NT, D])
        tri = c.sb(s, "triangles", [P, 3, P])
        bias = c.sb(s, "router_bias", [P, E])
        init = c.sb(s, "table_start", [P, TABLE, 4], I32)
        pay = c.sb(s, "payload", [P, NT, TOP_K, 4], I32)
        small = c.sb(s, "rank_tables", [P, 64 + 8])
        iota = c.sb(s, "block_numbers", [P, TABLE])
        sg = c.sb(s, "scores", [P, NT, E])
        sel = c.sb(s, "selection", [P, NT, E])
        top = c.sb(s, "sorted", [P, NT * GROUPS, 8])
        gs = c.sb(s, "group_scores", [P, NT, GROUPS])
        pair = c.sb(s, "pairs", [P, NT, GROUPS, GROUPS])
        equal = c.sb(s, "equal_pairs", [P, NT, GROUPS, GROUPS])
        mask = c.sb(s, "chosen", [P, NT, E])
        key = c.sb(s, "order", [P, NT, E])
        wt = c.sb(s, "weights", [P, NT, E])
        dest = c.sb(s, "destinations", [P, NT, E])
        tot = c.sb(s, "weight_sums", [P, NT])
        cnt = c.sb(s, "counts", [E, 4])
        nbw = c.sb(s, "block_counts_wide", [E, P])
        over = c.sb(s, "blocks_over", [E, TABLE])
        start = c.sb(s, "block_starts", [P, E])
        pick = c.sb(s, "picks", [P, TOP_K, E])
        got = c.sb(s, "picked", [P, NT, TOP_K])
        desti = c.sb(s, "destination_rows", [P, NT, TOP_K], I32)
        nrow = c.sb(s, "block_row", [1, TABLE])
        even = c.sb(s, "pair_flags", [1, TABLE])
        landed = c.sem("ro_landed")
        inited = c.sem("ro_table_started")
        logits = c.sem("ro_logits")
        scored = c.sem("ro_scores")
        chosen = c.sem("ro_chosen")
        counted = c.sem("ro_counted")
        blocked = c.sem("ro_blocked")
        summed = c.sem("ro_summed")
        compared = c.sem("ro_compared")
        numbered = c.sem("ro_numbered")
        filled = c.sem("ro_filled")
        sent = c.sem("ro_sent")
        turned = c.sem("ro_turned")
        copied = c.sem("ro_copied")
        stored = c.sem("ro_stored")
        block = s.enter_context(nc.Block())

        @block.sync
        def _(sp):
            for i, m in enumerate((0, 3, 4)):
                sp.dma_start(tri[:, i], t["tri"][m]).then_inc(landed, 16)
            sp.dma_start(bias[:], t["router_bias"].to_broadcast([P, E])).then_inc(landed, 16)
            sp.dma_start(pay[:], t["payload"]).then_inc(landed, 16)
            sp.dma_start(small[:], t["rank"].to_broadcast([P, 72])).then_inc(landed, 16)
            sp.dma_start(iota[:], t["blocks"].to_broadcast([P, TABLE])).then_inc(landed, 16)
            sp.dma_start(init[:], t["table"].rearrange("(p n) w -> p n w", p=P)).then_inc(landed, 16)
            load_weights(c, sp, [whole(cols(t["w_router"][0], 0, E))])
            sp.wait_ge(landed, 128)
            sp.dma_start(table.rearrange("(p n) w -> p n w", p=P), init[:]).then_inc(inited, 16)
            for tile in range(NT):
                sp.wait_ge(copied, 2 * tile + 2)
                sp.dma_start(h_dram[tile * P:(tile + 1) * P], ht[:, tile]).then_inc(stored, 16)
            sp.wait_ge(stored, 16 * NT)

        @block.tensor
        def _(pe):
            w = take(c, pe, 1)
            for tile in range(NT):
                for k in range(KD):
                    last = mm(c, c.ps[:, 0, tile * E:(tile + 1) * E], c.hT[:, k, tile * P:(tile + 1) * P], w[:, k * E:(k + 1) * E], k == 0, k == KD - 1)
            last.then_inc(logits, 1)
            for tile in range(NT):
                if tile:
                    pe.wait_ge(copied, 2 * tile)
                for k in range(KD):
                    last = nc.tensor.transpose(c.ps[:, 6 + k // 4, (k % 4) * P:(k % 4 + 1) * P], c.hT[:, k, tile * P:(tile + 1) * P], c.ident[:])
                last.then_inc(turned, 1)
            pe.wait_ge(landed, 128)
            pe.wait_ge(chosen, 1)
            for tile in range(NT):
                for j in range(tile + 1):
                    nc.tensor.matmul(c.ps[:, 1, tile * E:(tile + 1) * E], tri[:, LT if j == tile else ONES], mask[:, j], start=j == 0, stop=j == tile)
            for j in range(NT):
                last = nc.tensor.matmul(c.ps[0:E, 2, 0:1], mask[:, j], tri[:, ONES, 0:1], start=j == 0, stop=j == NT - 1)
            last.then_inc(counted, 1)
            pe.wait_ge(blocked, 1)
            nc.tensor.matmul(c.ps[:, 3, 0:E], nbw[:], tri[0:E, LT, 0:E], start=True, stop=True)
            nc.tensor.matmul(c.ps[:, 3, E:2 * E], nbw[:], tri[0:E, ONES, 0:E], start=True, stop=True)
            nc.tensor.matmul(c.ps[0:E, 4, 0:1], tri[0:E, LE, 0:E], nbw[:, 0:1], start=True, stop=True).then_inc(summed, 1)
            pe.wait_ge(compared, 1)
            nc.tensor.matmul(c.ps[0:1, 5, 0:TABLE], tri[0:E, ONES, 0:1], over[:], start=True, stop=True).then_inc(numbered, 1)

        @block.scalar
        def _(act):
            act.wait_ge(logits, 1)
            nc.scalar.activation(sg[:].rearrange("p t e -> p (t e)"), c.ps[:, 0, 0:NT * E], ACT.Sigmoid).then_inc(scored, 1)
            for tile in range(NT):
                act.wait_ge(turned, tile + 1)
                for b in range(2):
                    nc.scalar.activation(ht[:, tile, b * GW:(b + 1) * GW], c.ps[:, 6 + b], ACT.Copy).then_inc(copied, 1)

        @block.gpsimd
        def _(pool):
            pool.wait_ge(filled, 1)
            pool.wait_ge(inited, 16)
            for tile in range(NT):
                for r in range(TOP_K):
                    nc.gpsimd.indirect_dma_start(table, bass.IndirectOffsetOnAxis(desti[:, tile, r:r + 1], 0), pay[:, tile, r], None).then_inc(sent, 16)
            pool.wait_ge(sent, 16 * NT * TOP_K)

        @block.vector
        def _(dve):
            L = lambda ins: c.vlink(dve, ins)
            V = nc.vector
            dve.wait_ge(landed, 128)
            dve.wait_ge(scored, 1)
            L(V.tensor_tensor(sel[:], sg[:], bias[:].unsqueeze(1).to_broadcast([P, NT, E]), ALU.add))
            for n in range(NT * GROUPS):
                ins = V.max(top[:, n], sel[:, n // GROUPS, (n % GROUPS) * 8:(n % GROUPS + 1) * 8])
            L(ins)
            L(V.tensor_tensor(gs[:].rearrange("p t g -> p (t g)"), top[:, :, 0], top[:, :, 1], ALU.add))
            for tile in range(NT):
                other = gs[:, tile].unsqueeze(1).to_broadcast([P, GROUPS, GROUPS])
                own = gs[:, tile].unsqueeze(2).to_broadcast([P, GROUPS, GROUPS])
                V.tensor_tensor(pair[:, tile], other, own, ALU.is_gt)
                ins = V.tensor_tensor(equal[:, tile], other, own, ALU.is_equal)
            L(ins)
            before = small[:, 0:64].rearrange("p (i j) -> p i j", j=GROUPS)
            for tile in range(NT):
                ins = V.tensor_tensor(equal[:, tile], equal[:, tile], before, ALU.mult)
            L(ins)
            L(V.tensor_tensor(pair[:], pair[:], equal[:], ALU.add))
            L(V.tensor_reduce(gs[:], pair[:], AX, ALU.add))
            L(V.tensor_scalar(gs[:], gs[:], float(TOP_GROUPS), None, ALU.is_lt))
            for tile in range(NT):
                ins = V.tensor_tensor(sel[:, tile].rearrange("p (g e) -> p g e", e=8), sel[:, tile].rearrange("p (g e) -> p g e", e=8),
                                      gs[:, tile].unsqueeze(2).to_broadcast([P, GROUPS, 8]), ALU.mult)
            L(ins)
            L(V.tensor_scalar(gs[:], gs[:], -1.0, -NEG, ALU.add, ALU.mult))
            for tile in range(NT):
                ins = V.tensor_tensor(sel[:, tile].rearrange("p (g e) -> p g e", e=8), sel[:, tile].rearrange("p (g e) -> p g e", e=8),
                                      gs[:, tile].unsqueeze(2).to_broadcast([P, GROUPS, 8]), ALU.add)
            L(ins)
            for tile in range(NT):
                ins = V.max(top[:, tile], sel[:, tile])
            L(ins)
            for tile in range(NT):
                ins = V.match_replace(mask[:, tile], top[:, tile], sel[:, tile], PICKED)
            L(ins)
            V.tensor_scalar(mask[:], mask[:], 0.5 * (PICKED + NEG), None, ALU.is_lt).then_inc(chosen, 1)
            dve.wait_ge(chosen, 1)
            L(V.tensor_tensor(wt[:], sg[:], mask[:], ALU.mult))
            L(V.tensor_reduce(tot[:], wt[:], AX, ALU.add))
            L(V.reciprocal(tot[:], tot[:]))
            L(V.tensor_scalar(tot[:], tot[:], ROUTED_SCALE, None, ALU.mult))
            L(V.tensor_tensor(wt[:], wt[:], tot[:].unsqueeze(2).to_broadcast([P, NT, E]), ALU.mult))
            for tile in range(NT):
                ins = V.tensor_tensor_scan(key[:, tile], tri[:, ONES, 0:E], mask[:, tile], 0.0, ALU.mult, ALU.add)
            L(ins)
            L(V.tensor_tensor(key[:], key[:], mask[:], ALU.mult))
            dve.wait_ge(counted, 1)
            L(V.tensor_copy(cnt[:, 0:1], c.ps[0:E, 2, 0:1]))
            L(V.tensor_scalar(cnt[:, 1:2], cnt[:, 0:1], 0.0, None, ALU.is_gt))
            for n in range(1, NT):
                L(V.tensor_scalar(cnt[:, 2:3], cnt[:, 0:1], float(n * P), None, ALU.is_gt))
                L(V.tensor_tensor(cnt[:, 1:2], cnt[:, 1:2], cnt[:, 2:3], ALU.add))
            V.tensor_copy(nbw[:], cnt[:, 1:2].to_broadcast([E, P])).then_inc(blocked, 1)
            dve.wait_ge(summed, 1)
            L(V.tensor_copy(cnt[:, 3:4], c.ps[0:E, 4, 0:1]))
            V.tensor_scalar(over[:], iota[0:E], cnt[:, 3:4], None, ALU.is_ge).then_inc(compared, 1)
            L(V.tensor_scalar(start[:], c.ps[:, 3, 0:E], float(P), None, ALU.mult))
            L(V.tensor_tensor(dest[:], c.ps[:, 1, 0:NT * E].rearrange("p (t e) -> p t e", e=E), start[:].unsqueeze(1).to_broadcast([P, NT, E]), ALU.add))
            for src, out in ((dest, desti), (wt, None)):
                for tile in range(NT):
                    L(V.tensor_tensor(pick[:], key[:, tile].unsqueeze(1).to_broadcast([P, TOP_K, E]), small[:, 64:72].unsqueeze(2).to_broadcast([P, TOP_K, E]), ALU.is_equal))
                    L(V.tensor_tensor(pick[:], pick[:], src[:, tile].unsqueeze(1).to_broadcast([P, TOP_K, E]), ALU.mult))
                    L(V.tensor_reduce(got[:, tile], pick[:], AX, ALU.add))
                if out is not None:
                    L(V.tensor_copy(out[:], got[:]))
            V.tensor_copy(pay[:].bitcast(F32)[:, :, :, 1], got[:]).then_inc(filled, 1)
            dve.wait_ge(numbered, 1)
            L(V.tensor_scalar(nrow[:], c.ps[0:1, 5, 0:TABLE], float(E - 1), None, ALU.min))
            L(V.tensor_copy(erow[:], nrow[:]))
            L(V.tensor_reduce(nrow[:, 0:1], c.ps[0:1, 3, E:2 * E], AX, ALU.max))
            L(V.tensor_scalar(even[:, 0:TABLE // 2], iota[0:1, 0:TABLE:2], nrow[:, 0:1], None, ALU.is_lt))
            L(V.tensor_reduce(nrow[:, 1:2], even[:, 0:TABLE // 2], AX, ALU.add))
            L(V.tensor_scalar(nrow[:, 2:3], nrow[:, 1:2], 2.0, None, ALU.mult))
            V.tensor_copy(count[:], nrow[:, 2:3])


def shared_expert(c, acc):
    nc, t = c.nc, c.t
    with ExitStack() as s:
        sl = c.sb(s, "silu", [P, 2, SEQ])
        hid = c.sb(s, "hidden", [P, 2, SEQ])
        up = c.sem("se_up")
        silud = c.sem("se_silu")
        gated = c.sem("se_gated")
        down = c.sem("se_down")
        block = s.enter_context(nc.Block())

        @block.sync
        def _(sp):
            load_weights(c, sp, [[(0, KD, EF, cols(t["w_sh_gate"][0], 0, EF)), (KD * EF, KD, EF, cols(t["w_sh_up"][0], 0, EF))],
                                 whole(cols(t["w_sh_down"][0], 0, D))])

        @block.tensor
        def _(pe):
            w = take(c, pe, 2).rearrange("p (v k n) -> p v k n", v=2, k=KD)
            for f in range(2):
                for v in range(2):
                    for k in range(KD):
                        last = mm(c, c.ps[:, 2 * f + v], w[:, v, k, f * P:(f + 1) * P], c.hT[:, k], k == 0, k == KD - 1)
                last.then_inc(up, 1)
            w = take(c, pe, 1)[:, 0:2 * D].rearrange("p (k n) -> p k n", k=2)
            pe.wait_ge(gated, 2)
            for tile in range(NT):
                for hf in range(2):
                    for k in range(2):
                        last = mm(c, c.ps[:, 2 * tile + hf], hid[:, k, tile * P:(tile + 1) * P], w[:, k, hf * GW:(hf + 1) * GW], k == 0, k == 1)
                last.then_inc(down, 1)

        @block.scalar
        def _(act):
            for f in range(2):
                act.wait_ge(up, f + 1)
                nc.scalar.activation(sl[:, f], c.ps[:, 2 * f], ACT.Silu).then_inc(silud, 1)

        @block.vector
        def _(dve):
            for f in range(2):
                dve.wait_ge(silud, f + 1)
                nc.vector.tensor_tensor(hid[:, f], sl[:, f], c.ps[:, 2 * f + 1], ALU.mult).then_inc(gated, 1)
            for tile in range(NT):
                dve.wait_ge(down, tile + 1)
                nc.vector.tensor_copy(acc[:, tile], c.ps[:, 2 * tile:2 * tile + 2].rearrange("p b n -> p (b n)"))


def expert_blocks(c, h_dram, table, y_dram, erow, count):
    nc, t = c.nc, c.t
    ws = {n: t[n][0] for n in ("w_e_gate", "w_e_up", "w_e_down")}
    tab = table.rearrange("(b p) w -> b p w", p=P)
    with ExitStack() as s:
        both = lambda name, shape, dt=F32: [c.sb(s, f"{name}{p}", shape, dt) for p in range(2)]
        sems = lambda name: [c.sem(f"{name}{p}") for p in range(2)]
        wgu = both("gate_up", [P, KD, 2 * EF])
        wd = both("down", [P, 2, D])
        fetch = both("fetch_rows", [P, 4], I32)
        give = both("give_rows", [P, 4], I32)
        xg = both("gathered", [P, D])
        xT = both("gatheredT", [P, KD, P])
        sl = both("silu", [P, EF])
        hid = both("hidden", [P, EF])
        hidT = both("hiddenT", [P, 2, P])
        y = both("weighted_out", [P, D])
        wgu_in, wd_in, fetch_in, give_in = sems("gate_up_in"), sems("down_in"), sems("fetch_in"), sems("give_in")
        gathered, scattered = sems("gathered"), sems("scattered")
        up_done, silud, gated, turned, copied, down_done = sems("up_done"), sems("silued"), sems("gated"), sems("hid_turned"), sems("hid_copied"), sems("down_done")
        x_turned, x_low, x_high, y_ready = sems("x_turned"), sems("x_low"), sems("x_high"), sems("y_ready")
        passed = c.sem("waits_passed")
        block = s.enter_context(nc.Block())

        def trips(eng):
            return eng.value_load(count[0:1, 0:1], min_val=2, max_val=MOST_BLOCKS)

        @block.sync
        def _(sp):
            def weights(p, b):
                e = sp.value_load(erow[0:1, bass.ds(b, 1)], min_val=0, max_val=EXPERTS - 1)
                return e

            def gate_up(p, e):
                for v, name in enumerate(("w_e_gate", "w_e_up")):
                    sp.dma_start(wgu[p][:, :, v * EF:(v + 1) * EF], ws[name][bass.ds(e, 1)].rearrange("o (k p) n -> p (o k) n", p=P)).then_inc(wgu_in[p], 16)

            def down(p, e):
                sp.dma_start(wd[p][:], ws["w_e_down"][bass.ds(e, 1)].rearrange("o (k p) n -> p (o k) n", p=P)).then_inc(wd_in[p], 16)

            for p in range(2):
                e = weights(p, p)
                gate_up(p, e)
                down(p, e)
            n = trips(sp)
            with sp.Fori(0, n, 2) as i:
                for p in range(2):
                    e = weights(p, i + (2 + p))
                    sp.wait_ge(up_done[p], i + 2)
                    gate_up(p, e)
                    sp.wait_ge(down_done[p], i + 4)
                    down(p, e)
            for p in range(2):
                sp.wait_ge(wgu_in[p], 16 * n + 32)
                sp.wait_ge(wd_in[p], 8 * n + 16)
            sp.sem_inc(passed, 1)

        @block.gpsimd
        def _(pool):
            def rows(dst, sem, b):
                nc.gpsimd.dma_start(dst[:], tab[bass.ds(b, 1)].rearrange("o p w -> p (o w)")).then_inc(sem, 16)

            def gather(p):
                nc.gpsimd.indirect_dma_start(xg[p][:], None, h_dram, bass.IndirectOffsetOnAxis(fetch[p][:, 0:1], 0)).then_inc(gathered[p], 16)

            for p in range(2):
                rows(fetch[p], fetch_in[p], p)
            for p in range(2):
                pool.wait_ge(fetch_in[p], 16)
                gather(p)
            for p in range(2):
                rows(give[p], scattered[p], p)
            n = trips(pool)
            with pool.Fori(0, n, 2) as i:
                for p in range(2):
                    pool.wait_ge(scattered[p], 8 * i + 16)
                    rows(give[p], give_in[p], i + p)
                    pool.wait_ge(gathered[p], 8 * i + 16)
                    rows(fetch[p], fetch_in[p], i + (2 + p))
                for p in range(2):
                    pool.wait_ge(fetch_in[p], 8 * i + 32)
                    pool.wait_ge(x_turned[p], i + 2)
                    pool.sem_inc(passed, 1)
                    gather(p)
                for p in range(2):
                    pool.wait_ge(give_in[p], 8 * i + 16)
                    pool.wait_ge(y_ready[p], i + 4)
                    pool.sem_inc(passed, 1)
                    nc.gpsimd.indirect_dma_start(y_dram, bass.IndirectOffsetOnAxis(give[p][:, 2:3], 0), y[p][:], None,
                                                 bounds_check=SEQ * TOP_K - 1, oob_is_err=False).then_inc(scattered[p], 16)
            for p in range(2):
                pool.wait_ge(scattered[p], 8 * n + 16)
                pool.wait_ge(gathered[p], 8 * n + 16)
            pool.sem_inc(passed, 1)

        @block.tensor
        def _(pe):
            def x_transposes(p):
                for k in range(KD):
                    last = nc.tensor.transpose(c.ps[:, 5 + k // 4, (k % 4) * P:(k % 4 + 1) * P], xg[p][:, k * P:(k + 1) * P], c.ident[:])
                last.then_inc(x_turned[p], 2)

            for p in range(2):
                pe.wait_ge(gathered[p], 16)
                if p:
                    pe.wait_ge(x_low[0], 2)
                    pe.wait_ge(x_high[0], 2)
                x_transposes(p)
            for p in range(2):
                pe.sem_inc(turned[p], 2)
                pe.sem_inc(down_done[p], 2)
            n = trips(pe)
            with pe.Fori(0, n, 2) as i:
                for p in range(2):
                    pe.wait_ge(x_low[p], i + 2)
                    pe.wait_ge(x_high[p], i + 2)
                    pe.wait_ge(wgu_in[p], 16 * i + 32)
                    pe.wait_ge(gated[p], i + 2)
                    for k in range(KD):
                        last = nc.tensor.matmul(c.ps[:, p], xT[p][:, k], wgu[p][:, k], start=k == 0, stop=k == KD - 1)
                    last.then_inc(up_done[p], 2)
                for p in range(2):
                    pe.wait_ge(gated[p], i + 4)
                    pe.wait_ge(copied[1 - p], i + 2 + 2 * p)
                    for k in range(2):
                        last = nc.tensor.transpose(c.ps[:, 2, k * P:(k + 1) * P], hid[p][:, k * P:(k + 1) * P], c.ident[:])
                    last.then_inc(turned[p], 2)
                    pe.wait_ge(gathered[p], 8 * i + 32)
                    pe.wait_ge(x_low[1 - p], i + 2 + 2 * p)
                    pe.wait_ge(x_high[1 - p], i + 2 + 2 * p)
                    x_transposes(p)
                    pe.wait_ge(copied[p], i + 4)
                    pe.wait_ge(wd_in[p], 8 * i + 16)
                    pe.wait_ge(y_ready[1 - p], i + 2 + 2 * p)
                    for hf in range(2):
                        for k in range(2):
                            last = nc.tensor.matmul(c.ps[:, 3 + hf], hidT[p][:, k], wd[p][:, k, hf * GW:(hf + 1) * GW], start=k == 0, stop=k == 1)
                    last.then_inc(down_done[p], 2)

        @block.scalar
        def _(act):
            def x_low_half(p):
                nc.scalar.activation(xT[p][:, 0:4], c.ps[:, 5].rearrange("p (k n) -> p k n", n=P), ACT.Copy).then_inc(x_low[p], 2)

            for p in range(2):
                act.wait_ge(x_turned[p], 2)
                x_low_half(p)
            for p in range(2):
                act.sem_inc(y_ready[p], 2)
            n = trips(act)
            with act.Fori(0, n, 2) as i:
                for p in range(2):
                    act.wait_ge(up_done[p], i + 2)
                    act.wait_ge(gated[p], i + 2)
                    nc.scalar.activation(sl[p][:], c.ps[:, p, 0:EF], ACT.Silu).then_inc(silud[p], 2)
                for p in range(2):
                    act.wait_ge(x_turned[p], i + 4)
                    x_low_half(p)
                    act.wait_ge(down_done[p], i + 4)
                    act.wait_ge(scattered[p], 8 * i + 16)
                    act.wait_ge(give_in[p], 8 * i + 16)
                    nc.scalar.activation(y[p][:], c.ps[:, 3:5].rearrange("p b n -> p (b n)"), ACT.Copy, scale=give[p][:, 1:2].bitcast(F32)).then_inc(y_ready[p], 2)

        @block.vector
        def _(dve):
            def x_high_half(p):
                nc.vector.tensor_copy(xT[p][:, 4:8], c.ps[:, 6].rearrange("p (k n) -> p k n", n=P)).then_inc(x_high[p], 2)

            for p in range(2):
                dve.wait_ge(x_turned[p], 2)
                x_high_half(p)
            for p in range(2):
                dve.sem_inc(gated[p], 2)
                dve.sem_inc(copied[p], 2)
            n = trips(dve)
            with dve.Fori(0, n, 2) as i:
                for p in range(2):
                    dve.wait_ge(silud[p], i + 2)
                    dve.wait_ge(turned[p], i + 2)
                    nc.vector.tensor_tensor(hid[p][:], sl[p][:], c.ps[:, p, EF:2 * EF], ALU.mult).then_inc(gated[p], 2)
                for p in range(2):
                    dve.wait_ge(turned[p], i + 4)
                    dve.wait_ge(down_done[p], i + 2)
                    nc.vector.tensor_copy(hidT[p][:], c.ps[:, 2, 0:2 * P].rearrange("p (k n) -> p k n", n=P)).then_inc(copied[p], 2)
                    dve.wait_ge(x_turned[p], i + 4)
                    x_high_half(p)


def combine(c, y_dram, acc):
    nc = c.nc
    with ExitStack() as s:
        rows = c.sb(s, "expert_rows", [P, 2, TOP_K, D])
        tot = c.sb(s, "row_sums", [P, D])
        sq = c.sb(s, "squares", [P, D])
        ss = c.sb(s, "sum_squares", [P, NT])
        landed = [c.sem(f"rows_landed{p}") for p in range(2)]
        reduced = c.sem("co_reduced")
        added = c.sem("co_added")
        summed = c.sem("co_summed")
        meaned = c.sem("co_meaned")
        block = s.enter_context(nc.Block())
        src = y_dram.rearrange("(t p r) d -> t p r d", p=P, r=TOP_K)

        @block.sync
        def _(sp):
            for tile in range(NT):
                if tile >= 2:
                    sp.wait_ge(reduced, tile - 1)
                sp.dma_start(rows[:, tile % 2], src[tile]).then_inc(landed[tile % 2], 16)

        @block.scalar
        def _(act):
            for tile in range(NT):
                act.wait_ge(added, tile + 1)
                if tile:
                    act.wait_ge(summed, tile)
                nc.scalar.activation(sq[:], acc[:, tile], ACT.Square, accum_out=ss[:, tile:tile + 1]).then_inc(summed, 1)

        @block.gpsimd
        def _(pool):
            pool.wait_ge(meaned, 1)
            nc.gpsimd.tensor_tensor(ss[:], ss[:], c.half[:, 0:NT], ALU.pow).then_inc(meaned, 1)

        @block.vector
        def _(dve):
            for tile in range(NT):
                dve.wait_ge(landed[tile % 2], 16 * (tile // 2 + 1))
                if tile:
                    dve.wait_ge(added, tile)
                nc.vector.tensor_reduce(tot[:], rows[:, tile % 2].rearrange("p r d -> p d r"), AX, ALU.add).then_inc(reduced, 1)
                dve.wait_ge(reduced, tile + 1)
                nc.vector.tensor_tensor(acc[:, tile], acc[:, tile], tot[:], ALU.add).then_inc(added, 1)
            dve.wait_ge(summed, NT)
            nc.vector.tensor_scalar(ss[:], ss[:], 1.0 / D, EPS, ALU.mult, ALU.add).then_inc(meaned, 1)
            dve.wait_ge(meaned, 2)
            for tile in range(NT):
                ins = nc.vector.scalar_tensor_tensor(acc[:, tile], acc[:, tile], ss[:, tile:tile + 1], c.gate[:, 1], ALU.mult, ALU.mult)
            c.vlink(dve, ins)
            for tile in range(NT):
                nc.vector.tensor_tensor(c.x[:, tile], c.x[:, tile], acc[:, tile], ALU.add)


def moe_constants():
    g = np.arange(GROUPS)
    rank = np.concatenate([(g[None, :] < g[:, None]).reshape(-1), np.arange(1, TOP_K + 1)]).astype(np.float32)[None]
    tok = (np.arange(NT)[None, :] * P + np.arange(P)[:, None])
    pay = np.zeros((P, NT, TOP_K, 4), np.int32)
    pay[..., 0] = tok[:, :, None]
    pay[..., 2] = tok[:, :, None] * TOP_K + np.arange(TOP_K)
    table = np.zeros((TABLE * P, 4), np.int32)
    table[:, 2] = SKIPPED
    return {"rank": rank, "payload": pay, "table": table, "blocks": np.arange(TABLE, dtype=np.float32)[None]}


def build(nc, t, out):
    with ExitStack() as ctx:
        c = Chip(nc, ctx, t)
        landed = c.sem("x_landed")
        stored = c.sem("out_stored")
        c.sems = []
        with ExitStack() as s:
            block = s.enter_context(nc.Block())

            @block.sync
            def _(sp):
                sp.dma_start(c.x[:], t["x"][0].rearrange("(t p) d -> p t d", p=P)).then_inc(landed, 16)
                sp.dma_start(c.ident[:], t["ident"]).then_inc(landed, 16)
                sp.wait_ge(landed, 32)

            @block.vector
            def _(dve):
                nc.vector.memset(c.half[:], -0.5)
        block1_mixer(c)
        c.clear_sems()
        moe(c)
        c.clear_sems()
        block2(c)
        with ExitStack() as s:
            block = s.enter_context(nc.Block())

            @block.sync
            def _(sp):
                sp.dma_start(out[0].rearrange("(t p) d -> p t d", p=P), c.x[:]).then_inc(stored, 16)
                sp.wait_ge(stored, 16)


def kernel(**inputs):
    import numpy as _np
    import concourse.bacc as _bacc
    from concourse.bass_utils import run_bass_kernel_spmd as _run

    nc = _bacc.Bacc("TRN2", target_bir_lowering=False, num_devices=1)
    arrays = {f"in_{k}": _np.ascontiguousarray(v) for k, v in inputs.items()}
    arrays.update({f"const_{k}": v for k, v in constants().items()})
    arrays.update({f"const_{k}": v for k, v in moe_constants().items()})
    t = {k.split("_", 1)[1]: nc.dram_tensor(k, v.shape, mybir.dt.from_np(v.dtype), kind="ExternalInput").ap() for k, v in arrays.items()}
    out = nc.dram_tensor("out", (1, SEQ, D), F32, kind="ExternalOutput").ap()
    build(nc, t, out)
    r = _run(nc, [arrays], core_ids=[0])
    return r.results[0]["out"]
```

```python
import numpy as np
import concourse.bass as bass
from concourse import mybir
from contextlib import ExitStack

F32 = mybir.dt.float32
ACT = mybir.ActivationFunctionType
ALU = mybir.AluOpType
AX = mybir.AxisListType.X

P = 128
D = 1024
KD = D // P
SEQ = 512
NT = SEQ // P
CTX = 256
NC = CTX // P
EPS = 1e-6
GW = 512
SLOTS = 2
F32R = mybir.dt.float32r
RAW_SLOTS, PART = 4, 2048


class Link:

    def __init__(self, sem):
        self.sem, self.n = sem, 0

    def __call__(self, eng, ins):
        self.n += 1
        ins.then_inc(self.sem, 1)
        eng.wait_ge(self.sem, self.n)


class Ring:

    def __init__(self, buf, landed, used):
        self.buf, self.landed, self.used = buf, landed, used
        self.sent, self.taken, self.owed = 0, 0, False
        self.filled = [0] * SLOTS

    def slot(self, n):
        return self.buf[:, n % SLOTS]


class Chip:

    def __init__(self, nc, ctx, t):
        self.nc, self.ctx, self.t = nc, ctx, t
        self.uid = 0
        self.sems = []
        self.placed = {}
        self.ps = ctx.enter_context(nc.psum_tensor("banks", [P, 8, GW], F32))
        self.x = self.sb(ctx, "x_tok", [P, NT, D])
        self.hT = self.sb(ctx, "hT", [P, KD, SEQ])
        self.ident = self.sb(ctx, "ident", [P, P])
        self.vlink = Link(self.sem("vector_step"))
        self.alink = Link(self.sem("scalar_step"))
        self.glink = Link(self.sem("pool_step"))
        self.ring = Ring(self.sb(ctx, "weights", [P, SLOTS, KD * GW]),
                         [self.sem(f"weights_landed{i}") for i in range(SLOTS)], self.sem("weights_used"))
        self.gate = self.sb(ctx, "gate_rows", [P, 2, D])
        self.shift2 = self.sb(ctx, "shift2", [P, KD])
        self.scale2 = self.sb(ctx, "scale2", [P, KD])
        self.split = SplitRing(self)
        self.half = self.sb(ctx, "minus_half", [P, 8])
        self.sems = []

    def sb(self, ctx, name, shape, dt=F32):
        self.uid += 1
        start = (self.nc.sbuf_base + 31) // 32 * 32
        tensor = ctx.enter_context(self.nc.sbuf_tensor(f"{name}_{self.uid}", shape, dt))
        self.placed[id(tensor)] = (tensor, name, start, shape)
        return tensor

    def rounded(self, tensor):
        _, name, start, shape = self.placed[id(tensor)]
        self.uid += 1
        return self.nc.alloc_sbuf_tensor_at(f"{name}_r_{self.uid}", shape, F32R, offset=start)

    def sem(self, name):
        self.uid += 1
        s = self.nc.alloc_semaphore(f"{name}_{self.uid}")
        self.sems.append(s)
        return s

    def clear_sems(self):
        self.nc.clear_and_free_semaphores(self.sems)
        self.nc.all_engine_barrier()
        self.sems = []


def cols(ap, c0, n=GW):
    return ap[:, c0:c0 + n].rearrange("(k p) n -> p k n", p=P)


def load_weights(c, sp, tiles):
    r = c.ring
    for parts in tiles:
        n = r.sent
        if n >= SLOTS:
            sp.wait_ge(r.used, n - SLOTS + 1)
        for at, k, w, src in parts:
            dst = r.slot(n)[:, at:at + k * w].rearrange("p (k w) -> p k w", k=k)
            sp.dma_start(dst, src).then_inc(r.landed[n % SLOTS], 16)
        r.sent += 1


def whole(src):
    k, w = src.shape[1], src.shape[2]
    return [(0, k, w, src)]


def take(c, pe, parts):
    c.ring.owed = c.ring.taken > 0
    r = c.ring
    n = r.taken
    r.taken += 1
    r.filled[n % SLOTS] += 16 * parts
    pe.wait_ge(r.landed[n % SLOTS], r.filled[n % SLOTS])
    return r.slot(n)


def mm(c, out, lhs, rhs, start, stop):
    ins = c.nc.tensor.matmul(out, lhs, rhs, start=start, stop=stop)
    if c.ring.owed:
        c.ring.owed = False
        ins.then_inc(c.ring.used, 1)
    return ins


class SplitRing:

    def __init__(self, c):
        flat = c.ring.buf[:].rearrange("p s n -> p (s n)")
        self.raw = [flat[:, i * PART:(i + 1) * PART] for i in range(RAW_SLOTS)]
        self.landed = [c.sem(f"raw_landed{i}") for i in range(RAW_SLOTS)]
        self.high_ready, self.low_ready, self.used = c.sem("high_ready"), c.sem("low_ready"), c.sem("split_used")
        self.sizes, self.fill, self.filled = [], [], [0] * RAW_SLOTS
        self.highs = self.lows = self.taken = 0
        self.owed = False
        self.early = 0

    def buffers(self, c, s, spare=()):
        bufs = list(spare) + [c.sb(s, f"weight_part{i}", [P, PART], F32R)[:] for i in range(4 - len(spare))]
        self.parts = [bufs[0:2], bufs[2:4]]

    def ahead(self, sp, tiles):
        self.load(sp, tiles[:RAW_SLOTS])
        self.early = len(tiles[:RAW_SLOTS])

    def load(self, sp, tiles):
        tiles, self.early = tiles[self.early:], 0
        for parts in tiles:
            n = len(self.sizes)
            k = parts[0][0]
            width = sum(w for _, w, _ in parts)
            if n >= RAW_SLOTS:
                sp.wait_ge(self.low_ready, n - RAW_SLOTS + 1)
            dst = self.raw[n % RAW_SLOTS][:, 0:k * width].rearrange("p (k w) -> p k w", k=k)
            at = 0
            for _, w, src in parts:
                sp.dma_start(dst[:, :, at:at + w], src).then_inc(self.landed[n % RAW_SLOTS], 16)
                at += w
            self.filled[n % RAW_SLOTS] += 16 * len(parts)
            self.sizes.append(k * width)
            self.fill.append(self.filled[n % RAW_SLOTS])

    def high(self, c, act):
        n = self.highs
        self.highs += 1
        act.wait_ge(self.landed[n % RAW_SLOTS], self.fill[n])
        if n >= 2:
            act.wait_ge(self.used, n - 1)
        z = self.sizes[n]
        c.nc.scalar.activation(self.parts[n % 2][0][:, 0:z], self.raw[n % RAW_SLOTS][:, 0:z], ACT.Copy).then_inc(self.high_ready, 1)

    def low(self, c, dve):
        n = self.lows
        self.lows += 1
        dve.wait_ge(self.high_ready, n + 1)
        z = self.sizes[n]
        high, low = self.parts[n % 2]
        c.nc.vector.tensor_tensor(low[:, 0:z], self.raw[n % RAW_SLOTS][:, 0:z], high[:, 0:z].bitcast(F32), ALU.subtract).then_inc(self.low_ready, 1)

    def take(self, pe):
        n = self.taken
        self.taken += 1
        self.owed = n > 0
        pe.wait_ge(self.low_ready, n + 1)
        return self.parts[n % 2]


def split_stage(c, pairs):
    nc = c.nc
    with ExitStack() as s:
        rounded = c.sem("values_rounded")
        block = s.enter_context(nc.Block())

        @block.scalar
        def _(act):
            for high, _, values in pairs:
                nc.scalar.activation(high, values, ACT.Copy).then_inc(rounded, 1)

        @block.vector
        def _(dve):
            for n, (high, low, values) in enumerate(pairs):
                dve.wait_ge(rounded, n + 1)
                nc.vector.tensor_tensor(low, values, high.bitcast(F32), ALU.subtract)


def halves(parts, values):
    return [(parts[0][:, k:k + 4], parts[1][:, k:k + 4], values[:, k:k + 4]) for k in (0, 4)]


def mm3(c, out, lhs, rhs, start, stop):
    ins = c.nc.tensor.matmul(out, lhs[0], rhs[0], start=start, stop=False)
    if c.split.owed:
        c.split.owed = False
        ins.then_inc(c.split.used, 1)
    c.nc.tensor.matmul(out, lhs[0], rhs[1], start=False, stop=False)
    return c.nc.tensor.matmul(out, lhs[1], rhs[0], start=False, stop=stop)


def norm_transpose(c, src, nt, outs, order=None, ahead=None):
    nc = c.nc
    with ExitStack() as s:
        sq = c.sb(s, "squares", [P, D])
        ss = c.sb(s, "sum_squares", [P, nt])
        rs = c.sb(s, "rstd", [P, nt])
        xs = c.sb(s, "x_scaled", [P, 2, D])
        summed = c.sem("nt_summed")
        meaned = c.sem("nt_meaned")
        rooted = c.sem("nt_rooted")
        scaled = c.sem("nt_scaled")
        turned = c.sem("nt_turned")
        taken_v = c.sem("nt_taken_v")
        taken_a = c.sem("nt_taken_a")
        block = s.enter_context(nc.Block())

        if ahead:
            @block.sync
            def _(sp):
                ahead(sp)

        @block.scalar
        def _(act):
            for t in range(nt):
                if t:
                    act.wait_ge(summed, t)
                nc.scalar.activation(sq[:], src[:, t], ACT.Square, accum_out=ss[:, t:t + 1]).then_inc(summed, 1)
            for t in range(nt):
                act.wait_ge(turned, 2 * t + 2)
                for k in range(4, 8):
                    for dst, gain, shift in outs:
                        last = nc.scalar.activation(dst(k, t), turned_block(c, t, k, order), ACT.Identity,
                                                    scale=gain(k), bias=shift(k) if shift else 0.0)
                last.then_inc(taken_a, 1)

        @block.gpsimd
        def _(pool):
            pool.wait_ge(meaned, 1)
            nc.gpsimd.tensor_tensor(rs[:], rs[:], c.half[:, 0:nt], ALU.pow).then_inc(rooted, 1)

        @block.vector
        def _(dve):
            dve.wait_ge(summed, nt)
            nc.vector.tensor_scalar(rs[:], ss[:], 1.0 / D, EPS, ALU.mult, ALU.add).then_inc(meaned, 1)
            dve.wait_ge(rooted, 1)
            for t in range(nt + 1):
                if t < nt:
                    if t >= 2:
                        dve.wait_ge(turned, 2 * t - 2)
                    nc.vector.tensor_scalar(xs[:, t % 2], src[:, t], rs[:, t:t + 1], None, ALU.mult).then_inc(scaled, 1)
                if t:
                    u = t - 1
                    dve.wait_ge(turned, 2 * u + 1)
                    for k in range(4):
                        for dst, gain, shift in outs:
                            if shift:
                                last = nc.vector.tensor_scalar(dst(k, u), turned_block(c, u, k, order), gain(k), shift(k),
                                                               ALU.mult, ALU.add)
                            else:
                                last = nc.vector.tensor_scalar(dst(k, u), turned_block(c, u, k, order), gain(k), None, ALU.mult)
                    last.then_inc(taken_v, 1)

        @block.tensor
        def _(pe):
            for t in range(nt):
                pe.wait_ge(scaled, t + 1)
                if t >= 2:
                    pe.wait_ge(taken_v, t - 1)
                    pe.wait_ge(taken_a, t - 1)
                for k in range(KD):
                    b = 2 * (t % 2) + k // 4
                    last = nc.tensor.transpose(c.ps[:, b, (k % 4) * P:(k % 4 + 1) * P], xs[:, t % 2, k * P:(k + 1) * P],
                                               c.ident[:])
                    if k % 4 == 3:
                        last.then_inc(turned, 1)


def turned_block(c, t, k, order):
    blk = c.ps[:, 2 * (t % 2) + k // 4, (k % 4) * P:(k % 4 + 1) * P]
    return order(blk) if order else blk


def plain_transpose(c, src, nt, nk, dst, gain, ahead=None):
    nc = c.nc
    with ExitStack() as s:
        turned = c.sem("pt_turned")
        taken_v = c.sem("pt_taken_v")
        taken_a = c.sem("pt_taken_a")
        block = s.enter_context(nc.Block())

        if ahead:
            @block.sync
            def _(sp):
                c.split.ahead(sp, ahead)

        @block.scalar
        def _(act):
            for t in range(nt):
                act.wait_ge(turned, 2 * t + 2)
                for k in range(4, nk):
                    last = nc.scalar.activation(dst(k, t), turned_block(c, t, k, None), ACT.Copy, scale=gain(k) if gain else 1.0)
                last.then_inc(taken_a, 1)

        @block.vector
        def _(dve):
            for t in range(nt):
                dve.wait_ge(turned, 2 * t + 1)
                for k in range(4):
                    if gain:
                        last = nc.vector.tensor_scalar(dst(k, t), turned_block(c, t, k, None), gain(k), None, ALU.mult)
                    else:
                        last = nc.vector.tensor_copy(dst(k, t), turned_block(c, t, k, None))
                last.then_inc(taken_v, 1)

        @block.tensor
        def _(pe):
            for t in range(nt):
                if t >= 2:
                    pe.wait_ge(taken_v, t - 1)
                    pe.wait_ge(taken_a, t - 1)
                for k in range(nk):
                    b = 2 * (t % 2) + k // 4
                    last = nc.tensor.transpose(c.ps[:, b, (k % 4) * P:(k % 4 + 1) * P], src(t)[:, k * P:(k + 1) * P],
                                               c.ident[:])
                    if k in (3, nk - 1):
                        last.then_inc(turned, 1)


def residual_tiles(w, K):
    return [[(min(4, K - g), GW, w[g * P:min(g + 4, K) * P, hf * GW:(hf + 1) * GW].rearrange("(k p) n -> p k n", p=P))]
            for g in range(0, K, 4) for hf in range(2)]


def project_residual(c, w, K, lhs, gain_b, pair=None, f=None, spare=()):
    nc = c.nc
    groups = [(g, min(4, K - g)) for g in range(0, K, 4)]
    tiles = [(i, hf) for i in range(len(groups)) for hf in range(2)]
    with ExitStack() as s:
        if pair is None:
            pair = (c.sb(s, "lhs_high", [P, KD, SEQ], F32R), c.sb(s, "lhs_low", [P, KD, SEQ], F32R))
        c.split.buffers(c, s, spare)
        f = c.sb(s, "f", [P, NT, D]) if f is None else f
        ss = c.sb(s, "sum_squares", [P, NT, 2])
        rs = c.sb(s, "rstd", [P, NT])
        lhs_high = c.sem("pr_lhs_high")
        lhs_low = c.sem("pr_lhs_low")
        group_used = c.sem("pr_group_used")
        done = c.sem("pr_done")
        summed = c.sem("pr_summed")
        copied = c.sem("pr_copied")
        meaned = c.sem("pr_meaned")
        rooted = c.sem("pr_rooted")
        block = s.enter_context(nc.Block())

        def chunks(i):
            g, n = groups[i]
            return slice(4 * (i % 2), 4 * (i % 2) + n), slice(g, g + n)

        @block.sync
        def _(sp):
            c.split.load(sp, residual_tiles(w, K))

        @block.tensor
        def _(pe):
            for i, hf in tiles:
                g, n = groups[i]
                high, low = (x[:, 0:n * GW].rearrange("p (k n) -> p k n", n=GW) for x in c.split.take(pe))
                if hf == 0:
                    pe.wait_ge(lhs_low, i + 1)
                final = g + n == K
                for t in range(NT):
                    tok = slice(t * P, (t + 1) * P)
                    for j in range(n):
                        at = 4 * (i % 2) + j
                        last = mm3(c, c.ps[:, 4 * hf + t], (pair[0][:, at, tok], pair[1][:, at, tok]), (high[:, j], low[:, j]),
                                   g + j == 0, final and j == n - 1)
                    if final:
                        last.then_inc(done, 1)
                if hf == 1 and not final:
                    last.then_inc(group_used, 1)

        sq = c.split.raw[(len(c.split.sizes) - 2) % RAW_SLOTS][:, 0:GW]

        @block.scalar
        def _(act):
            def lhs_part(i):
                if i >= 2:
                    act.wait_ge(group_used, i - 1)
                to, frm = chunks(i)
                nc.scalar.activation(pair[0][:, to], lhs[:, frm], ACT.Copy).then_inc(lhs_high, 1)
            lhs_part(0)
            c.split.high(c, act)
            for i, hf in tiles[1:]:
                if hf == 0:
                    lhs_part(i)
                c.split.high(c, act)
            for i in range(2 * NT):
                hf, t = divmod(i, NT)
                act.wait_ge(copied, i + 1)
                if i:
                    act.wait_ge(summed, i)
                nc.scalar.activation(sq, f[:, t, hf * GW:(hf + 1) * GW], ACT.Square,
                                     accum_out=ss[:, t, hf:hf + 1]).then_inc(summed, 1)

        @block.gpsimd
        def _(pool):
            pool.wait_ge(meaned, 1)
            nc.gpsimd.tensor_tensor(rs[:], rs[:], c.half[:, 0:NT], ALU.pow).then_inc(rooted, 1)

        @block.vector
        def _(dve):
            for i, hf in tiles:
                if hf == 0:
                    dve.wait_ge(lhs_high, i + 1)
                    to, frm = chunks(i)
                    nc.vector.tensor_tensor(pair[1][:, to], lhs[:, frm], pair[0][:, to].bitcast(F32), ALU.subtract).then_inc(lhs_low, 1)
                c.split.low(c, dve)
            for i in range(2 * NT):
                hf, t = divmod(i, NT)
                dve.wait_ge(done, i + 1)
                nc.vector.tensor_copy(f[:, t, hf * GW:(hf + 1) * GW], c.ps[:, i]).then_inc(copied, 1)
            dve.wait_ge(summed, 2 * NT)
            c.vlink(dve, nc.vector.tensor_tensor(rs[:], ss[:, :, 0], ss[:, :, 1], ALU.add))
            nc.vector.tensor_scalar(rs[:], rs[:], 1.0 / D, EPS, ALU.mult, ALU.add).then_inc(meaned, 1)
            dve.wait_ge(rooted, 1)
            dve.wait_ge(copied, 2 * NT)
            for t in range(NT):
                last = nc.vector.scalar_tensor_tensor(f[:, t], f[:, t], rs[:, t:t + 1], gain_b, ALU.mult, ALU.mult)
                if t == NT - 1:
                    c.vlink(dve, last)
            for t in range(NT):
                nc.vector.tensor_tensor(c.x[:, t], c.x[:, t], f[:, t], ALU.add)
NEG = -1e30
A_HEADS, A_W = 12, 768
KA = A_W // P
B_HEADS = 16
DH = 64
FF = 2816
KF = FF // P
FT = 256


def attention(c, units):
    nc = c.nc
    U = len(units)
    with ExitStack() as s:
        pr = c.sb(s, "probs", [P, 3, SEQ])
        prT = c.sb(s, "probsT", [P, 2, NT, P])
        nm = c.sb(s, "minus_max", [P, 3])
        scored = c.sem("at_scored")
        maxed = c.sem("at_maxed")
        biased = c.sem("at_biased")
        expd = c.sem("at_exp")
        turned = c.sem("at_turned")
        copied = c.sem("at_copied")
        summed = c.sem("at_summed")
        left = c.sem("at_left")
        block = s.enter_context(nc.Block())

        def scores(i):
            return c.ps[:, (0, 1, 6)[i % 3]]

        @block.tensor
        def _(pe):
            for i in range(U + 3):
                if i < U:
                    u = units[i]
                    W = u["W"]
                    if i >= 3:
                        pe.wait_ge(expd, i - 2)
                    adds = u["adds"]
                    last = nc.tensor.matmul(scores(i)[:, 0:W], u["q"], u["k"], start=True, stop=not adds)
                    for n, (lhs, rhs, c0) in enumerate(adds):
                        last = nc.tensor.matmul(scores(i)[:, c0:W], lhs, rhs, start=False, stop=n == len(adds) - 1)
                    last.then_inc(scored, 1)
                if 0 <= i - 2 < U:
                    j = i - 2
                    pe.wait_ge(expd, j + 1)
                    if j >= 2:
                        pe.wait_ge(copied, j - 1)
                    for b in range(units[j]["W"] // P):
                        last = nc.tensor.transpose(c.ps[:, 2 + j % 2, b * P:(b + 1) * P], pr[:, j % 3, b * P:(b + 1) * P],
                                                   c.ident[:])
                    last.then_inc(turned, 1)
                if 0 <= i - 3 < U:
                    j = i - 3
                    u = units[j]
                    pe.wait_ge(copied, j + 1)
                    if j >= 2:
                        pe.wait_ge(left, j - 1)
                    nb = u["W"] // P
                    for b in range(nb):
                        last = nc.tensor.matmul(c.ps[:, 4 + j % 2, 0:DH], prT[:, j % 2, b], u["v"][b],
                                                start=b == 0, stop=b == nb - 1)
                    last.then_inc(summed, 1)

        @block.scalar
        def _(act):
            for i in range(U):
                u = units[i]
                act.wait_ge(biased, i + 1)
                if i >= 3:
                    act.wait_ge(turned, i - 2)
                nc.scalar.activation(pr[:, i % 3, 0:u["W"]], scores(i)[:, 0:u["W"]], ACT.Exp, bias=nm[:, i % 3:i % 3 + 1],
                                     scale=DH ** -0.5, accum_out=u["l"]).then_inc(expd, 1)

        @block.vector
        def _(dve):
            for i in range(U + 3):
                if i < U:
                    u = units[i]
                    dve.wait_ge(scored, i + 1)
                    nc.vector.reduce_max(u["m"], scores(i)[:, 0:u["W"]], AX).then_inc(maxed, 1)
                    dve.wait_ge(maxed, i + 1)
                    if i >= 3:
                        dve.wait_ge(expd, i - 2)
                    nc.vector.tensor_scalar(nm[:, i % 3:i % 3 + 1], u["m"], -DH ** -0.5, None, ALU.mult).then_inc(biased, 1)
                if 0 <= i - 2 < U:
                    j = i - 2
                    u = units[j]
                    dve.wait_ge(turned, j + 1)
                    if j >= 2:
                        dve.wait_ge(summed, j - 1)
                    nc.vector.tensor_copy(prT[:, j % 2, 0:u["W"] // P], c.ps[:, 2 + j % 2, 0:u["W"]]).then_inc(copied, 1)
                if 0 <= i - 3 < U:
                    j = i - 3
                    dve.wait_ge(summed, j + 1)
                    nc.vector.tensor_copy(units[j]["out"], c.ps[:, 4 + j % 2, 0:DH]).then_inc(left, 1)


def project_heads(c, jobs, src, ahead=None, given=None, spare=(), scratch=None):
    nc = c.nc
    works = [(n, w) for n, (_, ws) in enumerate(jobs) for w in ws]
    ropes = [w for _, w in works if w["rope"]]
    place = [sum(bool(v["rope"]) == bool(w["rope"]) for _, v in works[:i]) for i, (_, w) in enumerate(works)]
    first_of = [sum(len(v) for _, v in jobs[:n]) for n in range(len(jobs))]
    with ExitStack() as s:
        parts = given or (c.sb(s, "src_high", [P, KD, SEQ], F32R), c.sb(s, "src_low", [P, KD, SEQ], F32R))
        pieces = range(0) if given else range(2)
        c.split.buffers(c, s, spare)
        src_high = c.sem("ps_src_high")
        src_low = c.sem("ps_src_low")
        if ropes:
            scratch = c.sb(s, "rope_scratch", [P, 3, GW]) if scratch is None else scratch
            raw = scratch[:, 0:2]
            turn = scratch[:, 2]
        done = c.sem("ph_done")
        left = c.sem("ph_left")
        rawed = c.sem("ph_raw")
        rotd = c.sem("ph_rotated")
        roped = c.sem("ph_roped")
        mixed = c.sem("ph_mixed")
        block = s.enter_context(nc.Block())

        @block.sync
        def _(sp):
            c.split.load(sp, [tile for tile, _ in jobs])
            if ahead:
                c.split.ahead(sp, ahead)

        @block.tensor
        def _(pe):
            def rotate(r):
                pe.wait_ge(rawed, r + 1)
                w = ropes[r]
                if r >= 2:
                    pe.wait_ge(mixed, r - 1)
                nc.tensor.matmul(c.ps[:, 4 + r % 2, 0:w["n"]], w["rope"][2], raw[:, r % 2, 0:w["n"]],
                                 start=True, stop=True).then_inc(rotd, 1)

            i, r = 0, 0
            pending = None
            if pieces:
                pe.wait_ge(src_low, 2)
            for _, ws in jobs:
                slot = c.split.take(pe)
                for w in ws:
                    if i >= 4:
                        pe.wait_ge(rawed if works[i - 4][1]["rope"] else left, place[i - 4] + 1)
                    for k in range(KD):
                        last = mm3(c, c.ps[0:w["m"], i % 4, 0:w["n"]], [w["lhs"](slot[x], parts[x], k) for x in range(2)],
                                   [w["rhs"](slot[x], parts[x], k) for x in range(2)], k == 0, k == KD - 1)
                    last.then_inc(done, 1)
                    if pending is not None:
                        rotate(pending)
                        pending = None
                    if w["rope"]:
                        pending = r
                        r += 1
                    i += 1
            if pending is not None:
                rotate(pending)

        @block.scalar
        def _(act):
            for x in pieces:
                nc.scalar.activation(parts[0][:, 4 * x:4 * x + 4], src[:, 4 * x:4 * x + 4], ACT.Copy).then_inc(src_high, 1)
            c.split.high(c, act)
            r = 0
            for i, (job, w) in enumerate(works):
                if i == first_of[job] and job + 1 < len(jobs):
                    c.split.high(c, act)
                act.wait_ge(done, i + 1)
                n = w["n"]
                bank = c.ps[0:w["m"], i % 4, 0:n]
                if w["rope"]:
                    if r >= 2:
                        act.wait_ge(roped, r - 1)
                    nc.scalar.activation(raw[:, r % 2, 0:n], bank, ACT.Copy).then_inc(rawed, 1)
                    r += 1
                else:
                    nc.scalar.activation(w["out"], bank, ACT.Copy).then_inc(left, 1)

        @block.vector
        def _(dve):
            for x in pieces:
                dve.wait_ge(src_high, x + 1)
                nc.vector.tensor_tensor(parts[1][:, 4 * x:4 * x + 4], src[:, 4 * x:4 * x + 4], parts[0][:, 4 * x:4 * x + 4].bitcast(F32), ALU.subtract).then_inc(src_low, 1)
            c.split.low(c, dve)
            r = -1
            for i, (job, w) in enumerate(works):
                if i == first_of[job] and job + 1 < len(jobs):
                    c.split.low(c, dve)
                if not w["rope"]:
                    continue
                r += 1
                n = w["n"]
                cos, sin, _ = w["rope"]
                dve.wait_ge(rotd, r + 1)
                if r:
                    dve.wait_ge(roped, r)
                nc.vector.tensor_tensor(turn[:, 0:n], c.ps[:, 4 + r % 2, 0:n], sin, ALU.mult).then_inc(mixed, 1)
                c.vlink(dve, nc.vector.tensor_tensor(w["out"], raw[:, r % 2, 0:n], cos, ALU.mult))
                dve.wait_ge(mixed, r + 1)
                nc.vector.tensor_tensor(w["out"], w["out"], turn[:, 0:n], ALU.add).then_inc(roped, 1)


def up_tiles(w_up):
    return [[(KD, P, cols(w_up, f * P, P)), (KD, P, cols(w_up, FF + f * P, P))] for f in range(KF)]


def ffn_up(c, w_up, conv, bias, gT, parts, ahead):
    nc = c.nc
    with ExitStack() as s:
        c.split.buffers(c, s)
        a = c.sb(s, "convolved", [P, 2, 2, SEQ])
        g = c.sb(s, "gelu", [P, 2, SEQ])
        src_high = c.sem("up_src_high")
        src_low = c.sem("up_src_low")
        done = c.sem("up_done")
        begun = c.sem("up_begun")
        middle = c.sem("up_middle")
        convd = c.sem("up_convd")
        gelud = c.sem("up_gelu")
        multd = c.sem("up_multiplied")
        block = s.enter_context(nc.Block())

        @block.sync
        def _(sp):
            c.split.load(sp, up_tiles(w_up))
            c.split.ahead(sp, ahead)

        @block.tensor
        def _(pe):
            pe.wait_ge(src_low, 2)
            for f in range(KF):
                w = [x[:].rearrange("p (k v n) -> p k v n", v=2, k=KD) for x in c.split.take(pe)]
                if f >= 4:
                    pe.wait_ge(convd, 2 * (f - 3))
                for v in range(2):
                    for k in range(KD):
                        last = mm3(c, c.ps[:, 2 * (f % 4) + v], (w[0][:, k, v], w[1][:, k, v]), (parts[0][:, k], parts[1][:, k]), k == 0, k == KD - 1)
                    last.then_inc(done, 1)

        @block.scalar
        def _(act):
            for x in range(2):
                nc.scalar.activation(parts[0][:, 4 * x:4 * x + 4], c.hT[:, 4 * x:4 * x + 4], ACT.Copy).then_inc(src_high, 1)
            c.split.high(c, act)
            for f in range(KF + 1):
                if f + 1 < KF:
                    c.split.high(c, act)
                if f < KF:
                    for v in range(2):
                        act.wait_ge(done, 2 * f + v + 1)
                        if f >= 2:
                            act.wait_ge(multd, f - 1)
                        ch = v * KF + f
                        nc.scalar.activation(a[:, f % 2, v], c.ps[:, 2 * (f % 4) + v], ACT.Identity, scale=conv[:, 2, ch:ch + 1],
                                             bias=bias[:, ch:ch + 1]).then_inc(begun, 1)
                if f:
                    u = f - 1
                    act.wait_ge(convd, 2 * u + 2)
                    nc.scalar.activation(g[:, u % 2], a[:, u % 2, 0], ACT.Gelu_apprx_tanh).then_inc(gelud, 1)

        @block.vector
        def _(dve):
            for x in range(2):
                dve.wait_ge(src_high, x + 1)
                nc.vector.tensor_tensor(parts[1][:, 4 * x:4 * x + 4], c.hT[:, 4 * x:4 * x + 4], parts[0][:, 4 * x:4 * x + 4].bitcast(F32), ALU.subtract).then_inc(src_low, 1)
            c.split.low(c, dve)
            for f in range(KF + 1):
                if f + 1 < KF:
                    c.split.low(c, dve)
                if f < KF:
                    for v in range(2):
                        ch = v * KF + f
                        dve.wait_ge(begun, 2 * f + v + 1)
                        nc.vector.scalar_tensor_tensor(a[:, f % 2, v, 1:], c.ps[:, 2 * (f % 4) + v, 0:SEQ - 1], conv[:, 1, ch:ch + 1],
                                                       a[:, f % 2, v, 1:], ALU.mult, ALU.add).then_inc(middle, 1)
                    for v in range(2):
                        ch = v * KF + f
                        dve.wait_ge(middle, 2 * f + v + 1)
                        nc.vector.scalar_tensor_tensor(a[:, f % 2, v, 2:], c.ps[:, 2 * (f % 4) + v, 0:SEQ - 2], conv[:, 0, ch:ch + 1],
                                                       a[:, f % 2, v, 2:], ALU.mult, ALU.add).then_inc(convd, 1)
                if f:
                    u = f - 1
                    dve.wait_ge(gelud, u + 1)
                    dve.wait_ge(convd, 2 * u + 2)
                    nc.vector.tensor_tensor(gT[:, u], g[:, u % 2], a[:, u % 2, 1], ALU.mult).then_inc(multd, 1)


def block2(c):
    nc, t = c.nc, c.t
    gains = t["norm_gains_2"]
    with ExitStack() as s2:
        gcol = c.sb(s2, "gain_columns", [P, 5, KD])
        got = c.sem("constants_landed")
        with ExitStack() as s:
            block = s.enter_context(nc.Block())

            @block.sync
            def _(sp):
                n = 0
                for l in range(2):
                    for i in range(2):
                        sp.dma_start(gcol[:, 2 * l + i], gains[l, 2 * i].rearrange("(k p) -> p k", p=P), allow_slow_non_contiguous=True).then_inc(got, 16)
                        n += 1
                sp.dma_start(gcol[:, 4], t["kv_norm_2"].rearrange("(k p) -> p k", p=P), allow_slow_non_contiguous=True).then_inc(got, 16)
                sp.wait_ge(got, 16 * (n + 1))

        def gain_rows(sp, l):
            landed = c.sem("gain_rows_landed")
            for i in range(2):
                sp.dma_start(c.gate[:, i], gains[l, 2 * i + 1:2 * i + 2].to_broadcast([P, D])).then_inc(landed, 16)
            sp.wait_ge(landed, 32)

        def col(i):
            return lambda k: gcol[:, i, k:k + 1]

        def plain(k, tile):
            return c.hT[:, k, tile * P:(tile + 1) * P]

        def ffn(l):
            with ExitStack() as s:
                gT = c.sb(s, "gated", [P, KF, SEQ])
                conv = c.sb(s, "taps", [P, 3, 2 * KF])
                bias = c.sb(s, "conv_bias", [P, 2 * KF])
                landed = c.sem("taps_landed")

                def ahead(sp):
                    for j in range(3):
                        sp.dma_start(conv[:, j], t["conv_w_2"][l, j].rearrange("(k p) -> p k", p=P), allow_slow_non_contiguous=True).then_inc(landed, 16)
                    sp.dma_start(bias[:], t["conv_b_2"][l].rearrange("(k p) -> p k", p=P), allow_slow_non_contiguous=True).then_inc(landed, 16)
                    c.split.ahead(sp, up_tiles(t["w_up_2"][l]))
                    sp.wait_ge(landed, 64)

                norm_transpose(c, c.x, NT, [(plain, col(2 * l + 1), None)], ahead=ahead)
                pair = (c.sb(s, "high_parts", [P, KD, SEQ], F32R), c.sb(s, "low_parts", [P, KD, SEQ], F32R))
                ffn_up(c, t["w_up_2"][l], conv, bias, gT, pair, residual_tiles(t["w_down_2"][l], KF))
                project_residual(c, t["w_down_2"][l], KF, gT, c.gate[:, 1], pair)

        with ExitStack() as s:
            o = c.sb(s, "heads_out", [P, NT, A_W])
            with ExitStack() as sa:
                qT = c.sb(sa, "qT", [P, KA, SEQ])
                kT = c.sb(sa, "kT", [P, KA, SEQ])
                v = c.sb(sa, "v", [P, NT, A_W])
                rope = c.sb(sa, "rope", [P, 2, SEQ])
                rot = c.sb(sa, "rotation", [P, P])
                band = c.sb(sa, "band", [P, NT, SEQ])
                diag = c.sb(sa, "diagonal_masks", [P, 2, P])
                m = c.sb(sa, "maxima", [P, NT, A_HEADS])
                l = c.sb(sa, "sums", [P, NT, A_HEADS])
                landed = c.sem("masks_landed")
                def ahead(sp):
                    c.split.ahead(sp, [[(KD, FT, cols(t["w_qkv_a_2"][0], n * FT, FT))] for n in range(RAW_SLOTS)])
                    sp.dma_start(rope[:], t["rope2"].rearrange("a p n -> p a n")).then_inc(landed, 16)
                    sp.dma_start(rot[:], t["rot2"]).then_inc(landed, 16)
                    sp.dma_start(band[:], t["band"].rearrange("a p n -> p a n")).then_inc(landed, 16)
                    sp.dma_start(diag[:], t["diag"].rearrange("a p n -> p a n")).then_inc(landed, 16)
                    gain_rows(sp, 0)
                    sp.wait_ge(landed, 64)

                norm_transpose(c, c.x, NT, [(lambda k, tile: c.hT[:, k].rearrange("p (c u) -> p u c", c=4)[:, 32 * tile:32 * tile + 32, :],
                                             col(0), None)], order=lambda a: a.rearrange("p (u c) -> p u c", c=4), ahead=ahead)
                jobs = []
                for dst, off in ((qT, 0), (kT, A_W)):
                    for n in range(3):
                        jobs.append(([(KD, FT, cols(t["w_qkv_a_2"][0], off + n * FT, FT))],
                                     [dict(m=P, n=SEQ, out=dst[:, 2 * n + f], rope=(rope[:, 0], rope[:, 1], rot[:]),
                                           lhs=lambda w, h, k, f=f: w[:, k * FT + f * P:k * FT + (f + 1) * P],
                                           rhs=lambda w, h, k: h[:, k]) for f in range(2)]))
                for n in range(3):
                    jobs.append(([(KD, FT, cols(t["w_qkv_a_2"][0], 2 * A_W + n * FT, FT))],
                                 [dict(m=P, n=FT, out=v[:, tile, n * FT:(n + 1) * FT], rope=None,
                                       lhs=lambda w, h, k, tile=tile: h[:, k, tile * P:(tile + 1) * P],
                                       rhs=lambda w, h, k: w[:, k * FT:(k + 1) * FT]) for tile in range(NT)]))
                project_heads(c, jobs, c.hT)
                units = []
                for cc in range(4):
                    for h in range(A_HEADS):
                        p0 = DH * (h % 2)
                        g = h // 4
                        keys = slice(0, SEQ) if g == 0 else slice(cc * P, (cc + 1) * P)
                        units.append(dict(
                            W=SEQ if g == 0 else P, q=qT[p0:p0 + DH, h // 2, cc * P:(cc + 1) * P], k=kT[p0:p0 + DH, h // 2, keys],
                            adds=[(c.ident[:], band[:, cc] if g == 0 else diag[:, g - 1], 0)],
                            v=[v[:, b, h * DH:(h + 1) * DH] for b in (range(NT) if g == 0 else [cc])],
                            out=o[:, cc, h * DH:(h + 1) * DH], m=m[:, cc, h:h + 1], l=l[:, cc, h:h + 1]))
                attention(c, units)
                with ExitStack() as b:
                    lse = c.sb(b, "lse", [P, NT, A_HEADS])
                    top = c.sb(b, "top", [P, NT, 4])
                    ready = c.sem("alpha_ready")
                    block = b.enter_context(nc.Block())

                    @block.scalar
                    def _(act):
                        nc.scalar.activation(lse[:], l[:], ACT.Ln).then_inc(ready, 1)
                        act.wait_ge(ready, 2)
                        nc.scalar.activation(lse[:], lse[:], ACT.Exp).then_inc(ready, 1)

                    @block.vector
                    def _(dve):
                        g = lambda i: lse[:, :, 4 * i:4 * i + 4]
                        L = lambda ins: c.vlink(dve, ins)
                        dve.wait_ge(ready, 1)
                        L(nc.vector.scalar_tensor_tensor(lse[:], m[:], DH ** -0.5, lse[:], ALU.mult, ALU.add))
                        L(nc.vector.tensor_tensor(top[:], g(0), g(1), ALU.max))
                        L(nc.vector.tensor_tensor(top[:], top[:], g(2), ALU.max))
                        L(nc.vector.tensor_tensor(g(0), g(0), top[:], ALU.subtract))
                        L(nc.vector.tensor_tensor(g(1), g(1), top[:], ALU.subtract))
                        nc.vector.tensor_tensor(g(2), g(2), top[:], ALU.subtract).then_inc(ready, 1)
                        dve.wait_ge(ready, 3)
                        L(nc.vector.tensor_tensor(top[:], g(0), g(1), ALU.add))
                        L(nc.vector.tensor_tensor(top[:], top[:], g(2), ALU.add))
                        L(nc.vector.reciprocal(top[:], top[:]))
                        L(nc.vector.reciprocal(l[:], l[:]))
                        for i in range(3):
                            L(nc.vector.tensor_tensor(g(i), g(i), top[:], ALU.mult))
                        L(nc.vector.tensor_tensor(lse[:], lse[:], l[:], ALU.mult))
                        for cc in range(4):
                            oc = o[:, cc].rearrange("p (h d) -> p h d", d=DH)
                            nc.vector.tensor_tensor(oc, oc, lse[:, cc].unsqueeze(2).to_broadcast([P, A_HEADS, DH]), ALU.mult)
            oT = c.sb(s, "oT", [P, KA, SEQ])
            plain_transpose(c, lambda tile: o[:, tile], NT, KA,
                            lambda k, cc: oT[:, k].rearrange("p (u c) -> p u c", c=4)[:, :, cc], None,
                            ahead=residual_tiles(t["w_o_a_2"][0], KA))
            project_residual(c, t["w_o_a_2"][0], KA, oT, c.gate[:, 0])
        ffn(0)

        with ExitStack() as s:
            o = c.sb(s, "heads_out", [P, NT, D])
            with ExitStack() as sa:
                hk = o[:].rearrange("p t d -> p (t d)").rearrange("p (k n) -> p k n", n=SEQ)

                def ahead(sp):
                    c.split.ahead(sp, [[(KD, FT, cols(t["w_q_b_2"][0], n * FT, FT))] for n in range(D // FT)])
                    gain_rows(sp, 1)

                norm_transpose(c, c.x, NT, [(plain, col(2), None),
                                            (lambda k, tile: hk[:, k, tile * P:(tile + 1) * P], col(4), None)],
                               ahead=ahead)
                qT = c.sb(sa, "qT", [P, KD, SEQ])
                kT = c.sb(sa, "kT", [P, KD, SEQ])
                v = c.sb(sa, "v", [P, NT, D])
                lf = c.sb(sa, "log_forget", [P, NT, B_HEADS])
                landed = c.sem("fox_landed")

                def features(w, c0, dst):
                    return [([(KD, FT, cols(w, c0 + n * FT, FT))],
                             [dict(m=P, n=SEQ, out=dst[:, 2 * n + f], rope=None,
                                   lhs=lambda w, h, k, f=f: w[:, k * FT + f * P:k * FT + (f + 1) * P],
                                   rhs=lambda w, h, k: h[:, k]) for f in range(2)]) for n in range(D // FT)]

                def tokens(w, c0, width, out):
                    return ([(KD, width, cols(w, c0, width))],
                            [dict(m=P, n=width, out=out(tile), rope=None,
                                  lhs=lambda w, h, k, tile=tile: h[:, k, tile * P:(tile + 1) * P],
                                  rhs=lambda w, h, k: w[:, k * width:(k + 1) * width]) for tile in range(NT)])

                kvf = t["w_kvf_2"]
                kvf_jobs = (features(kvf, 0, kT) +
                                    [tokens(kvf, D + n * FT, FT, lambda tile, n=n: v[:, tile, n * FT:(n + 1) * FT]) for n in range(D // FT)] +
                                    [tokens(kvf, 2 * D, B_HEADS, lambda tile: lf[:, tile])])
                project_heads(c, features(t["w_q_b_2"][0], 0, qT), c.hT, ahead=[tile for tile, _ in kvf_jobs])
                project_heads(c, kvf_jobs, hk)
                cT = c.sb(sa, "cumulated", [B_HEADS, SEQ])
                m = c.sb(sa, "maxima", [P, NT, B_HEADS])
                l = c.sb(sa, "sums", [P, NT, B_HEADS])
                tri = c.sb(sa, "triangles", [P, 3, P])
                pick = c.sb(sa, "minus_head", [B_HEADS, B_HEADS, P])
                bf = c.sb(sa, "forget_bias", [P, B_HEADS])
                with ExitStack() as b:
                    z = c.sb(b, "z", [P, NT, B_HEADS])
                    e = c.sb(b, "e", [P, NT, B_HEADS])
                    ready = c.sem("forget_ready")
                    summed = c.sem("forget_summed")
                    block = b.enter_context(nc.Block())

                    @block.sync
                    def _(sp):
                        sp.dma_start(tri[:, 0], t["tri"][0]).then_inc(landed, 16)
                        sp.dma_start(tri[:, 1], t["tri"][4]).then_inc(landed, 16)
                        sp.dma_start(tri[:, 2], t["causal"]).then_inc(landed, 16)
                        sp.dma_start(pick[:], t["pick"]).then_inc(landed, 16)
                        sp.dma_start(bf[:], t["b_f_2"].unsqueeze(0).to_broadcast([P, B_HEADS])).then_inc(landed, 16)
                        sp.wait_ge(landed, 80)

                    @block.scalar
                    def _(act):
                        act.wait_ge(ready, 1)
                        nc.scalar.activation(e[:], e[:], ACT.Exp, scale=-1.0).then_inc(ready, 1)
                        act.wait_ge(ready, 2)
                        nc.scalar.activation(e[:], e[:], ACT.Ln, bias=1.0).then_inc(ready, 1)

                    @block.vector
                    def _(dve):
                        L = lambda ins: c.vlink(dve, ins)
                        dve.wait_ge(landed, 80)
                        L(nc.vector.tensor_tensor(z[:], lf[:], bf[:].unsqueeze(1).to_broadcast([P, NT, B_HEADS]), ALU.add))
                        nc.vector.scalar_tensor_tensor(e[:], z[:], -1.0, z[:], ALU.mult, ALU.max).then_inc(ready, 1)
                        dve.wait_ge(ready, 3)
                        nc.vector.scalar_tensor_tensor(lf[:], z[:], 0.0, e[:], ALU.min, ALU.subtract).then_inc(ready, 1)
                        dve.wait_ge(summed, 1)
                        nc.vector.tensor_copy(cT[:], c.ps[0:B_HEADS, 0])

                    @block.tensor
                    def _(pe):
                        pe.wait_ge(ready, 4)
                        for i in range(NT):
                            for j in range(i + 1):
                                last = nc.tensor.matmul(c.ps[0:B_HEADS, 0, i * P:(i + 1) * P], lf[:, j], tri[:, 0 if j == i else 1],
                                                        start=j == 0, stop=j == i)
                        last.then_inc(summed, 1)
                units = []
                for i in range(NT):
                    for h in range(B_HEADS):
                        p0 = DH * (h % 2)
                        W = (i + 1) * P
                        units.append(dict(
                            W=W, q=qT[p0:p0 + DH, h // 2, i * P:(i + 1) * P], k=kT[p0:p0 + DH, h // 2, 0:W],
                            adds=[(pick[:, h], cT[:, 0:W], 0), (c.ident[:], tri[:, 2], i * P)],
                            v=[v[:, b, h * DH:(h + 1) * DH] for b in range(i + 1)],
                            out=o[:, i, h * DH:(h + 1) * DH], m=m[:, i, h:h + 1], l=l[:, i, h:h + 1]))
                attention(c, units)
                with ExitStack() as b:
                    block = b.enter_context(nc.Block())

                    @block.vector
                    def _(dve):
                        c.vlink(dve, nc.vector.reciprocal(l[:], l[:]))
                        for i in range(NT):
                            oi = o[:, i].rearrange("p (h d) -> p h d", d=DH)
                            nc.vector.tensor_tensor(oi, oi, l[:, i].unsqueeze(2).to_broadcast([P, B_HEADS, DH]), ALU.mult)
            oT = c.sb(s, "oT", [P, KD, SEQ])
            plain_transpose(c, lambda tile: o[:, tile], NT, KD, lambda k, tile: oT[:, k, tile * P:(tile + 1) * P], None,
                            ahead=residual_tiles(t["w_o_b_2"][0], KD))
            project_residual(c, t["w_o_b_2"][0], KD, oT, c.gate[:, 0])
        ffn(1)


def constants():
    i = np.arange(P)
    out = {"ident": np.eye(P)}
    le = i[:, None] <= i[None, :]
    out["tri"] = np.stack([le, i[:, None] > i[None, :], i[:, None] >= i[None, :], i[:, None] < i[None, :], le | True])
    out["causal"] = np.where(i[:, None] >= i[None, :], 0.0, NEG)
    tok = np.concatenate([np.arange(SEQ)[r::4] for r in range(4)])
    rel = tok[:, None] - tok[None, :]
    out["band"] = np.where((rel >= 0) & (rel <= 128), 0.0, NEG).reshape(NT, P, SEQ)
    causal = i[:, None] >= i[None, :]
    out["diag"] = np.stack([np.where(causal, 0.0, NEG), np.where(causal & (i[:, None] % 4 == i[None, :] % 4), 0.0, NEG)])
    pick = np.zeros((B_HEADS, B_HEADS, P))
    pick[np.arange(B_HEADS), np.arange(B_HEADS)] = -(DH ** 0.5)
    out["pick"] = pick
    rd = DH // 4
    half = rd // 2
    inv = np.float32(500000.0) ** (-np.arange(0, rd, 2, dtype=np.float32) / np.float32(rd))
    ang = tok.astype(np.float32)[None, :] * inv[:, None]
    cos, sin = np.ones((DH, SEQ), np.float32), np.zeros((DH, SEQ), np.float32)
    cos[:rd] = np.tile(np.cos(ang), (2, 1))
    sin[:rd] = np.tile(np.sin(ang), (2, 1))
    out["rope2"] = np.stack([np.tile(cos, (2, 1)), np.tile(sin, (2, 1))])
    rot = np.zeros((P, P))
    for base in (0, DH):
        for d in range(half):
            rot[base + half + d, base + d] = -1.0
            rot[base + d, base + half + d] = 1.0
    out["rot2"] = rot
    dh1, ax = 64, 32
    inv = np.float32(10000.0) ** (-np.arange(0, ax, 2, dtype=np.float32) / np.float32(ax))
    row = (np.arange(SEQ) // 64).astype(np.float32)
    colm = (np.arange(SEQ) % 64).astype(np.float32)
    ang = np.concatenate([inv[:, None] * row, inv[:, None] * colm], 0)
    ang = np.concatenate([ang, ang], 0)
    out["rope1"] = np.stack([np.tile(np.cos(ang), (2, 1)), np.tile(np.sin(ang), (2, 1))])
    rot = np.zeros((P, P))
    for base in (0, 64):
        for d in range(32):
            rot[base + 32 + d, base + d] = -1.0
            rot[base + d, base + 32 + d] = 1.0
    out["rot1"] = rot
    return {k: np.ascontiguousarray(v, dtype=np.float32) for k, v in out.items()}
Q0, K0, V0, Z0, XBC0, DT0, G0 = 0, 1024, 2048, 3072, 4096, 6144, 6176
LAM_INIT = 0.2
FT2 = 256
SSD_H, SSD_G, SSD_P = 16, 4, 64
TC = NC + NT


def block1_mixer(c):
    nc, t = c.nc, c.t
    w_in = t["w_in"][0]
    with ExitStack() as s1:
        hcT = c.sb(s1, "hc_high", [P, KD, CTX], F32R)
        low = c.sb(s1, "h_low", [P, KD, SEQ])
        lowc = c.sb(s1, "hc_low", [P, KD, CTX])
        lam = c.sb(s1, "minus_lambda", [P, 1])
        modulation(c, s1, low, lowc, lam)
        h = (c.rounded(c.hT), c.rounded(low))
        hc = (hcT, c.rounded(lowc))
        split_stage(c, halves(h, low) + halves(hc, lowc))
        yT = c.sb(s1, "yT", [P, KD, SEQ])
        with ExitStack() as s:
            xt = c.sb(s, "x_ssd", [P, TC, D])
            with ExitStack() as st:
                ssd(c, st, w_in, h, hc, xt, yT)
            gate_y(c, w_in, h, xt, yT)
        oT = c.sb(s1, "oT", [P, KD, SEQ])
        diff_attention(c, w_in, h, hc, lam, oT)
        merge(c, w_in, h, yT, oT, [a[:].rearrange("p k n -> p (k n)") for a in hc])


def modulation(c, s1, hT, hcT, lam):
    nc, t = c.nc, c.t
    b_ada = t["b_ada"]
    SHIFT1, SCALE1, SHIFT2, SCALE2 = range(4)
    with ExitStack() as s:
        cc = c.sb(s, "conditions", [P, KD, 2])
        cb = c.sb(s, "condition_wide", [P, KD, P])
        brow = c.sb(s, "bias_rows", [2, 4, D])
        mrow = c.sb(s, "mod_rows", [2, 4, D])
        mcol = c.sb(s, "mod_columns", [P, 4, KD, 2])
        gcol = c.sb(s, "gain_columns", [P, 2, KD])
        prow = c.sb(s, "post_rows", [P, 2, D])
        lv = c.sb(s, "lambda_rows", [P, 4, 64])
        lp = c.sb(s, "lambda_products", [P, 2, 64])
        le = c.sb(s, "lambda_sums", [P, 2])
        ctx_tok = c.sb(s, "context", [P, NC, D])
        cond_landed = c.sem("conditions_landed")
        landed = c.sem("ada_landed")
        silud = c.sem("ada_silu")
        wide = c.sem("ada_wide")
        done = c.sem("ada_done")
        left = c.sem("ada_left")
        turned = c.sem("ada_turned")
        lamd = c.sem("lambda_steps")
        LOADS = 2 + 4 + 2 + 2 + 4 + 1
        with ExitStack() as b:
            block = b.enter_context(nc.Block())

            @block.sync
            def _(sp):
                def load(dst, src, slow=False, sem=landed):
                    sp.dma_start(dst, src, allow_slow_non_contiguous=slow).then_inc(sem, 16)
                weights = [whole(cols(t["w_ada"][0], n * GW)) for n in range(12)]
                load(cc[:, :, 0], t["c"][0].rearrange("(k p) -> p k", p=P), True, cond_landed)
                load(cc[:, :, 1], t["c_ctx"].rearrange("(k p) -> p k", p=P), True, cond_landed)
                load_weights(c, sp, weights[:SLOTS])
                for i, kind in enumerate((2, 5)):
                    load(c.gate[:, i], b_ada[:, kind * D:(kind + 1) * D].to_broadcast([P, D]))
                for i, kind in enumerate((0, 1, 3, 4)):
                    load(brow[:, i], b_ada[:, kind * D:(kind + 1) * D].to_broadcast([2, D]))
                load(gcol[:, 0], t["g_pre_mix"][0].rearrange("(k p) -> p k", p=P), True)
                load(gcol[:, 1], t["g_pre_ffn"][0].rearrange("(k p) -> p k", p=P), True)
                load(prow[:, 0], t["g_post_mix"].to_broadcast([P, D]))
                load(prow[:, 1], t["g_post_ffn"].to_broadcast([P, D]))
                for i, name in enumerate(("lam_q1", "lam_k1", "lam_q2", "lam_k2")):
                    load(lv[:, i], t[name].to_broadcast([P, 64]))
                load(ctx_tok[:], t["ctx"][0].rearrange("(t p) d -> p t d", p=P))
                load_weights(c, sp, weights[SLOTS:])
                sp.wait_ge(landed, 16 * LOADS)

            @block.scalar
            def _(act):
                act.wait_ge(cond_landed, 32)
                nc.scalar.activation(cc[:], cc[:], ACT.Silu).then_inc(silud, 1)
                act.wait_ge(lamd, 2)
                nc.scalar.activation(le[:], le[:], ACT.Exp).then_inc(lamd, 1)

            @block.tensor
            def _(pe):
                pe.wait_ge(wide, 1)
                pe.wait_ge(silud, 1)
                for n in range(12):
                    w = take(c, pe, 1).rearrange("p (k n) -> p k n", n=GW)
                    gate = n // 2 in (2, 5)
                    if n >= 4:
                        pe.wait_ge(left, n - 3)
                    for k in range(KD):
                        out = c.ps[:, n % 4] if gate else c.ps[0:2, n % 4]
                        last = mm(c, out, cb[:, k] if gate else cc[:, k], w[:, k], k == 0, k == KD - 1)
                    last.then_inc(done, 1)
                pe.wait_ge(left, 12)
                for i in range(4):
                    for k in range(KD):
                        j = i * KD + k
                        last = nc.tensor.transpose(c.ps[:, 4, 2 * j:2 * j + 2], mrow[:, i, k * P:(k + 1) * P], c.ident[0:2, 0:2])
                last.then_inc(turned, 1)

            @block.vector
            def _(dve):
                dve.wait_ge(silud, 1)
                nc.vector.tensor_copy(cb[:], cc[:, :, 0:1].to_broadcast([P, KD, P])).then_inc(wide, 1)
                dve.wait_ge(landed, 16 * LOADS)
                c.vlink(dve, nc.vector.tensor_tensor(lp[:, 0], lv[:, 0], lv[:, 1], ALU.mult))
                c.vlink(dve, nc.vector.tensor_tensor(lp[:, 1], lv[:, 2], lv[:, 3], ALU.mult))
                nc.vector.reduce_sum(le[:, 0:1], lp[:, 0], AX).then_inc(lamd, 1)
                nc.vector.reduce_sum(le[:, 1:2], lp[:, 1], AX).then_inc(lamd, 1)
                dve.wait_ge(lamd, 3)
                c.vlink(dve, nc.vector.tensor_tensor(lam[:], le[:, 1:2], le[:, 0:1], ALU.subtract))
                c.vlink(dve, nc.vector.tensor_scalar(lam[:], lam[:], -LAM_INIT, None, ALU.add))
                kinds = (0, 1, None, 2, 3, None)
                for n in range(12):
                    i, hf = kinds[n // 2], slice((n % 2) * GW, (n % 2 + 1) * GW)
                    dve.wait_ge(done, n + 1)
                    if i is None:
                        g = c.gate[:, n // 6, hf]
                        c.vlink(dve, nc.vector.tensor_tensor(g, c.ps[:, n % 4], g, ALU.add))
                        nc.vector.tensor_tensor(g, g, prow[:, n // 6, hf], ALU.mult).then_inc(left, 1)
                    else:
                        nc.vector.tensor_tensor(mrow[:, i, hf], c.ps[0:2, n % 4], brow[:, i, hf], ALU.add).then_inc(left, 1)
                dve.wait_ge(turned, 1)
                c.vlink(dve, nc.vector.tensor_copy(mcol[:], c.ps[:, 4, 0:8 * KD]))
                for n, (kind, who, g) in enumerate(((SCALE1, 0, 0), (SCALE1, 1, 0), (SCALE2, 0, 1))):
                    nc.vector.scalar_tensor_tensor(mcol[:, kind, :, who], mcol[:, kind, :, who], 1.0, gcol[:, g], ALU.add, ALU.mult)
                c.vlink(dve, nc.vector.tensor_copy(c.shift2[:], mcol[:, SHIFT2, :, 0]))
                c.vlink(dve, nc.vector.tensor_copy(c.scale2[:], mcol[:, SCALE2, :, 0]))
        norm_transpose(c, c.x, NT, [(lambda k, tile: hT[:, k, tile * P:(tile + 1) * P],
                                     lambda k: mcol[:, SCALE1, k, 0:1], lambda k: mcol[:, SHIFT1, k, 0:1])])
        norm_transpose(c, ctx_tok, NC, [(lambda k, tile: hcT[:, k, tile * P:(tile + 1) * P],
                                         lambda k: mcol[:, SCALE1, k, 1:2], lambda k: mcol[:, SHIFT1, k, 1:2])])


def ssd(c, s0, w_in, h, hc, xt, yT):
    nc, t = c.nc, c.t
    HG = SSD_H // SSD_G
    GP = HG * SSD_P
    bT = c.sb(s0, "B_T", [P, SSD_G, CTX + SEQ])
    cT = c.sb(s0, "C_T", [P, SSD_G, SEQ])
    dt = c.sb(s0, "dt", [P, TC, 2 * SSD_H])
    da = c.sb(s0, "dt_a", [P, TC, 2 * SSD_H])
    tri = c.sb(s0, "triangles", [P, 5, P])
    LE, GT, GE, LT, ONES = range(5)
    ex = c.sb(s0, "decays", [P, TC, 6 * SSD_H])
    drow = c.sb(s0, "d_skip", [P, SSD_H])
    hs = [yT[:].rearrange("p k n -> p (k n)").rearrange("p (t d) -> p t d", d=D),
          c.sb(s0, "states_backward", [P, NT, D])]
    with ExitStack() as s:
        btok = c.sb(s, "B_tokens", [P, TC, SSD_G * P])
        with ExitStack() as b:
            taps = c.sb(b, "taps", [P, 3, 16])
            bias = c.sb(b, "conv_bias", [P, 16])
            arow = c.sb(b, "a_row", [P, 2 * SSD_H])
            dbias = c.sb(b, "dt_bias", [P, 2 * SSD_H])
            landed = c.sem("ssd_landed")
            with ExitStack() as bb:
                block = bb.enter_context(nc.Block())

                @block.sync
                def _(sp):
                    for j in range(3):
                        sp.dma_start(taps[:, j], t["conv_w"][0, j].rearrange("(k p) -> p k", p=P), allow_slow_non_contiguous=True).then_inc(landed, 16)
                    sp.dma_start(bias[:], t["conv_b"][0].rearrange("(k p) -> p k", p=P), allow_slow_non_contiguous=True).then_inc(landed, 16)
                    sp.dma_start(arow[:], t["a_log"].rearrange("a d h -> a (d h)").to_broadcast([P, 2 * SSD_H])).then_inc(landed, 16)
                    sp.dma_start(dbias[:], t["dt_bias"].rearrange("a d h -> a (d h)").to_broadcast([P, 2 * SSD_H])).then_inc(landed, 16)
                    sp.dma_start(tri[:], t["tri"].rearrange("a p n -> p a n")).then_inc(landed, 16)
                    sp.dma_start(drow[:], t["d_skip"].to_broadcast([P, SSD_H])).then_inc(landed, 16)
                    c.split.ahead(sp, conv_tiles(w_in))
                    sp.wait_ge(landed, 128)
            spare = c.rounded(hs[1])
            spare = [spare[:, n] for n in range(NT)]
            conv_project(c, w_in, h, hc, xt, bT, cT, btok, taps, bias, spare, yT[:].rearrange("p k n -> p (k n)"))
            with ExitStack() as bb:
                z = c.sb(bb, "z", [P, TC, 2 * SSD_H])
                raw = c.sb(bb, "dt_raw", [2 * SSD_H, CTX + SEQ])
                c.split.buffers(c, bb, spare)
                rawed = c.sem("dt_rawed")
                across = c.sem("dt_across")
                done = c.sem("dt_done")
                step = c.sem("dt_steps")
                summed = c.sem("dt_summed")
                block = bb.enter_context(nc.Block())

                @block.sync
                def _(sp):
                    c.split.load(sp, dt_tiles(w_in))

                @block.tensor
                def _(pe):
                    w = c.split.take(pe)
                    for bank, parts, n in ((3, hc, CTX), (4, h, SEQ)):
                        for k in range(KD):
                            last = mm3(c, c.ps[0:2 * SSD_H, bank, 0:n], [a[:, k * 32:(k + 1) * 32] for a in w], [a[:, k] for a in parts], k == 0, k == KD - 1)
                        last.then_inc(across, 1)
                    pe.wait_ge(rawed, 2)
                    for tile in range(TC):
                        last = nc.tensor.transpose(c.ps[:, 0, tile * 32:(tile + 1) * 32], raw[:, tile * P:(tile + 1) * P], c.ident[0:32, 0:32])
                    last.then_inc(done, 1)
                    pe.wait_ge(step, 5)
                    for tile in range(TC):
                        bank, at = 1 + tile // 3, (tile % 3) * 6 * SSD_H
                        for n, (m, c0, w) in enumerate(((LE, 0, 16), (GT, 0, 16), (GE, 16, 16), (LT, 16, 16), (ONES, 0, 32))):
                            last = nc.tensor.matmul(c.ps[:, bank, at + 16 * n:at + 16 * n + w], tri[:, m], da[:, tile, c0:c0 + w],
                                                    start=True, stop=True)
                    last.then_inc(summed, 1)

                @block.scalar
                def _(act):
                    c.split.high(c, act)
                    nc.scalar.activation(arow[:], arow[:], ACT.Exp).then_inc(step, 1)
                    for n, (bank, a, z) in enumerate(((3, 0, CTX), (4, CTX, CTX + SEQ))):
                        act.wait_ge(across, n + 1)
                        nc.scalar.activation(raw[:, a:z], c.ps[0:2 * SSD_H, bank, 0:z - a], ACT.Copy).then_inc(rawed, 1)
                    act.wait_ge(step, 2)
                    nc.scalar.activation(dt[:], dt[:], ACT.Exp, scale=-1.0).then_inc(step, 1)
                    act.wait_ge(step, 3)
                    nc.scalar.activation(dt[:], dt[:], ACT.Ln, bias=1.0).then_inc(step, 1)
                    act.wait_ge(summed, 1)
                    for n in range(2):
                        nc.scalar.activation(ex[:, 3 * n:3 * n + 3], c.ps[:, 1 + n, 0:18 * SSD_H], ACT.Exp)

                @block.vector
                def _(dve):
                    c.split.low(c, dve)
                    dve.wait_ge(done, 1)
                    dve.wait_ge(step, 1)
                    c.vlink(dve, nc.vector.tensor_tensor(z[:], c.ps[:, 0, 0:TC * 32].rearrange("p (t h) -> p t h", h=32),
                                                         dbias[:].unsqueeze(1).to_broadcast([P, TC, 32]), ALU.add))
                    nc.vector.scalar_tensor_tensor(dt[:], z[:], -1.0, z[:], ALU.mult, ALU.max).then_inc(step, 1)
                    dve.wait_ge(step, 4)
                    c.vlink(dve, nc.vector.scalar_tensor_tensor(dt[:], z[:], 0.0, dt[:], ALU.max, ALU.add))
                    c.vlink(dve, nc.vector.tensor_scalar(arow[:], arow[:], -1.0, None, ALU.mult))
                    nc.vector.tensor_tensor(da[:], dt[:], arow[:].unsqueeze(1).to_broadcast([P, TC, 32]), ALU.mult).then_inc(step, 1)

        with ExitStack() as b:
            wt = c.sb(b, "end_weights", [P, TC, 2 * SSD_H])
            xw = c.sb(b, "x_weighted", [P, 2, D])
            weighted = c.sem("st_weighted")
            outer = c.sem("st_outer")
            kept = c.sem("st_kept")
            block = b.enter_context(nc.Block())
            plan = []
            for n in range(5):
                plan.append((0, n, max(n - 1, 0), max(n - 2, 0) if n else None))
                plan.append((1, (1, 0, 5, 4, 3)[n], (3, 3, 2, 1, 0)[n], (None, 3, 3, 2, 1)[n]))

            @block.tensor
            def _(pe):
                for i, (d, ch, _, _) in enumerate(plan):
                    pe.wait_ge(weighted, i + 1)
                    if i >= 2:
                        pe.wait_ge(kept, i - 1)
                    for g in range(SSD_G):
                        last = nc.tensor.matmul(c.ps[:, 2 * (i % 2) + g // 2, (g % 2) * GP:(g % 2 + 1) * GP],
                                                btok[:, ch, g * P:(g + 1) * P], xw[:, i % 2, g * GP:(g + 1) * GP], start=True, stop=True)
                    last.then_inc(outer, 1)

            @block.vector
            def _(dve):
                L = lambda ins: c.vlink(dve, ins)
                nc.vector.tensor_tensor(wt[:, :, 0:16], dt[:, :, 0:16], ex[:, :, 16:32], ALU.mult)
                L(nc.vector.tensor_tensor(wt[:, :, 16:32], dt[:, :, 16:32], ex[:, :, 48:64], ALU.mult))

                def weigh(i):
                    d, ch, _, _ = plan[i]
                    if i >= 2:
                        dve.wait_ge(outer, i - 1)
                    nc.vector.tensor_tensor(xw[:, i % 2].rearrange("p (h q) -> p h q", q=SSD_P), xt[:, ch].rearrange("p (h q) -> p h q", q=SSD_P),
                                            wt[:, ch, 16 * d:16 * d + 16].unsqueeze(2).to_broadcast([P, SSD_H, SSD_P]), ALU.mult).then_inc(weighted, 1)
                weigh(0)
                for i, (d, ch, to, frm) in enumerate(plan):
                    if i + 1 < len(plan):
                        weigh(i + 1)
                    if i >= 2:
                        dve.wait_ge(kept, i - 1)
                    new = hs[d][:, to]
                    psum = c.ps[:, 2 * (i % 2):2 * (i % 2) + 2].rearrange("p b n -> p (b n)")
                    if frm is None:
                        dve.wait_ge(outer, i + 1)
                        nc.vector.tensor_copy(new, psum).then_inc(kept, 1)
                    else:
                        L(nc.vector.tensor_tensor(new.rearrange("p (h q) -> p h q", q=SSD_P), hs[d][:, frm].rearrange("p (h q) -> p h q", q=SSD_P),
                                                  ex[:, ch, 64 + 16 * d:80 + 16 * d].unsqueeze(2).to_broadcast([P, SSD_H, SSD_P]), ALU.mult))
                        dve.wait_ge(outer, i + 1)
                        nc.vector.tensor_tensor(new, new, psum, ALU.add).then_inc(kept, 1)

    with ExitStack() as s:
        dtail = c.sb(s, "dt_a_masked", [P, 2, 2, HG, P])
        xd = c.sb(s, "x_dt", [P, 3, 2, GP])
        mt = c.split.raw[0].rearrange("p (i d h n) -> p i d h n", i=2, d=2, h=HG)
        cb = c.sb(s, "masked_CB", [P, 2, P])
        off = c.sb(s, "from_states", [P, 2 * GP])
        skip = c.sb(s, "skip", [P, GP])
        spread = c.sem("so_spread")
        done = c.sem("so_products")
        expd = c.sem("so_exp")
        mixed = c.sem("so_mixed")
        diag = c.sem("so_diagonal")
        ready = c.sem("so_ready")
        block = s.enter_context(nc.Block())
        units = [(tile, g) for tile in range(NT) for g in range(SSD_G)]
        U = len(units)
        heads4 = lambda a: a.rearrange("p (h q) -> p h q", q=SSD_P)

        @block.gpsimd
        def _(pool):
            for i, (tile, g) in enumerate(units):
                ch = tile + NC
                if i >= 2:
                    pool.wait_ge(done, i - 1)
                if i >= 3:
                    pool.wait_ge(diag, i - 2)
                for d, m in ((0, LE), (1, GE)):
                    nc.gpsimd.tensor_tensor(dtail[:, i % 2, d], tri[:, m:m + 1].to_broadcast([P, HG, P]),
                                            da[:, ch, 16 * d + HG * g:16 * d + HG * (g + 1)].unsqueeze(2).to_broadcast([P, HG, P]), ALU.mult)
                for d in range(2):
                    last = nc.gpsimd.tensor_tensor(heads4(xd[:, i % 3, d]), heads4(xt[:, ch, g * GP:(g + 1) * GP]),
                                                   dt[:, ch, 16 * d + HG * g:16 * d + HG * (g + 1)].unsqueeze(2).to_broadcast([P, HG, SSD_P]), ALU.mult)
                last.then_inc(spread, 1)

        @block.tensor
        def _(pe):
            for i in range(U + 1):
                if i < U:
                    tile, g = units[i]
                    b = 4 * (i % 2)
                    pe.wait_ge(spread, i + 1)
                    if i >= 2:
                        pe.wait_ge(ready, i - 1)
                    tok = slice(tile * P, (tile + 1) * P)
                    nc.tensor.matmul(c.ps[:, b, 0:P], bT[:, g, CTX + tile * P:CTX + (tile + 1) * P], cT[:, g, tok], start=True, stop=True)
                    nc.tensor.matmul(c.ps[:, b + 1], tri[:, GT], dtail[:, i % 2, 0], start=True, stop=True)
                    nc.tensor.matmul(c.ps[:, b + 2], tri[:, LT], dtail[:, i % 2, 1], start=True, stop=True)
                    for d in range(2):
                        last = nc.tensor.matmul(c.ps[:, b + 3, d * GP:(d + 1) * GP], cT[:, g, tok], hs[d][:, tile, g * GP:(g + 1) * GP],
                                                start=True, stop=True)
                    last.then_inc(done, 1)
                if i:
                    j = i - 1
                    b = 4 * (j % 2)
                    pe.wait_ge(mixed, j + 1)
                    for h in range(HG):
                        for d in range(2):
                            last = nc.tensor.matmul(c.ps[:, b, GP + h * SSD_P:GP + (h + 1) * SSD_P], mt[:, j % 2, d, h],
                                                    xd[:, j % 3, d, h * SSD_P:(h + 1) * SSD_P], start=d == 0, stop=d == 1)
                    last.then_inc(diag, 1)

        @block.scalar
        def _(act):
            for i in range(U):
                b = 4 * (i % 2)
                act.wait_ge(done, i + 1)
                if i >= 2:
                    act.wait_ge(diag, i - 1)
                nc.scalar.activation(mt[:, i % 2].rearrange("p d h n -> p (d h n)"), c.ps[:, b + 1:b + 3].rearrange("p b n -> p (b n)"), ACT.Exp).then_inc(expd, 1)

        @block.vector
        def _(dve):
            L = lambda ins: c.vlink(dve, ins)
            for i in range(U + 1):
                if i < U:
                    b = 4 * (i % 2)
                    dve.wait_ge(done, i + 1)
                    if i:
                        dve.wait_ge(mixed, i)
                    nc.vector.tensor_tensor(cb[:, 0], c.ps[:, b, 0:P], tri[:, LE], ALU.mult)
                    L(nc.vector.tensor_tensor(cb[:, 1], c.ps[:, b, 0:P], tri[:, GE], ALU.mult))
                if i:
                    j = i - 1
                    tile, g = units[j]
                    ch = tile + NC
                    b = 4 * (j % 2)
                    x_g = xt[:, ch, g * GP:(g + 1) * GP]
                    if j:
                        dve.wait_ge(ready, j)
                    for d in range(2):
                        nc.vector.tensor_tensor(heads4(off[:, d * GP:(d + 1) * GP]), heads4(c.ps[:, b + 3, d * GP:(d + 1) * GP]),
                                                ex[:, ch, 32 * d + HG * g:32 * d + HG * (g + 1)].unsqueeze(2).to_broadcast([P, HG, SSD_P]), ALU.mult)
                    L(nc.vector.tensor_tensor(heads4(skip[:]), heads4(x_g), drow[:, HG * g:HG * (g + 1)].unsqueeze(2).to_broadcast([P, HG, SSD_P]), ALU.mult))
                    L(nc.vector.tensor_tensor(off[:, 0:GP], off[:, 0:GP], off[:, GP:], ALU.add))
                    L(nc.vector.tensor_tensor(skip[:], skip[:], off[:, 0:GP], ALU.add))
                    dve.wait_ge(diag, j + 1)
                    nc.vector.tensor_tensor(x_g, skip[:], c.ps[:, b, GP:2 * GP], ALU.add).then_inc(ready, 1)
                if i < U:
                    dve.wait_ge(expd, i + 1)
                    for d in range(2):
                        last = nc.vector.tensor_tensor(mt[:, i % 2, d], mt[:, i % 2, d],
                                                       cb[:, d:d + 1].to_broadcast([P, HG, P]), ALU.mult)
                    last.then_inc(mixed, 1)


def conv_tiles(w_in):
    return [[(KD, P, cols(w_in, XBC0 + n * P, P))] for n in range(16)]


def dt_tiles(w_in):
    return [[(KD, 2 * SSD_H, cols(w_in, DT0, 2 * SSD_H))]]


def conv_project(c, w_in, h, hc, xt, bT, cT, btok, taps, bias, spare, scratch):
    nc = c.nc
    N = 16
    ALL = CTX + SEQ
    parts = lambda i: ((0, CTX), (CTX, ALL)) if i < 12 else ((CTX, ALL),)
    with ExitStack() as s:
        c.split.buffers(c, s, spare)
        ua, xf = (scratch[:, i * 2 * ALL:(i + 1) * 2 * ALL].rearrange("p (i n) -> p i n", n=ALL) for i in range(2))
        done = c.sem("cp_done")
        begun = c.sem("cp_begun")
        back = c.sem("cp_back")
        convd = c.sem("cp_convd")
        silud = c.sem("cp_silu")
        turned = c.sem("cp_turned")
        taken_v = c.sem("cp_taken_v")
        taken_a = c.sem("cp_taken_a")
        block = s.enter_context(nc.Block())

        def bank(i, a):
            return c.ps[:, 2 + i % 2, 0:CTX] if a == 0 else c.ps[:, i % 2]

        def feature(i):
            return xf[:, i % 2] if i < 8 else bT[:, i - 8] if i < 12 else cT[:, i - 12]

        @block.sync
        def _(sp):
            c.split.load(sp, conv_tiles(w_in))
            c.split.ahead(sp, dt_tiles(w_in))

        @block.tensor
        def _(pe):
            for i in range(N + 1):
                if i < N:
                    w = [a[:, 0:KD * P].rearrange("p (k n) -> p k n", n=P) for a in c.split.take(pe)]
                    if i >= 2:
                        pe.wait_ge(convd, i - 1)
                    for a, z in parts(i):
                        for k in range(KD):
                            last = mm3(c, bank(i, a), [part[:, k] for part in w], [part[:, k] for part in (hc if a == 0 else h)], k == 0, k == KD - 1)
                    last.then_inc(done, 1)
                if i and i - 1 < 12:
                    j = i - 1
                    pe.wait_ge(silud, j + 1)
                    if j >= 2:
                        pe.wait_ge(taken_v, j - 1)
                        pe.wait_ge(taken_a, j - 1)
                    for tile in range(TC):
                        last = nc.tensor.transpose(c.ps[:, 4 + 2 * (j % 2) + tile // 4, (tile % 4) * P:(tile % 4 + 1) * P],
                                                   feature(j)[:, tile * P:(tile + 1) * P], c.ident[:])
                    last.then_inc(turned, 1)

        def tokens(j, a, z):
            return xt[:, a:z, j * P:(j + 1) * P] if j < 8 else btok[:, a:z, (j - 8) * P:(j - 7) * P]

        @block.scalar
        def _(act):
            c.split.high(c, act)
            for i in range(N + 2):
                if i + 1 < N:
                    c.split.high(c, act)
                if i < N:
                    act.wait_ge(done, i + 1)
                    if i >= 2:
                        act.wait_ge(silud, i - 1)
                    for a, z in parts(i):
                        last = nc.scalar.activation(ua[:, i % 2, a:z], bank(i, a), ACT.Identity, scale=taps[:, 1, i:i + 1], bias=bias[:, i:i + 1])
                    last.then_inc(begun, 1)
                    act.wait_ge(convd, i + 1)
                    if 2 <= i < 8:
                        act.wait_ge(turned, i - 1)
                    a = 0 if i < 12 else CTX
                    nc.scalar.activation(feature(i), ua[:, i % 2, a:], ACT.Silu).then_inc(silud, 1)
                if i and i - 1 < 12:
                    j = i - 1
                    act.wait_ge(turned, j + 1)
                    nc.scalar.activation(tokens(j, 4, 6), c.ps[:, 5 + 2 * (j % 2), 0:2 * P].rearrange("p (t n) -> p t n", n=P), ACT.Copy).then_inc(taken_a, 1)

        @block.vector
        def _(dve):
            c.split.low(c, dve)
            for i in range(N + 1):
                if i + 1 < N:
                    c.split.low(c, dve)
                if i < N:
                    dve.wait_ge(begun, i + 1)
                    for a, z in parts(i):
                        src = bank(i, a)
                        last = nc.vector.scalar_tensor_tensor(ua[:, i % 2, a + 1:z], src[:, 0:z - a - 1], taps[:, 0, i:i + 1], ua[:, i % 2, a + 1:z], ALU.mult, ALU.add)
                    last.then_inc(back, 1)
                    dve.wait_ge(back, i + 1)
                    for a, z in parts(i):
                        src = bank(i, a)
                        last = nc.vector.scalar_tensor_tensor(ua[:, i % 2, a:z - 1], src[:, 1:z - a], taps[:, 2, i:i + 1], ua[:, i % 2, a:z - 1], ALU.mult, ALU.add)
                    last.then_inc(convd, 1)
                if i and i - 1 < 12:
                    j = i - 1
                    dve.wait_ge(turned, j + 1)
                    nc.vector.tensor_copy(tokens(j, 0, 4), c.ps[:, 4 + 2 * (j % 2)].rearrange("p (t n) -> p t n", n=P)).then_inc(taken_v, 1)


def gate_y(c, w_in, h, xt, yT):
    nc, t = c.nc, c.t
    GP = D // SSD_G
    U = SSD_G * NT
    with ExitStack() as s:
        gcol = c.sb(s, "ssd_gain", [P, KD])
        with ExitStack() as b:
            c.split.buffers(c, b)
            sz = c.sb(b, "silu_z", [P, 2, GP])
            sq = c.sb(b, "squares", [P, GP])
            ss = c.sb(b, "sum_squares", [P, NT, SSD_G])
            landed = c.sem("gy_landed")
            done = c.sem("gy_done")
            silud = c.sem("gy_silu")
            gated = c.sem("gy_gated")
            summed = c.sem("gy_summed")
            meaned = c.sem("gy_meaned")
            block = b.enter_context(nc.Block())

            @block.sync
            def _(sp):
                sp.dma_start(gcol[:], t["g_ssd_norm"][0].rearrange("(k p) -> p k", p=P), allow_slow_non_contiguous=True).then_inc(landed, 16)
                c.split.load(sp, [[(KD, GP, cols(w_in, Z0 + g * GP, GP))] for g in range(SSD_G)])
                sp.wait_ge(landed, 16)

            @block.tensor
            def _(pe):
                for i in range(U):
                    tile = i % NT
                    if tile == 0:
                        w = [a[:].rearrange("p (k n) -> p k n", n=GP) for a in c.split.take(pe)]
                    if i >= 4:
                        pe.wait_ge(silud, i - 3)
                    for k in range(KD):
                        last = mm3(c, c.ps[:, i % 4, 0:GP], [a[:, k, tile * P:(tile + 1) * P] for a in h], [a[:, k] for a in w], k == 0, k == KD - 1)
                    last.then_inc(done, 1)

            @block.scalar
            def _(act):
                c.split.high(c, act)
                for i in range(U + 1):
                    if i % NT == 0 and i + NT < U:
                        c.split.high(c, act)
                    if i < U:
                        act.wait_ge(done, i + 1)
                        if i >= 2:
                            act.wait_ge(gated, i - 1)
                        nc.scalar.activation(sz[:, i % 2], c.ps[:, i % 4, 0:GP], ACT.Silu).then_inc(silud, 1)
                    if i:
                        g, tile = divmod(i - 1, NT)
                        act.wait_ge(gated, i)
                        if i >= 2:
                            act.wait_ge(summed, i - 1)
                        nc.scalar.activation(sq[:], xt[:, NC + tile, g * GP:(g + 1) * GP], ACT.Square,
                                             accum_out=ss[:, tile, g:g + 1]).then_inc(summed, 1)

            @block.gpsimd
            def _(pool):
                pool.wait_ge(meaned, 1)
                nc.gpsimd.tensor_tensor(ss[:], ss[:], c.half[:, 0:4].unsqueeze(1).to_broadcast([P, NT, SSD_G]), ALU.pow).then_inc(meaned, 1)

            @block.vector
            def _(dve):
                c.split.low(c, dve)
                for i in range(U):
                    g, tile = divmod(i, NT)
                    if tile == 0 and i + NT < U:
                        c.split.low(c, dve)
                    dve.wait_ge(silud, i + 1)
                    y = xt[:, NC + tile, g * GP:(g + 1) * GP]
                    nc.vector.tensor_tensor(y, y, sz[:, i % 2], ALU.mult).then_inc(gated, 1)
                dve.wait_ge(summed, U)
                nc.vector.tensor_scalar(ss[:], ss[:], 1.0 / GP, EPS, ALU.mult, ALU.add).then_inc(meaned, 1)
                dve.wait_ge(meaned, 2)
                dve.wait_ge(gated, U)
                for tile in range(NT):
                    y = xt[:, NC + tile].rearrange("p (g q) -> p g q", q=GP)
                    nc.vector.tensor_tensor(y, y, ss[:, tile].unsqueeze(2).to_broadcast([P, SSD_G, GP]), ALU.mult)
        plain_transpose(c, lambda tile: xt[:, NC + tile], NT, KD, lambda k, tile: yT[:, k, tile * P:(tile + 1) * P], lambda k: gcol[:, k:k + 1],
                        ahead=[[(KD, FT2, cols(w_in, c0 + n * FT2, FT2))] for c0 in (Q0, K0) for n in range(2)])


def diff_attention(c, w_in, h, hc, lam, oT):
    nc, t = c.nc, c.t
    ALL = CTX + SEQ
    with ExitStack() as s:
        o = c.sb(s, "heads_out", [P, NT, D])
        ss = c.sb(s, "sum_squares", [P, NT, 8])
        gcol = c.sb(s, "subln_gain", [P, 1])
        with ExitStack() as sa:
            rope = c.sb(sa, "rope", [P, 2, SEQ])
            rot = c.sb(sa, "rotation", [P, P])
            landed = c.sem("rope_landed")
            with ExitStack() as b:
                block = b.enter_context(nc.Block())

                @block.sync
                def _(sp):
                    sp.dma_start(rope[:], t["rope1"].rearrange("a p n -> p a n")).then_inc(landed, 16)
                    sp.dma_start(rot[:], t["rot1"]).then_inc(landed, 16)
                    sp.dma_start(gcol[:], t["g_attn_subln"].rearrange("a p -> p a"), allow_slow_non_contiguous=True).then_inc(landed, 16)
                    sp.wait_ge(landed, 48)

                @block.vector
                def _(dve):
                    dve.wait_ge(landed, 48)
                    nc.vector.tensor_scalar(gcol[:], gcol[:], 1.0 - LAM_INIT, None, ALU.mult)
            for hh in range(2):
                with ExitStack() as sh:
                    qT = c.sb(sh, "qT", [P, 4, SEQ])
                    kT = c.sb(sh, "kT", [P, 4, ALL])
                    v = c.sb(sh, "v", [P, TC, GW])
                    parts = list(zip(h, hc))
                    turns = (rope[:, 0], rope[:, 1], rot[:])

                    def work(out, rope, f, context):
                        return dict(m=P, n=CTX if context else SEQ, out=out, rope=rope,
                                    lhs=lambda w, src, k: w[:, k * FT2 + (f % 2) * P:k * FT2 + (f % 2 + 1) * P],
                                    rhs=lambda w, src, k: src[1 if context else 0][:, k])

                    def token_work(tile, n):
                        src_at, t0 = (1, tile) if tile < NC else (0, tile - NC)
                        return dict(m=P, n=FT2, out=v[:, tile, n * FT2:(n + 1) * FT2], rope=None,
                                    lhs=lambda w, src, k: src[src_at][:, k, t0 * P:(t0 + 1) * P],
                                    rhs=lambda w, src, k: w[:, k * FT2:(k + 1) * FT2])

                    jobs = []
                    for n in range(2):
                        jobs.append(([(KD, FT2, cols(w_in, Q0 + hh * GW + n * FT2, FT2))], [work(qT[:, f], turns, f, False) for f in (2 * n, 2 * n + 1)]))
                    for n in range(2):
                        jobs.append(([(KD, FT2, cols(w_in, K0 + hh * GW + n * FT2, FT2))],
                                     [work(kT[:, f, CTX:], turns, f, False) for f in (2 * n, 2 * n + 1)] +
                                     [work(kT[:, f, 0:CTX], None, f, True) for f in (2 * n, 2 * n + 1)]))
                    for n in range(2):
                        jobs.append(([(KD, FT2, cols(w_in, V0 + hh * GW + n * FT2, FT2))], [token_work(tile, n) for tile in range(TC)]))
                    spare = c.rounded(oT)[:].rearrange("p k n -> p (k n)").rearrange("p (i n) -> p i n", n=PART)
                    project_heads(c, jobs, None, given=parts, spare=[spare[:, i] for i in range(2)],
                                  scratch=o[:, 0:3, GW:2 * GW])
                    diff_units(c, hh, qT, kT, v, o, ss, lam, oT)
        with ExitStack() as b:
            step = c.sem("sub_steps")
            block = b.enter_context(nc.Block())

            @block.gpsimd
            def _(pool):
                pool.wait_ge(step, 1)
                nc.gpsimd.tensor_tensor(ss[:], ss[:], c.half[:].unsqueeze(1).to_broadcast([P, NT, 8]), ALU.pow).then_inc(step, 1)

            @block.vector
            def _(dve):
                nc.vector.tensor_scalar(ss[:], ss[:], 1.0 / P, EPS, ALU.mult, ALU.add).then_inc(step, 1)
                dve.wait_ge(step, 2)
                for tile in range(NT):
                    ot = o[:, tile].rearrange("p (h q) -> p h q", q=P)
                    nc.vector.tensor_tensor(ot, ot, ss[:, tile].unsqueeze(2).to_broadcast([P, 8, P]), ALU.mult)
        plain_transpose(c, lambda tile: o[:, tile], NT, KD, lambda k, tile: oT[:, k, tile * P:(tile + 1) * P], lambda k: gcol[:],
                        ahead=merge_tiles(c))


def diff_units(c, hh, qT, kT, v, o, ss, lam, scratch):
    nc = c.nc
    ALL = CTX + SEQ
    SC = 64 ** -0.5
    units = [(tile, h) for tile in range(NT) for h in range(4)]
    U = len(units)
    with ExitStack() as s:
        pr = c.sb(s, "probs", [P, 3, 2, ALL])
        prT = scratch[:, 0:3].rearrange("p a n -> p (a n)").rearrange("p (i t n) -> p i t n", i=2, t=TC)
        sq = scratch[:, 3, 0:P]
        mx = c.sb(s, "maxima", [P, 2, 2])
        ls = c.sb(s, "sums", [P, 3, 2])
        scored = c.sem("du_scored")
        first = c.sem("du_first_component")
        biased = c.sem("du_biased")
        expd = c.sem("du_exp")
        mixed = c.sem("du_mixed")
        turned = c.sem("du_turned")
        copied_a = c.sem("du_copied_a")
        copied_v = c.sem("du_copied_v")
        summed = c.sem("du_summed")
        left = c.sem("du_left")
        squared = c.sem("du_squared")
        block = s.enter_context(nc.Block())

        def scores(i):
            return c.ps[:, 3 * (i % 2):3 * (i % 2) + 3].rearrange("p b n -> p (b n)")

        @block.tensor
        def _(pe):
            for i in range(U + 3):
                def score(m, a, z):
                    tile, h = units[i]
                    r = slice(64 * m, 64 * m + 64)
                    return nc.tensor.matmul(scores(i)[:, m * ALL + a:m * ALL + z], qT[r, h, tile * P:(tile + 1) * P], kT[r, h, a:z], start=True, stop=True)
                if i < U:
                    if i >= 2:
                        pe.wait_ge(expd, 2 * (i - 1))
                    score(0, 512, ALL).then_inc(first, 1)
                    score(0, 0, 512)
                if 0 <= i - 3 < U:
                    j = i - 3
                    tile, h = units[j]
                    pe.wait_ge(copied_a, j + 1)
                    pe.wait_ge(copied_v, j + 1)
                    for b in range(TC):
                        last = nc.tensor.matmul(c.ps[:, 7, 2 * P:3 * P], prT[:, j % 2, b], v[:, b, h * P:(h + 1) * P], start=b == 0, stop=b == TC - 1)
                    last.then_inc(summed, 1)
                if i < U:
                    pe.wait_ge(first, i + 1)
                    score(1, 0, 256)
                    score(1, 256, ALL).then_inc(scored, 1)
                if 0 <= i - 2 < U:
                    j = i - 2
                    pe.wait_ge(mixed, j + 1)
                    if j:
                        pe.wait_ge(left, j)
                        pe.wait_ge(copied_a, j)
                    for b in range(TC):
                        last = nc.tensor.transpose(c.ps[:, 6 + b // 4, (b % 4) * P:(b % 4 + 1) * P], pr[:, j % 3, 0, b * P:(b + 1) * P], c.ident[:])
                    last.then_inc(turned, 1)

        @block.scalar
        def _(act):
            for i in range(U + 3):
                if i < U:
                    act.wait_ge(biased, i + 1)
                    if i >= 3:
                        act.wait_ge(turned, i - 2)
                    for m in range(2):
                        nc.scalar.activation(pr[:, i % 3, m], scores(i)[:, m * ALL:(m + 1) * ALL], ACT.Exp, bias=mx[:, i % 2, m:m + 1], scale=SC,
                                             accum_out=ls[:, i % 3, m:m + 1]).then_inc(expd, 1)
                if 0 <= i - 2 < U:
                    j = i - 2
                    act.wait_ge(turned, j + 1)
                    if j >= 2:
                        act.wait_ge(summed, j - 1)
                    nc.scalar.activation(prT[:, j % 2, 0:4], c.ps[:, 6].rearrange("p (b n) -> p b n", n=P), ACT.Copy).then_inc(copied_a, 1)
                if 0 <= i - 3 < U:
                    j = i - 3
                    tile, h = units[j]
                    n = hh * 4 + h
                    act.wait_ge(left, j + 1)
                    if j:
                        act.wait_ge(squared, j)
                    nc.scalar.activation(sq, o[:, tile, n * P:(n + 1) * P], ACT.Square, accum_out=ss[:, tile, n:n + 1]).then_inc(squared, 1)

        @block.vector
        def _(dve):
            L = lambda ins: c.vlink(dve, ins)
            for i in range(U + 3):
                if 0 <= i - 3 < U:
                    j = i - 3
                    tile, h = units[j]
                    n = hh * 4 + h
                    dve.wait_ge(summed, j + 1)
                    nc.vector.tensor_copy(o[:, tile, n * P:(n + 1) * P], c.ps[:, 7, 2 * P:3 * P]).then_inc(left, 1)
                if i < U:
                    dve.wait_ge(scored, i + 1)
                    if i >= 2:
                        dve.wait_ge(expd, 2 * (i - 1))
                    L(nc.vector.tensor_reduce(mx[:, i % 2], scores(i).rearrange("p (m n) -> p m n", n=ALL), AX, ALU.max))
                    nc.vector.tensor_scalar(mx[:, i % 2], mx[:, i % 2], -SC, None, ALU.mult).then_inc(biased, 1)
                if 0 <= i - 1 < U:
                    j = i - 1
                    r = ls[:, j % 3]
                    dve.wait_ge(expd, 2 * j + 2)
                    L(nc.vector.reciprocal(r, r))
                    nc.vector.tensor_scalar(pr[:, j % 3, 0], pr[:, j % 3, 0], r[:, 0:1], None, ALU.mult)
                    L(nc.vector.tensor_tensor(r[:, 1:2], r[:, 1:2], lam[:], ALU.mult))
                    nc.vector.scalar_tensor_tensor(pr[:, j % 3, 0], pr[:, j % 3, 1], r[:, 1:2], pr[:, j % 3, 0], ALU.mult, ALU.add).then_inc(mixed, 1)
                if 0 <= i - 2 < U:
                    j = i - 2
                    dve.wait_ge(turned, j + 1)
                    if j >= 2:
                        dve.wait_ge(summed, j - 1)
                    nc.vector.tensor_copy(prT[:, j % 2, 4:6], c.ps[:, 7, 0:2 * P].rearrange("p (b n) -> p b n", n=P)).then_inc(copied_v, 1)


def merge_tiles(c):
    t = c.t
    w_in, w_attn, w_ssd = t["w_in"][0], t["w_branch_attn"][0], t["w_branch_ssd"][0]
    return [[(KD, P, cols(src, c0 + i * P, P)) for src, c0 in kind] for i in range(KD)
            for kind in (((w_in, G0), (w_in, G0 + D)), ((w_attn, 0), (w_ssd, 0)))]


def merge(c, w_in, h, yT, oT, spare):
    nc, t = c.nc, c.t
    with ExitStack() as s:
        mT = c.sb(s, "mergedT", [P, KD, SEQ])
        with ExitStack() as b:
            branch = [(c.sb(b, "branch_high", [P, KD, SEQ], F32R), c.rounded(a)) for a in (oT, yT)]
            c.split.buffers(c, b, spare)
            split_stage(c, halves(branch[0], oT) + halves(branch[1], yT))
            sg = c.sb(b, "sigmoids", [P, 2, SEQ])
            tmp = c.sb(b, "gated_ssd", [P, SEQ])
            done = c.sem("mg_done")
            gates = c.sem("mg_gates")
            sigd = c.sem("mg_sigmoid")
            left = c.sem("mg_left")
            block = b.enter_context(nc.Block())

            @block.sync
            def _(sp):
                c.split.load(sp, merge_tiles(c))
                c.split.ahead(sp, residual_tiles(t["w_out"][0], KD))

            @block.tensor
            def _(pe):
                for i in range(KD):
                    b0 = 4 * (i % 2)
                    for pair in range(2):
                        w = [a[:].rearrange("p (k v n) -> p k v n", v=2, k=KD) for a in c.split.take(pe)]
                        if i >= 2 and pair == 0:
                            pe.wait_ge(left, i - 1)
                        for v in range(2):
                            src = h if pair == 0 else branch[v]
                            for k in range(KD):
                                last = mm3(c, c.ps[:, b0 + 2 * pair + v], [a[:, k, v] for a in w], [a[:, k] for a in src], k == 0, k == KD - 1)
                        last.then_inc(gates if pair == 0 else done, 1)

            @block.scalar
            def _(act):
                c.split.high(c, act)
                for i in range(KD):
                    for _ in range(2 if i + 1 < KD else 1):
                        c.split.high(c, act)
                    act.wait_ge(gates, i + 1)
                    if i:
                        act.wait_ge(left, i)
                    nc.scalar.activation(sg[:].rearrange("p v n -> p (v n)"), c.ps[:, 4 * (i % 2):4 * (i % 2) + 2].rearrange("p b n -> p (b n)"),
                                         ACT.Sigmoid).then_inc(sigd, 1)

            @block.vector
            def _(dve):
                c.split.low(c, dve)
                for i in range(KD):
                    for _ in range(2 if i + 1 < KD else 1):
                        c.split.low(c, dve)
                    dve.wait_ge(done, i + 1)
                    dve.wait_ge(sigd, i + 1)
                    b0 = 4 * (i % 2)
                    if i:
                        dve.wait_ge(left, i)
                    nc.vector.tensor_tensor(tmp[:], c.ps[:, b0 + 3], sg[:, 1], ALU.mult)
                    c.vlink(dve, nc.vector.tensor_tensor(mT[:, i], c.ps[:, b0 + 2], sg[:, 0], ALU.mult))
                    nc.vector.tensor_tensor(mT[:, i], mT[:, i], tmp[:], ALU.add).then_inc(left, 1)
        project_residual(c, t["w_out"][0], KD, mT, c.gate[:, 0], f=yT[:].rearrange("p k n -> p (k n)").rearrange("p (t d) -> p t d", d=D), spare=spare)
I32 = mybir.dt.int32
EXPERTS, TOP_K, GROUPS, TOP_GROUPS, EF = 64, 8, 8, 4, 256
ROUTED_SCALE = 2.5
MOST_BLOCKS = SEQ * TOP_K // P + EXPERTS
TABLE = MOST_BLOCKS + 8
SKIPPED = 1 << 20
PICKED = -3e30


def moe(c):
    nc, t = c.nc, c.t
    h_dram = nc.dram_tensor("h2_tokens", (SEQ, D), F32, kind="Internal").ap()
    table = nc.dram_tensor("block_table", (TABLE * P, 4), I32, kind="Internal").ap()
    y_dram = nc.dram_tensor("expert_rows", (SEQ * TOP_K, D), F32, kind="Internal").ap()
    norm_transpose(c, c.x, NT, [(lambda k, tile: c.hT[:, k, tile * P:(tile + 1) * P],
                                 lambda k: c.scale2[:, k:k + 1], lambda k: c.shift2[:, k:k + 1])])
    with ExitStack() as s:
        acc = c.sb(s, "ffn_out", [P, NT, D])
        erow = c.sb(s, "block_expert", [1, TABLE], I32)
        count = c.sb(s, "block_count", [1, 1], I32)
        route(c, h_dram, table, erow, count)
        shared_expert(c, acc)
        expert_blocks(c, h_dram, table, y_dram, erow, count)
        combine(c, y_dram, acc)


def route(c, h_dram, table, erow, count):
    nc, t = c.nc, c.t
    LE, LT, ONES = range(3)
    E = EXPERTS
    with ExitStack() as s:
        ht = c.sb(s, "h_tokens", [P, NT, D])
        tri = c.sb(s, "triangles", [P, 3, P])
        bias = c.sb(s, "router_bias", [P, E])
        init = c.sb(s, "table_start", [P, TABLE, 4], I32)
        pay = c.sb(s, "payload", [P, NT, TOP_K, 4], I32)
        small = c.sb(s, "rank_tables", [P, 64 + 8])
        iota = c.sb(s, "block_numbers", [P, TABLE])
        sg = c.sb(s, "scores", [P, NT, E])
        sel = c.sb(s, "selection", [P, NT, E])
        top = c.sb(s, "sorted", [P, NT * GROUPS, 8])
        gs = c.sb(s, "group_scores", [P, NT, GROUPS])
        pair = c.sb(s, "pairs", [P, NT, GROUPS, GROUPS])
        equal = c.sb(s, "equal_pairs", [P, NT, GROUPS, GROUPS])
        mask = c.sb(s, "chosen", [P, NT, E])
        key = c.sb(s, "order", [P, NT, E])
        wt = c.sb(s, "weights", [P, NT, E])
        dest = c.sb(s, "destinations", [P, NT, E])
        tot = c.sb(s, "weight_sums", [P, NT])
        cnt = c.sb(s, "counts", [E, 4])
        nbw = c.sb(s, "block_counts_wide", [E, P])
        over = c.sb(s, "blocks_over", [E, TABLE])
        start = c.sb(s, "block_starts", [P, E])
        pick = c.sb(s, "picks", [P, TOP_K, E])
        got = c.sb(s, "picked", [P, NT, TOP_K])
        desti = c.sb(s, "destination_rows", [P, NT, TOP_K], I32)
        nrow = c.sb(s, "block_row", [1, TABLE])
        even = c.sb(s, "pair_flags", [1, TABLE])
        landed = c.sem("ro_landed")
        inited = c.sem("ro_table_started")
        logits = c.sem("ro_logits")
        scored = c.sem("ro_scores")
        chosen = c.sem("ro_chosen")
        counted = c.sem("ro_counted")
        blocked = c.sem("ro_blocked")
        summed = c.sem("ro_summed")
        compared = c.sem("ro_compared")
        numbered = c.sem("ro_numbered")
        filled = c.sem("ro_filled")
        sent = c.sem("ro_sent")
        turned = c.sem("ro_turned")
        copied = c.sem("ro_copied")
        stored = c.sem("ro_stored")
        block = s.enter_context(nc.Block())

        @block.sync
        def _(sp):
            for i, m in enumerate((0, 3, 4)):
                sp.dma_start(tri[:, i], t["tri"][m]).then_inc(landed, 16)
            sp.dma_start(bias[:], t["router_bias"].to_broadcast([P, E])).then_inc(landed, 16)
            sp.dma_start(pay[:], t["payload"]).then_inc(landed, 16)
            sp.dma_start(small[:], t["rank"].to_broadcast([P, 72])).then_inc(landed, 16)
            sp.dma_start(iota[:], t["blocks"].to_broadcast([P, TABLE])).then_inc(landed, 16)
            sp.dma_start(init[:], t["table"].rearrange("(p n) w -> p n w", p=P)).then_inc(landed, 16)
            load_weights(c, sp, [whole(cols(t["w_router"][0], 0, E))])
            sp.wait_ge(landed, 128)
            sp.dma_start(table.rearrange("(p n) w -> p n w", p=P), init[:]).then_inc(inited, 16)
            for tile in range(NT):
                sp.wait_ge(copied, 2 * tile + 2)
                sp.dma_start(h_dram[tile * P:(tile + 1) * P], ht[:, tile]).then_inc(stored, 16)
            sp.wait_ge(stored, 16 * NT)

        @block.tensor
        def _(pe):
            w = take(c, pe, 1)
            for tile in range(NT):
                for k in range(KD):
                    last = mm(c, c.ps[:, 0, tile * E:(tile + 1) * E], c.hT[:, k, tile * P:(tile + 1) * P], w[:, k * E:(k + 1) * E], k == 0, k == KD - 1)
            last.then_inc(logits, 1)
            for tile in range(NT):
                if tile:
                    pe.wait_ge(copied, 2 * tile)
                for k in range(KD):
                    last = nc.tensor.transpose(c.ps[:, 6 + k // 4, (k % 4) * P:(k % 4 + 1) * P], c.hT[:, k, tile * P:(tile + 1) * P], c.ident[:])
                last.then_inc(turned, 1)
            pe.wait_ge(landed, 128)
            pe.wait_ge(chosen, 1)
            for tile in range(NT):
                for j in range(tile + 1):
                    nc.tensor.matmul(c.ps[:, 1, tile * E:(tile + 1) * E], tri[:, LT if j == tile else ONES], mask[:, j], start=j == 0, stop=j == tile)
            for j in range(NT):
                last = nc.tensor.matmul(c.ps[0:E, 2, 0:1], mask[:, j], tri[:, ONES, 0:1], start=j == 0, stop=j == NT - 1)
            last.then_inc(counted, 1)
            pe.wait_ge(blocked, 1)
            nc.tensor.matmul(c.ps[:, 3, 0:E], nbw[:], tri[0:E, LT, 0:E], start=True, stop=True)
            nc.tensor.matmul(c.ps[:, 3, E:2 * E], nbw[:], tri[0:E, ONES, 0:E], start=True, stop=True)
            nc.tensor.matmul(c.ps[0:E, 4, 0:1], tri[0:E, LE, 0:E], nbw[:, 0:1], start=True, stop=True).then_inc(summed, 1)
            pe.wait_ge(compared, 1)
            nc.tensor.matmul(c.ps[0:1, 5, 0:TABLE], tri[0:E, ONES, 0:1], over[:], start=True, stop=True).then_inc(numbered, 1)

        @block.scalar
        def _(act):
            act.wait_ge(logits, 1)
            nc.scalar.activation(sg[:].rearrange("p t e -> p (t e)"), c.ps[:, 0, 0:NT * E], ACT.Sigmoid).then_inc(scored, 1)
            for tile in range(NT):
                act.wait_ge(turned, tile + 1)
                for b in range(2):
                    nc.scalar.activation(ht[:, tile, b * GW:(b + 1) * GW], c.ps[:, 6 + b], ACT.Copy).then_inc(copied, 1)

        @block.gpsimd
        def _(pool):
            pool.wait_ge(filled, 1)
            pool.wait_ge(inited, 16)
            for tile in range(NT):
                for r in range(TOP_K):
                    nc.gpsimd.indirect_dma_start(table, bass.IndirectOffsetOnAxis(desti[:, tile, r:r + 1], 0), pay[:, tile, r], None).then_inc(sent, 16)
            pool.wait_ge(sent, 16 * NT * TOP_K)

        @block.vector
        def _(dve):
            L = lambda ins: c.vlink(dve, ins)
            V = nc.vector
            dve.wait_ge(landed, 128)
            dve.wait_ge(scored, 1)
            L(V.tensor_tensor(sel[:], sg[:], bias[:].unsqueeze(1).to_broadcast([P, NT, E]), ALU.add))
            for n in range(NT * GROUPS):
                ins = V.max(top[:, n], sel[:, n // GROUPS, (n % GROUPS) * 8:(n % GROUPS + 1) * 8])
            L(ins)
            L(V.tensor_tensor(gs[:].rearrange("p t g -> p (t g)"), top[:, :, 0], top[:, :, 1], ALU.add))
            for tile in range(NT):
                other = gs[:, tile].unsqueeze(1).to_broadcast([P, GROUPS, GROUPS])
                own = gs[:, tile].unsqueeze(2).to_broadcast([P, GROUPS, GROUPS])
                V.tensor_tensor(pair[:, tile], other, own, ALU.is_gt)
                ins = V.tensor_tensor(equal[:, tile], other, own, ALU.is_equal)
            L(ins)
            before = small[:, 0:64].rearrange("p (i j) -> p i j", j=GROUPS)
            for tile in range(NT):
                ins = V.tensor_tensor(equal[:, tile], equal[:, tile], before, ALU.mult)
            L(ins)
            L(V.tensor_tensor(pair[:], pair[:], equal[:], ALU.add))
            L(V.tensor_reduce(gs[:], pair[:], AX, ALU.add))
            L(V.tensor_scalar(gs[:], gs[:], float(TOP_GROUPS), None, ALU.is_lt))
            for tile in range(NT):
                ins = V.tensor_tensor(sel[:, tile].rearrange("p (g e) -> p g e", e=8), sel[:, tile].rearrange("p (g e) -> p g e", e=8),
                                      gs[:, tile].unsqueeze(2).to_broadcast([P, GROUPS, 8]), ALU.mult)
            L(ins)
            L(V.tensor_scalar(gs[:], gs[:], -1.0, -NEG, ALU.add, ALU.mult))
            for tile in range(NT):
                ins = V.tensor_tensor(sel[:, tile].rearrange("p (g e) -> p g e", e=8), sel[:, tile].rearrange("p (g e) -> p g e", e=8),
                                      gs[:, tile].unsqueeze(2).to_broadcast([P, GROUPS, 8]), ALU.add)
            L(ins)
            for tile in range(NT):
                ins = V.max(top[:, tile], sel[:, tile])
            L(ins)
            for tile in range(NT):
                ins = V.match_replace(mask[:, tile], top[:, tile], sel[:, tile], PICKED)
            L(ins)
            V.tensor_scalar(mask[:], mask[:], 0.5 * (PICKED + NEG), None, ALU.is_lt).then_inc(chosen, 1)
            dve.wait_ge(chosen, 1)
            L(V.tensor_tensor(wt[:], sg[:], mask[:], ALU.mult))
            L(V.tensor_reduce(tot[:], wt[:], AX, ALU.add))
            L(V.reciprocal(tot[:], tot[:]))
            L(V.tensor_scalar(tot[:], tot[:], ROUTED_SCALE, None, ALU.mult))
            L(V.tensor_tensor(wt[:], wt[:], tot[:].unsqueeze(2).to_broadcast([P, NT, E]), ALU.mult))
            for tile in range(NT):
                ins = V.tensor_tensor_scan(key[:, tile], tri[:, ONES, 0:E], mask[:, tile], 0.0, ALU.mult, ALU.add)
            L(ins)
            L(V.tensor_tensor(key[:], key[:], mask[:], ALU.mult))
            dve.wait_ge(counted, 1)
            L(V.tensor_copy(cnt[:, 0:1], c.ps[0:E, 2, 0:1]))
            L(V.tensor_scalar(cnt[:, 1:2], cnt[:, 0:1], 0.0, None, ALU.is_gt))
            for n in range(1, NT):
                L(V.tensor_scalar(cnt[:, 2:3], cnt[:, 0:1], float(n * P), None, ALU.is_gt))
                L(V.tensor_tensor(cnt[:, 1:2], cnt[:, 1:2], cnt[:, 2:3], ALU.add))
            V.tensor_copy(nbw[:], cnt[:, 1:2].to_broadcast([E, P])).then_inc(blocked, 1)
            dve.wait_ge(summed, 1)
            L(V.tensor_copy(cnt[:, 3:4], c.ps[0:E, 4, 0:1]))
            V.tensor_scalar(over[:], iota[0:E], cnt[:, 3:4], None, ALU.is_ge).then_inc(compared, 1)
            L(V.tensor_scalar(start[:], c.ps[:, 3, 0:E], float(P), None, ALU.mult))
            L(V.tensor_tensor(dest[:], c.ps[:, 1, 0:NT * E].rearrange("p (t e) -> p t e", e=E), start[:].unsqueeze(1).to_broadcast([P, NT, E]), ALU.add))
            for src, out in ((dest, desti), (wt, None)):
                for tile in range(NT):
                    L(V.tensor_tensor(pick[:], key[:, tile].unsqueeze(1).to_broadcast([P, TOP_K, E]), small[:, 64:72].unsqueeze(2).to_broadcast([P, TOP_K, E]), ALU.is_equal))
                    L(V.tensor_tensor(pick[:], pick[:], src[:, tile].unsqueeze(1).to_broadcast([P, TOP_K, E]), ALU.mult))
                    L(V.tensor_reduce(got[:, tile], pick[:], AX, ALU.add))
                if out is not None:
                    L(V.tensor_copy(out[:], got[:]))
            V.tensor_copy(pay[:].bitcast(F32)[:, :, :, 1], got[:]).then_inc(filled, 1)
            dve.wait_ge(numbered, 1)
            L(V.tensor_scalar(nrow[:], c.ps[0:1, 5, 0:TABLE], float(E - 1), None, ALU.min))
            L(V.tensor_copy(erow[:], nrow[:]))
            L(V.tensor_reduce(nrow[:, 0:1], c.ps[0:1, 3, E:2 * E], AX, ALU.max))
            L(V.tensor_scalar(even[:, 0:TABLE // 2], iota[0:1, 0:TABLE:2], nrow[:, 0:1], None, ALU.is_lt))
            L(V.tensor_reduce(nrow[:, 1:2], even[:, 0:TABLE // 2], AX, ALU.add))
            L(V.tensor_scalar(nrow[:, 2:3], nrow[:, 1:2], 2.0, None, ALU.mult))
            V.tensor_copy(count[:], nrow[:, 2:3])


def shared_expert(c, acc):
    nc, t = c.nc, c.t
    with ExitStack() as s:
        sl = c.sb(s, "silu", [P, 2, SEQ])
        hid = c.sb(s, "hidden", [P, 2, SEQ])
        up = c.sem("se_up")
        silud = c.sem("se_silu")
        gated = c.sem("se_gated")
        down = c.sem("se_down")
        block = s.enter_context(nc.Block())

        @block.sync
        def _(sp):
            load_weights(c, sp, [[(0, KD, EF, cols(t["w_sh_gate"][0], 0, EF)), (KD * EF, KD, EF, cols(t["w_sh_up"][0], 0, EF))],
                                 whole(cols(t["w_sh_down"][0], 0, D))])

        @block.tensor
        def _(pe):
            w = take(c, pe, 2).rearrange("p (v k n) -> p v k n", v=2, k=KD)
            for f in range(2):
                for v in range(2):
                    for k in range(KD):
                        last = mm(c, c.ps[:, 2 * f + v], w[:, v, k, f * P:(f + 1) * P], c.hT[:, k], k == 0, k == KD - 1)
                last.then_inc(up, 1)
            w = take(c, pe, 1)[:, 0:2 * D].rearrange("p (k n) -> p k n", k=2)
            pe.wait_ge(gated, 2)
            for tile in range(NT):
                for hf in range(2):
                    for k in range(2):
                        last = mm(c, c.ps[:, 2 * tile + hf], hid[:, k, tile * P:(tile + 1) * P], w[:, k, hf * GW:(hf + 1) * GW], k == 0, k == 1)
                last.then_inc(down, 1)

        @block.scalar
        def _(act):
            for f in range(2):
                act.wait_ge(up, f + 1)
                nc.scalar.activation(sl[:, f], c.ps[:, 2 * f], ACT.Silu).then_inc(silud, 1)

        @block.vector
        def _(dve):
            for f in range(2):
                dve.wait_ge(silud, f + 1)
                nc.vector.tensor_tensor(hid[:, f], sl[:, f], c.ps[:, 2 * f + 1], ALU.mult).then_inc(gated, 1)
            for tile in range(NT):
                dve.wait_ge(down, tile + 1)
                nc.vector.tensor_copy(acc[:, tile], c.ps[:, 2 * tile:2 * tile + 2].rearrange("p b n -> p (b n)"))


def expert_blocks(c, h_dram, table, y_dram, erow, count):
    nc, t = c.nc, c.t
    ws = {n: t[n][0] for n in ("w_e_gate", "w_e_up", "w_e_down")}
    tab = table.rearrange("(b p) w -> b p w", p=P)
    with ExitStack() as s:
        both = lambda name, shape, dt=F32: [c.sb(s, f"{name}{p}", shape, dt) for p in range(2)]
        sems = lambda name: [c.sem(f"{name}{p}") for p in range(2)]
        wgu = both("gate_up", [P, KD, 2 * EF])
        wd = both("down", [P, 2, D])
        fetch = both("fetch_rows", [P, 4], I32)
        give = both("give_rows", [P, 4], I32)
        xg = both("gathered", [P, D])
        xT = both("gatheredT", [P, KD, P])
        sl = both("silu", [P, EF])
        hid = both("hidden", [P, EF])
        hidT = both("hiddenT", [P, 2, P])
        y = both("weighted_out", [P, D])
        wgu_in, wd_in, fetch_in, give_in = sems("gate_up_in"), sems("down_in"), sems("fetch_in"), sems("give_in")
        gathered, scattered = sems("gathered"), sems("scattered")
        up_done, silud, gated, turned, copied, down_done = sems("up_done"), sems("silued"), sems("gated"), sems("hid_turned"), sems("hid_copied"), sems("down_done")
        x_turned, x_low, x_high, y_ready = sems("x_turned"), sems("x_low"), sems("x_high"), sems("y_ready")
        passed = c.sem("waits_passed")
        cleared = c.sem("gathered_cleared")
        block = s.enter_context(nc.Block())

        def trips(eng):
            return eng.value_load(count[0:1, 0:1], min_val=2, max_val=MOST_BLOCKS)

        @block.sync
        def _(sp):
            def weights(p, b):
                return sp.value_load(erow[0:1, bass.ds(b, 1)], min_val=0, max_val=EXPERTS - 1)

            def gate_up(p, e):
                for v, name in enumerate(("w_e_gate", "w_e_up")):
                    sp.dma_start(wgu[p][:, :, v * EF:(v + 1) * EF], ws[name][bass.ds(e, 1)].rearrange("o (k p) n -> p (o k) n", p=P)).then_inc(wgu_in[p], 16)

            def down(p, e):
                sp.dma_start(wd[p][:], ws["w_e_down"][bass.ds(e, 1)].rearrange("o (k p) n -> p (o k) n", p=P)).then_inc(wd_in[p], 16)

            e = [weights(p, p) for p in range(2)]
            for p in range(2):
                gate_up(p, e[p])
            for p in range(2):
                down(p, e[p])
            n = trips(sp)
            with sp.Fori(2, n, 2) as i:
                e = [weights(p, i + p) for p in range(2)]
                for p in range(2):
                    sp.wait_ge(up_done[p], i)
                    sp.sem_inc(passed, 1)
                    gate_up(p, e[p])
                for p in range(2):
                    sp.wait_ge(down_done[p], i + 2)
                    sp.sem_inc(passed, 1)
                    down(p, e[p])
            for p in range(2):
                sp.wait_ge(wgu_in[p], 16 * n)
                sp.sem_inc(passed, 1)
                sp.wait_ge(wd_in[p], 8 * n)
                sp.sem_inc(passed, 1)

        @block.gpsimd
        def _(pool):
            def rows(dst, sem, b):
                nc.gpsimd.dma_start(dst[:], tab[bass.ds(b, 1)].rearrange("o p w -> p (o w)")).then_inc(sem, 16)

            def gather(p):
                nc.gpsimd.indirect_dma_start(xg[p][:], None, h_dram, bass.IndirectOffsetOnAxis(fetch[p][:, 0:1], 0),
                                             bounds_check=SEQ - 1, oob_is_err=False).then_inc(gathered[p], 16)

            for p in range(2):
                rows(fetch[p], fetch_in[p], p)
            for p in range(2):
                pool.wait_ge(cleared, 2)
                pool.wait_ge(fetch_in[p], 16)
                gather(p)
            for p in range(2):
                pool.wait_ge(gathered[p], 16)
                rows(fetch[p], fetch_in[p], 2 + p)
            for p in range(2):
                rows(give[p], scattered[p], p)
            n = trips(pool)
            with pool.Fori(0, n, 2) as i:
                for p in range(2):
                    pool.wait_ge(fetch_in[p], 8 * i + 32)
                    pool.wait_ge(x_turned[p], i + 2)
                    pool.sem_inc(passed, 1)
                    gather(p)
                for p in range(2):
                    pool.wait_ge(scattered[p], 8 * i + 16)
                    rows(give[p], give_in[p], i + p)
                for p in range(2):
                    pool.wait_ge(give_in[p], 8 * i + 16)
                    pool.wait_ge(y_ready[p], i + 4)
                    pool.sem_inc(passed, 1)
                    nc.gpsimd.indirect_dma_start(y_dram, bass.IndirectOffsetOnAxis(give[p][:, 2:3], 0), y[p][:], None,
                                                 bounds_check=SEQ * TOP_K - 1, oob_is_err=False).then_inc(scattered[p], 16)
                    if p == 0:
                        for q in range(2):
                            pool.wait_ge(gathered[q], 8 * i + 32)
                            rows(fetch[q], fetch_in[q], i + (4 + q))
            for p in range(2):
                pool.wait_ge(scattered[p], 8 * n + 16)
                pool.wait_ge(gathered[p], 8 * n + 16)
                pool.wait_ge(fetch_in[p], 8 * n + 32)
            pool.sem_inc(passed, 1)

        @block.tensor
        def _(pe):
            def x_transposes(p):
                for k in range(KD):
                    last = nc.tensor.transpose(c.ps[:, 5 + k // 4, (k % 4) * P:(k % 4 + 1) * P], xg[p][:, k * P:(k + 1) * P], c.ident[:])
                last.then_inc(x_turned[p], 2)

            for p in range(2):
                pe.wait_ge(gathered[p], 16)
                if p:
                    pe.wait_ge(x_low[0], 2)
                    pe.wait_ge(x_high[0], 2)
                x_transposes(p)
            for p in range(2):
                pe.sem_inc(turned[p], 2)
                pe.sem_inc(down_done[p], 2)
            n = trips(pe)
            with pe.Fori(0, n, 2) as i:
                for p in range(2):
                    pe.wait_ge(x_low[p], i + 2)
                    pe.wait_ge(x_high[p], i + 2)
                    pe.wait_ge(wgu_in[p], 16 * i + 32)
                    pe.wait_ge(gated[p], i + 2)
                    for k in range(KD):
                        last = nc.tensor.matmul(c.ps[:, p], xT[p][:, k], wgu[p][:, k], start=k == 0, stop=k == KD - 1)
                    last.then_inc(up_done[p], 2)
                for p in range(2):
                    pe.wait_ge(gated[p], i + 4)
                    pe.wait_ge(copied[1 - p], i + 2 + 2 * p)
                    for k in range(2):
                        last = nc.tensor.transpose(c.ps[:, 2, k * P:(k + 1) * P], hid[p][:, k * P:(k + 1) * P], c.ident[:])
                    last.then_inc(turned[p], 2)
                    pe.wait_ge(gathered[p], 8 * i + 32)
                    pe.wait_ge(x_low[1 - p], i + 2 + 2 * p)
                    pe.wait_ge(x_high[1 - p], i + 2 + 2 * p)
                    x_transposes(p)
                    pe.wait_ge(copied[p], i + 4)
                    pe.wait_ge(wd_in[p], 8 * i + 16)
                    pe.wait_ge(y_ready[1 - p], i + 2 + 2 * p)
                    for hf in range(2):
                        for k in range(2):
                            last = nc.tensor.matmul(c.ps[:, 3 + hf], hidT[p][:, k], wd[p][:, k, hf * GW:(hf + 1) * GW], start=k == 0, stop=k == 1)
                    last.then_inc(down_done[p], 2)

        @block.scalar
        def _(act):
            def x_low_half(p):
                nc.scalar.activation(xT[p][:, 0:4], c.ps[:, 5].rearrange("p (k n) -> p k n", n=P), ACT.Copy).then_inc(x_low[p], 2)

            for p in range(2):
                act.wait_ge(x_turned[p], 2)
                x_low_half(p)
            for p in range(2):
                act.sem_inc(y_ready[p], 2)
            n = trips(act)
            with act.Fori(0, n, 2) as i:
                for p in range(2):
                    act.wait_ge(up_done[p], i + 2)
                    act.wait_ge(gated[p], i + 2)
                    nc.scalar.activation(sl[p][:], c.ps[:, p, 0:EF], ACT.Silu).then_inc(silud[p], 2)
                for p in range(2):
                    act.wait_ge(x_turned[p], i + 4)
                    x_low_half(p)
                    act.wait_ge(down_done[p], i + 4)
                    act.wait_ge(scattered[p], 8 * i + 16)
                    act.wait_ge(give_in[p], 8 * i + 16)
                    nc.scalar.activation(y[p][:], c.ps[:, 3:5].rearrange("p b n -> p (b n)"), ACT.Copy, scale=give[p][:, 1:2].bitcast(F32)).then_inc(y_ready[p], 2)

        @block.vector
        def _(dve):
            def x_high_half(p):
                nc.vector.tensor_copy(xT[p][:, 4:8], c.ps[:, 6].rearrange("p (k n) -> p k n", n=P)).then_inc(x_high[p], 2)

            for p in range(2):
                nc.vector.memset(xg[p][:], 0.0).then_inc(cleared, 1)
            for p in range(2):
                dve.wait_ge(x_turned[p], 2)
                x_high_half(p)
            for p in range(2):
                dve.sem_inc(gated[p], 2)
                dve.sem_inc(copied[p], 2)
            n = trips(dve)
            with dve.Fori(0, n, 2) as i:
                for p in range(2):
                    dve.wait_ge(silud[p], i + 2)
                    dve.wait_ge(turned[p], i + 2)
                    nc.vector.tensor_tensor(hid[p][:], sl[p][:], c.ps[:, p, EF:2 * EF], ALU.mult).then_inc(gated[p], 2)
                for p in range(2):
                    dve.wait_ge(turned[p], i + 4)
                    dve.wait_ge(down_done[p], i + 2)
                    nc.vector.tensor_copy(hidT[p][:], c.ps[:, 2, 0:2 * P].rearrange("p (k n) -> p k n", n=P)).then_inc(copied[p], 2)
                    dve.wait_ge(x_turned[p], i + 4)
                    x_high_half(p)


def combine(c, y_dram, acc):
    nc = c.nc
    with ExitStack() as s:
        rows = c.sb(s, "expert_rows", [P, 2, TOP_K, D])
        tot = c.sb(s, "row_sums", [P, D])
        sq = c.sb(s, "squares", [P, D])
        ss = c.sb(s, "sum_squares", [P, NT])
        landed = [c.sem(f"rows_landed{p}") for p in range(2)]
        reduced = c.sem("co_reduced")
        added = c.sem("co_added")
        summed = c.sem("co_summed")
        meaned = c.sem("co_meaned")
        block = s.enter_context(nc.Block())
        src = y_dram.rearrange("(t p r) d -> t p r d", p=P, r=TOP_K)

        @block.sync
        def _(sp):
            for tile in range(NT):
                if tile >= 2:
                    sp.wait_ge(reduced, tile - 1)
                sp.dma_start(rows[:, tile % 2], src[tile]).then_inc(landed[tile % 2], 16)

        @block.scalar
        def _(act):
            for tile in range(NT):
                act.wait_ge(added, tile + 1)
                if tile:
                    act.wait_ge(summed, tile)
                nc.scalar.activation(sq[:], acc[:, tile], ACT.Square, accum_out=ss[:, tile:tile + 1]).then_inc(summed, 1)

        @block.gpsimd
        def _(pool):
            pool.wait_ge(meaned, 1)
            nc.gpsimd.tensor_tensor(ss[:], ss[:], c.half[:, 0:NT], ALU.pow).then_inc(meaned, 1)

        @block.vector
        def _(dve):
            for tile in range(NT):
                dve.wait_ge(landed[tile % 2], 16 * (tile // 2 + 1))
                if tile:
                    dve.wait_ge(added, tile)
                nc.vector.tensor_reduce(tot[:], rows[:, tile % 2].rearrange("p r d -> p d r"), AX, ALU.add).then_inc(reduced, 1)
                dve.wait_ge(reduced, tile + 1)
                nc.vector.tensor_tensor(acc[:, tile], acc[:, tile], tot[:], ALU.add).then_inc(added, 1)
            dve.wait_ge(summed, NT)
            nc.vector.tensor_scalar(ss[:], ss[:], 1.0 / D, EPS, ALU.mult, ALU.add).then_inc(meaned, 1)
            dve.wait_ge(meaned, 2)
            for tile in range(NT):
                ins = nc.vector.scalar_tensor_tensor(acc[:, tile], acc[:, tile], ss[:, tile:tile + 1], c.gate[:, 1], ALU.mult, ALU.mult)
            c.vlink(dve, ins)
            for tile in range(NT):
                nc.vector.tensor_tensor(c.x[:, tile], c.x[:, tile], acc[:, tile], ALU.add)


def moe_constants():
    g = np.arange(GROUPS)
    rank = np.concatenate([(g[None, :] < g[:, None]).reshape(-1), np.arange(1, TOP_K + 1)]).astype(np.float32)[None]
    tok = (np.arange(NT)[None, :] * P + np.arange(P)[:, None])
    pay = np.zeros((P, NT, TOP_K, 4), np.int32)
    pay[..., 0] = tok[:, :, None]
    pay[..., 2] = tok[:, :, None] * TOP_K + np.arange(TOP_K)
    table = np.zeros((TABLE * P, 4), np.int32)
    table[:, 0] = SKIPPED
    table[:, 2] = SKIPPED
    return {"rank": rank, "payload": pay, "table": table, "blocks": np.arange(TABLE, dtype=np.float32)[None]}


def build(nc, t, out):
    with ExitStack() as ctx:
        c = Chip(nc, ctx, t)
        landed = c.sem("x_landed")
        stored = c.sem("out_stored")
        c.sems = []
        with ExitStack() as s:
            block = s.enter_context(nc.Block())

            @block.sync
            def _(sp):
                sp.dma_start(c.x[:], t["x"][0].rearrange("(t p) d -> p t d", p=P)).then_inc(landed, 16)
                sp.dma_start(c.ident[:], t["ident"]).then_inc(landed, 16)
                sp.wait_ge(landed, 32)

            @block.vector
            def _(dve):
                nc.vector.memset(c.half[:], -0.5)
        block1_mixer(c)
        c.clear_sems()
        moe(c)
        c.clear_sems()
        block2(c)
        with ExitStack() as s:
            block = s.enter_context(nc.Block())

            @block.sync
            def _(sp):
                sp.dma_start(out[0].rearrange("(t p) d -> p t d", p=P), c.x[:]).then_inc(stored, 16)
                sp.wait_ge(stored, 16)


def kernel(**inputs):
    import numpy as _np
    import concourse.bacc as _bacc
    from concourse.bass_utils import run_bass_kernel_spmd as _run

    nc = _bacc.Bacc("TRN2", target_bir_lowering=False, num_devices=1)
    arrays = {f"in_{k}": _np.ascontiguousarray(v) for k, v in inputs.items()}
    arrays.update({f"const_{k}": v for k, v in constants().items()})
    arrays.update({f"const_{k}": v for k, v in moe_constants().items()})
    t = {k.split("_", 1)[1]: nc.dram_tensor(k, v.shape, mybir.dt.from_np(v.dtype), kind="ExternalInput").ap() for k, v in arrays.items()}
    out = nc.dram_tensor("out", (1, SEQ, D), F32, kind="ExternalOutput").ap()
    build(nc, t, out)
    r = _run(nc, [arrays], core_ids=[0])
    return r.results[0]["out"]
```
